# Optimizing a Trainium2 kernel written in Bass

```python
import jax, jax.numpy as jnp
from jax import lax
import numpy as np

D_MODEL = 1024
BATCH = 1
SEQ = 256
DEPTH = 1

CHUNK = 64
N_META = 16
META_PAD = CHUNK - N_META
D_MIX = D_MODEL
GLA_HEADS = 4
GLA_VAL = D_MIX // 2
GLA_DV = GLA_VAL // GLA_HEADS
GLA_KEY = GLA_VAL // 2
GLA_DK = GLA_KEY // GLA_HEADS
GLA_GATE_RANK = 16
GLA_TAU = 16.0
SSD_INNER = D_MIX - GLA_VAL
SSD_HEADDIM = 64
SSD_HEADS = SSD_INNER // SSD_HEADDIM
SSD_GROUPS = 2
SSD_HEADS_PER_GROUP = SSD_HEADS // SSD_GROUPS
SSD_STATE = 128
SSD_CONV = 4
SSD_CONV_CH = SSD_INNER + 2 * SSD_GROUPS * SSD_STATE
IN_SPLITS = (GLA_KEY, GLA_KEY, GLA_VAL, GLA_VAL, GLA_GATE_RANK, SSD_INNER, SSD_CONV_CH, SSD_HEADS)
D_IN_PROJ = sum(IN_SPLITS)
N_EXPERTS = 32
TOP_K = 4
D_FF = D_MODEL
SWIGLU_LIMIT = 7.0
SWIGLU_ALPHA = 1.702
MOE_BLOCK = 256
DEEPNORM_ALPHA = (2.0 * DEPTH) ** 0.25
DEEPNORM_BETA = (8.0 * DEPTH) ** -0.25
LN_EPS = 1e-5
RMS_EPS = 1e-6

kernel_name = "hymba_gla_ssd_deepnorm_moe"

def layer_norm(t, g, b):
    tf = t.astype(jnp.float32)
    mu = jnp.mean(tf, axis=-1, keepdims=True)
    var = jnp.mean(jnp.square(tf - mu), axis=-1, keepdims=True)
    return ((tf - mu) * lax.rsqrt(var + LN_EPS) * g + b).astype(t.dtype)

def rms_norm(t, g):
    tf = t.astype(jnp.float32)
    return tf * lax.rsqrt(jnp.mean(jnp.square(tf), axis=-1, keepdims=True) + RMS_EPS) * g

def split_last(t, sizes):
    idx = [int(i) for i in np.cumsum(sizes)[:-1]]
    return jnp.split(t, idx, axis=-1)

def causal_depthwise_conv(u, w, b):
    out = lax.conv_general_dilated(
        u, w[:, None, :].astype(u.dtype), window_strides=(1,), padding=[(SSD_CONV - 1, 0)],
        dimension_numbers=("NWC", "WIO", "NWC"), feature_group_count=u.shape[-1])
    return out + b

def gla_chunk_causal(q, k, v, log_a):
    b, lp, _ = q.shape
    nc = lp // CHUNK
    qc = q.reshape(b, nc, CHUNK, GLA_HEADS, GLA_DK).astype(jnp.float32)
    kc = k.reshape(b, nc, CHUNK, GLA_HEADS, GLA_DK).astype(jnp.float32)
    vc = v.reshape(b, nc, CHUNK, GLA_HEADS, GLA_DV).astype(jnp.float32)
    cum = jnp.cumsum(log_a.reshape(b, nc, CHUNK, GLA_HEADS, GLA_DK), axis=2)
    total = cum[:, :, -1]
    k_dec = kc * jnp.exp(total[:, :, None] - cum)
    u = jnp.einsum("bcqhk,bcqhv->bchkv", k_dec, vc)

    def step(s, inp):
        dec, uc = inp
        s = dec[..., None] * s + uc
        return s, s

    _, states = lax.scan(step, jnp.zeros_like(u[:, 0]),
                         (jnp.moveaxis(jnp.exp(total), 1, 0), jnp.moveaxis(u, 1, 0)))
    states = jnp.moveaxis(states, 0, 1)
    o = jnp.einsum("bcqhk,bchkv->bcqhv", qc, states)
    return o.reshape(b, lp, GLA_VAL)

def ssd_chunk_causal(xs, dt, a, bm, cm):
    b, lp, _ = xs.shape
    nc = lp // CHUNK
    g, hg = SSD_GROUPS, SSD_HEADS_PER_GROUP
    xh = xs.reshape(b, nc, CHUNK, g, hg, SSD_HEADDIM).astype(jnp.float32)
    dtc = dt.reshape(b, nc, CHUNK, g, hg)
    bc = bm.reshape(b, nc, CHUNK, g, SSD_STATE).astype(jnp.float32)
    cc = cm.reshape(b, nc, CHUNK, g, SSD_STATE).astype(jnp.float32)
    cum = jnp.cumsum(dtc * a.reshape(g, hg), axis=2)
    total = cum[:, :, -1]
    w = jnp.exp(total[:, :, None] - cum) * dtc
    u = jnp.einsum("bcqgn,bcqgh,bcqghp->bcghnp", bc, w, xh)

    def step(s, inp):
        dec, uc = inp
        s = dec[..., None, None] * s + uc
        return s, s

    _, states = lax.scan(step, jnp.zeros_like(u[:, 0]),
                         (jnp.moveaxis(jnp.exp(total), 1, 0), jnp.moveaxis(u, 1, 0)))
    states = jnp.moveaxis(states, 0, 1)
    y = jnp.einsum("bcqgn,bcghnp->bcqghp", cc, states)
    return y.reshape(b, lp, SSD_INNER)

def hybrid_mixer(h, w_in, gla_w_a2, gla_b_a, gla_norm_g, ssd_conv_w, ssd_conv_b,
                 ssd_dt_bias, ssd_a_log, ssd_d, ssd_norm_g, w_out):
    b, l, _ = h.shape
    proj = h @ w_in
    proj = jnp.pad(proj, ((0, 0), (META_PAD, 0), (0, 0)))
    lp = l + META_PAD
    valid = (jnp.arange(lp) >= META_PAD)[None, :, None]
    q, k, v, og, a1, z, xbc, dt_raw = split_last(proj, IN_SPLITS)

    log_a = jax.nn.log_sigmoid((a1 @ gla_w_a2 + gla_b_a).astype(jnp.float32)) / GLA_TAU
    log_a = jnp.where(valid, log_a, 0.0)
    o_gla = gla_chunk_causal(q * (GLA_DK ** -0.5), k, v, log_a)[:, META_PAD:]
    o_gla = rms_norm(o_gla.reshape(b, l, GLA_HEADS, GLA_DV), gla_norm_g.reshape(GLA_HEADS, GLA_DV))
    o_gla = o_gla.reshape(b, l, GLA_VAL) * jax.nn.silu(og[:, META_PAD:].astype(jnp.float32))

    xbc = jax.nn.silu(causal_depthwise_conv(xbc, ssd_conv_w, ssd_conv_b))
    xs, bm, cm = split_last(xbc, (SSD_INNER, SSD_GROUPS * SSD_STATE, SSD_GROUPS * SSD_STATE))
    dt = jax.nn.softplus(dt_raw.astype(jnp.float32) + ssd_dt_bias)
    dt = jnp.where(valid, dt, 0.0)
    a = -jnp.exp(ssd_a_log.astype(jnp.float32))
    y = ssd_chunk_causal(xs, dt, a, bm, cm)
    y = y + (xs.reshape(b, lp, SSD_HEADS, SSD_HEADDIM) * ssd_d[:, None]).reshape(b, lp, SSD_INNER)
    y = y[:, META_PAD:] * jax.nn.silu(z[:, META_PAD:].astype(jnp.float32))
    gsz = SSD_INNER // SSD_GROUPS
    y = rms_norm(y.reshape(b, l, SSD_GROUPS, gsz), ssd_norm_g.reshape(SSD_GROUPS, gsz))
    y = y.reshape(b, l, SSD_INNER)

    mix = jnp.concatenate([o_gla, y], axis=-1).astype(h.dtype)
    return mix @ w_out

def clamped_swiglu(a, u):
    a = jnp.minimum(a, SWIGLU_LIMIT)
    u = jnp.clip(u, -SWIGLU_LIMIT, SWIGLU_LIMIT)
    return a * jax.nn.sigmoid(SWIGLU_ALPHA * a) * (u + 1.0)

def moe_ffn(t, router_w, router_b, w_gate, w_up, b_gate, b_up, w_down, b_down):
    n, d = t.shape
    logits = (t @ router_w + router_b).astype(jnp.float32)
    top_v, top_i = lax.top_k(logits, TOP_K)
    gates = jax.nn.softmax(top_v, axis=-1)
    flat_e = top_i.reshape(-1)
    flat_tok = jnp.arange(n * TOP_K, dtype=jnp.int32) // TOP_K
    flat_g = gates.reshape(-1)
    order = jnp.argsort(flat_e)
    sorted_e = flat_e[order]
    counts = jnp.zeros((N_EXPERTS,), jnp.int32).at[flat_e].add(1)
    starts = jnp.cumsum(counts) - counts
    padded = (counts + MOE_BLOCK - 1) // MOE_BLOCK * MOE_BLOCK
    pad_end = jnp.cumsum(padded)
    pad_start = pad_end - padded
    dest = pad_start[sorted_e] + (jnp.arange(n * TOP_K, dtype=jnp.int32) - starts[sorted_e])
    n_blocks = -(-(n * TOP_K) // MOE_BLOCK) + N_EXPERTS
    rows = n_blocks * MOE_BLOCK
    row_tok = jnp.full((rows,), n, jnp.int32).at[dest].set(flat_tok[order])
    row_gate = jnp.zeros((rows,), jnp.float32).at[dest].set(flat_g[order])
    block_e = jnp.minimum(
        jnp.searchsorted(pad_end, jnp.arange(n_blocks, dtype=jnp.int32) * MOE_BLOCK, side="right"),
        N_EXPERTS - 1)
    t_pad = jnp.concatenate([t, jnp.zeros((1, d), t.dtype)], axis=0)

    def expert_block(inp):
        tok, gt, e = inp
        xb = t_pad[tok]
        hid = clamped_swiglu(xb @ w_gate[e] + b_gate[e], xb @ w_up[e] + b_up[e])
        yb = hid @ w_down[e] + b_down[e]
        return (yb * gt[:, None].astype(yb.dtype)).astype(t.dtype)

    yb = lax.map(expert_block, (row_tok.reshape(n_blocks, MOE_BLOCK),
                                row_gate.reshape(n_blocks, MOE_BLOCK), block_e))
    out = jax.ops.segment_sum(yb.reshape(rows, d), row_tok, num_segments=n + 1)
    return out[:n]

def setup_inputs(seed: int = 0) -> dict:
    key = jax.random.key(seed)
    ks = jax.random.split(key, 32)
    f32 = jnp.float32

    def nrm(k, shape, scale):
        return jax.random.normal(k, shape, f32) * scale

    dt0 = jnp.exp(jax.random.uniform(ks[10], (DEPTH, SSD_HEADS), f32, np.log(1e-3), np.log(1e-1)))
    return {
        "x": nrm(ks[0], (BATCH, SEQ, D_MODEL), 1.0),
        "meta_tokens": nrm(ks[1], (N_META, D_MODEL), 1.0),
        "ln_in_g": 1.0 + nrm(ks[2], (D_MODEL,), 0.02),
        "ln_in_b": nrm(ks[3], (D_MODEL,), 0.02),
        "w_in": nrm(ks[4], (DEPTH, D_MODEL, D_IN_PROJ), D_MODEL ** -0.5),
        "gla_w_a2": nrm(ks[5], (DEPTH, GLA_GATE_RANK, GLA_KEY), GLA_GATE_RANK ** -0.5),
        "gla_b_a": nrm(ks[6], (DEPTH, GLA_KEY), 0.1),
        "gla_norm_g": 1.0 + nrm(ks[7], (DEPTH, GLA_VAL), 0.02),
        "ssd_conv_w": nrm(ks[8], (DEPTH, SSD_CONV, SSD_CONV_CH), SSD_CONV ** -0.5),
        "ssd_conv_b": nrm(ks[9], (DEPTH, SSD_CONV_CH), 0.02),
        "ssd_dt_bias": dt0 + jnp.log(-jnp.expm1(-dt0)),
        "ssd_a_log": jnp.log(jax.random.uniform(ks[11], (DEPTH, SSD_HEADS), f32, 1.0, 16.0)),
        "ssd_d": 1.0 + nrm(ks[12], (DEPTH, SSD_HEADS), 0.1),
        "ssd_norm_g": 1.0 + nrm(ks[13], (DEPTH, SSD_INNER), 0.02),
        "w_out": nrm(ks[14], (DEPTH, D_MIX, D_MODEL), D_MIX ** -0.5 * DEEPNORM_BETA),
        "ln1_g": 1.0 + nrm(ks[15], (DEPTH, D_MODEL), 0.02),
        "ln1_b": nrm(ks[16], (DEPTH, D_MODEL), 0.02),
        "router_w": nrm(ks[17], (DEPTH, D_MODEL, N_EXPERTS), D_MODEL ** -0.5),
        "router_b": nrm(ks[18], (DEPTH, N_EXPERTS), 0.01),
        "moe_w_gate": nrm(ks[19], (DEPTH, N_EXPERTS, D_MODEL, D_FF), D_MODEL ** -0.5),
        "moe_w_up": nrm(ks[20], (DEPTH, N_EXPERTS, D_MODEL, D_FF), D_MODEL ** -0.5),
        "moe_b_gate": nrm(ks[21], (DEPTH, N_EXPERTS, D_FF), 0.02),
        "moe_b_up": nrm(ks[22], (DEPTH, N_EXPERTS, D_FF), 0.02),
        "moe_w_down": nrm(ks[23], (DEPTH, N_EXPERTS, D_FF, D_MODEL), D_FF ** -0.5 * DEEPNORM_BETA),
        "moe_b_down": nrm(ks[24], (DEPTH, N_EXPERTS, D_MODEL), 0.02 * DEEPNORM_BETA),
        "ln2_g": 1.0 + nrm(ks[25], (DEPTH, D_MODEL), 0.02),
        "ln2_b": nrm(ks[26], (DEPTH, D_MODEL), 0.02),
    }

def reference(x, meta_tokens, ln_in_g, ln_in_b, w_in, gla_w_a2, gla_b_a, gla_norm_g,
              ssd_conv_w, ssd_conv_b, ssd_dt_bias, ssd_a_log, ssd_d, ssd_norm_g, w_out,
              ln1_g, ln1_b, router_w, router_b, moe_w_gate, moe_w_up, moe_b_gate, moe_b_up,
              moe_w_down, moe_b_down, ln2_g, ln2_b):
    b = x.shape[0]
    meta = jnp.broadcast_to(meta_tokens[None].astype(x.dtype), (b, N_META, D_MODEL))
    h = jnp.concatenate([meta, x], axis=1)
    h = layer_norm(h, ln_in_g, ln_in_b)
    for l in range(DEPTH):
        mix = hybrid_mixer(h, w_in[l], gla_w_a2[l], gla_b_a[l], gla_norm_g[l], ssd_conv_w[l],
                           ssd_conv_b[l], ssd_dt_bias[l], ssd_a_log[l], ssd_d[l], ssd_norm_g[l],
                           w_out[l])
        h = layer_norm(DEEPNORM_ALPHA * h + mix, ln1_g[l], ln1_b[l])
        ff = moe_ffn(h.reshape(-1, D_MODEL), router_w[l], router_b[l], moe_w_gate[l], moe_w_up[l],
                     moe_b_gate[l], moe_b_up[l], moe_w_down[l], moe_b_down[l]).reshape(h.shape)
        h = layer_norm(DEEPNORM_ALPHA * h + ff, ln2_g[l], ln2_b[l])
    return h[:, N_META:]


_drawn_inputs = setup_inputs


def setup_inputs(seed=0):
    import zlib

    import numpy as np

    out = dict(_drawn_inputs(seed))
    spreads = {}
    factors = {'gla_b_a': 3.031,
     'gla_norm_g': 11.735,
     'ssd_conv_b': 3.119,
     'ssd_norm_g': 10.966,
     'router_b': 4.214,
     'moe_b_gate': 8.0,
     'moe_b_up': 8.0,
     'moe_b_down': 8.0,
     'ln2_g': 22.18,
     'ln2_b': 22.137}
    for name, (base, spread) in spreads.items():
        noise = np.random.default_rng([zlib.crc32(name.encode()), seed]).standard_normal(out[name].shape)
        drawn = base * np.exp(spread * noise) if base else spread * noise
        out[name] = __import__('jax').numpy.asarray(drawn.astype(out[name].dtype))
    for name, factor in factors.items():
        out[name] = (out[name] * factor).astype(out[name].dtype)
    return out
```

```python
import concourse.bass as bass
from concourse import mybir
from contextlib import ExitStack

F32 = mybir.dt.float32
BF16 = mybir.dt.bfloat16
I32 = mybir.dt.int32
U32 = mybir.dt.uint32
ALU = mybir.AluOpType
ACT = mybir.ActivationFunctionType
AX_X = mybir.AxisListType.X

P = 128
D = 1024
KT = D // P
SEQ = 256
NT = SEQ // P
META = 16
TOK = META + SEQ
CHUNK = 64
NCH = SEQ // CHUNK
GKEY, GVAL, GH, GDK, GDV, GRANK = 256, 512, 4, 64, 128, 16
TAU = 16.0
SIN, SHD, SHEADS, SGRP, SST, NCONV = 512, 64, 8, 2, 128, 4
XBC = SIN + 2 * SGRP * SST
XC = XBC // P
NE, FF = 32, 1024
LIMIT, SALPHA = 7.0, 1.702
DN_ALPHA = 2.0 ** 0.25
LN_EPS, RMS_EPS = 1e-5, 1e-6

C_Q, C_K, C_V, C_OG, C_A1, C_Z = 0, 256, 512, 1024, 1536, 1552
C_XBC, C_DT = C_Z + SIN, C_Z + SIN + XBC

RING = 16
UW = 2048
UPE = 3 * D * FF // (P * UW)
UNROLL = 4
SL = 64
NJ = SEQ // SL
MAXX = NT * P * 4 // SL

W_ORDER = [C_XBC + 256 * i for i in range(4)] + [C_K, C_V, C_V + 256, C_Q, C_Z, C_Z + 256, C_OG, C_OG + 256]
U_XBC, U_K, U_V, U_Q, U_Z, U_OG, U_OUT = 0, 4, 5, 7, 8, 10, 12


def build(nc, x, meta, ln_in_g, ln_in_b, w_in, gla_w_a2, gla_b_a, gla_norm_g, ssd_conv_w, ssd_conv_b,
          ssd_dt_bias, ssd_a_log, ssd_d, ssd_norm_g, w_out, ln1_g, ln1_b, router_w, router_b,
          w_gate, w_up, b_gate, b_up, w_down, b_down, ln2_g, ln2_b, out):
    with ExitStack() as ctx:
        def sb(name, shape, dt=F32):
            return ctx.enter_context(nc.sbuf_tensor(name, shape, dt))

        def sem(name):
            return ctx.enter_context(nc.semaphore(name))

        ring = sb("ring", [P, RING, UW])
        arena = sb("arena", [P, 19392])
        bank = [ctx.enter_context(nc.psum_tensor(f"bank{i}", [P, 512], F32)) for i in range(8)]

        def cut(at, *shape, parts=P, dt=F32):
            n = 1
            for s in shape:
                n *= s
            words = n if dt in (F32, I32, U32) else n // 2
            v = arena[0:parts, at:at + words]
            if dt is not F32:
                v = v.bitcast(dt)
            if len(shape) == 2:
                v = v.rearrange("p (a b) -> p a b", a=shape[0])
            if len(shape) == 3:
                v = v.rearrange("p (a b c) -> p a b c", a=shape[0], b=shape[1])
            return v

        xh = cut(0, NT, D)
        metah = cut(2048, D, parts=META)
        k_m = cut(2048, GKEY, parts=META)
        v_m = cut(2304, GVAL, parts=META)
        la_m = cut(2816, GKEY, parts=META)
        hT = cut(3072, KT, TOK)
        mixT = cut(3072, KT, SEQ)
        h1T = cut(3072, KT, SEQ)
        lnbc = cut(5248, 2, D)
        normg = cut(7296, D)
        v_t = cut(8320, NT, GVAL)
        og = cut(8320, NT, GVAL)
        k_t = cut(9344, NT, GKEY)
        tmp = cut(9856, NT, GKEY)
        z_t = cut(9344, NT, SIN)
        la = cut(10368, NT, GKEY)
        expD = cut(10880, GKEY)
        qT = cut(11136, 2, SEQ)
        cacc = cut(11648, 2, TOK)
        csig = cut(12192, 2, TOK)
        CT = cut(12736, SGRP, SEQ)
        xs = cut(13248, 3, SIN)
        y1 = cut(14784, NT, SIN)
        Bt = cut(15808, 3, SGRP * SST)
        Sg = cut(16576, NCH + 1, 2, GDV)
        prow = cut(16576, P, parts=72)
        w_a2e = cut(16704, GKEY, parts=25)
        w_small = cut(16960, KT, 24)
        Ss = cut(17856, 3, SIN)
        sT = cut(17856, TOK, parts=25)
        b_dn = cut(11648, D, parts=NE)
        rw = cut(12672, KT, NE)
        rb = cut(12928, NE)
        eid = cut(13100, NE + 1)
        bparts = cut(13248, 2, FF, parts=96, dt=BF16)
        braw = cut(16576, 2, FF, parts=96)
        xT = cut(8320, 2, KT, SL)
        a_c = cut(9344, 512)
        s_c = cut(9856, 512)
        u_c = cut(11136, 512)
        hidT = cut(10368, 4, P)
        y_s = cut(14784, 512)
        GT = cut(15296, SEQ, parts=NE)
        selG = cut(7296, 2, NT, P)
        sel = cut(7808, 2, NT, SL)
        selGT = cut(15808, SEQ)
        oh = cut(16064, 2, SL, parts=96, dt=BF16)
        iota = cut(18624, NJ, P)
        tri_s = cut(12960, P)
        z2 = cut(11648, NT, D)
        logit = cut(2048, NT, NE)
        top8 = cut(2112, NT, 8)
        idx8 = cut(2128, NT, 8, dt=U32)
        idxf = cut(2144, NT, 4)
        onehot = cut(2160, NT, 4, NE)
        ghot = cut(2416, NT, 4, NE)
        mask = cut(2672, NT, NE)
        gate = cut(2736, NT, NE + 1)
        posm = cut(2802, NT, NE + 1)
        gate4 = cut(2868, NT, 8)
        flag = cut(8064, 3, NE, parts=1)
        rank = cut(8160, 3 * NE, parts=1)
        xcount = cut(8256, 1, parts=1, dt=I32)
        xlist2 = cut(8260, 2, MAXX, parts=1, dt=I32)
        xlist = xlist2[:, 0, :]
        flag_e = cut(9344, 3, NE, parts=1)
        flag_j = cut(9440, 3, NE, parts=1)
        xlf = cut(9536, 2, MAXX, parts=1)
        xscr = cut(9568, 3 * NE, parts=1)

        small = sb("small", [P, 332])
        o = [0]

        def sm(*shape):
            n = 1
            for s in shape:
                n *= s
            v = small[:, o[0]:o[0] + n]
            o[0] += n
            if len(shape) == 2:
                v = v.rearrange("p (a b) -> p a b", a=shape[0])
            return v

        stats = sm(2, 6)
        mv = sm(3, 2)
        rstd = sm(3)
        vtmp = sm(3)
        pcol = sm(72)
        dtb = sm(SHEADS)
        alog = sm(SHEADS)
        dskip = sm(SHEADS)
        dt_x = sm(3, SHEADS)
        dt_a = sm(3, SHEADS)
        dt_b = sm(3, SHEADS)
        dt_c = sm(3, SHEADS)
        dt_w = sm(3, SHEADS)
        decs = sm(NCH, SHEADS)
        decg = sm(8)
        ssy, sso = sm(4), sm(8)
        rmy, rmo = sm(4), sm(8)
        rry, rro = sm(4), sm(8)
        rmt = sm(8)
        vnew = sm(3)
        gmax = sm(NT)
        gsum = sm(NT)
        ident = sb("ident", [P, P])
        tri = sb("tri", [P, P])
        ones = sb("ones", [P, P])
        x_in = [sem(f"x_in{t}") for t in range(NT)]
        meta_in, params_in, small_in, lnin_in, normg_in = sem("meta_in"), sem("params_in"), sem("small_in"), sem("lnin_in"), sem("normg_in")
        ln1_in, ln2_in, bias_in, late_in, out_done = sem("ln1_in"), sem("ln2_in"), sem("bias_in"), sem("late_in"), sem("out_done")
        landed = [sem(f"landed{s}") for s in range(RING)]
        unit_used = sem("unit_used")
        half_used = sem("half_used")
        consts, zeroed, pads = sem("consts"), sem("zeroed"), sem("pads")
        pe_step, dve_step, act_step, pool_step, xstep = sem("pe_step"), sem("dve_step"), sem("act_step"), sem("pool_step"), sem("xstep")
        var_in, rstd_in, xhat = sem("var_in"), sem("rstd_in"), sem("xhat")
        pcol_ps, pcol_ok, hT_ps, hT_act, hT_dve, h_ok = sem("pcol_ps"), sem("pcol_ok"), sem("hT_ps"), sem("hT_act"), sem("hT_dve"), sem("h_ok")
        conv_ps, conv, csig_ok, silu, cT_ps, cT_ok = sem("conv_ps"), sem("conv"), sem("csig_ok"), sem("silu"), sem("cT_ps"), sem("cT_ok")
        sT_ps, sT_ok, dtT_ps, dtx_ok, dt_e, dt_ok = sem("sT_ps"), sem("sT_ok"), sem("dtT_ps"), sem("dtx_ok"), sem("dt_e"), sem("dt_ok")
        dsum_ps, dsum_ok, wx_ok, y1_ok = sem("dsum_ps"), sem("dsum_ok"), sem("wx_ok"), sem("y1_ok")
        la_ps, la_sp, la_ok, D_ps, D_ok, kdec = sem("la_ps"), sem("la_sp"), sem("la_ok"), sem("D_ps"), sem("D_ok"), sem("kdec")
        k_ps, v_ps, v_ok, q_ps, q_ok = sem("k_ps"), sem("v_ps"), sem("v_ok"), sem("q_ps"), sem("q_ok")
        us_ps, Ss_ok, ug_ps, Sg_ok, y_ps, o_ps = sem("us_ps"), sem("Ss_ok"), sem("ug_ps"), sem("Sg_ok"), sem("y_ps"), sem("o_ps")
        z_ps, z_sig, z_ok, og_ps, og_sig, og_ok, og_g = sem("z_ps"), sem("z_sig"), sem("z_ok"), sem("og_ps"), sem("og_sig"), sem("og_ok"), sem("og_g")
        rms_in, y_mid, ssq_y, rms_y, mix_y, ssq_o, rms_o, mix_o = sem("rms_in"), sem("y_mid"), sem("ssq_y"), sem("rms_y"), sem("mix_y"), sem("ssq_o"), sem("rms_o"), sem("mix_o")
        mixT_ps, mixT_act, mixT_dve, wout_ps = sem("mixT_ps"), sem("mixT_act"), sem("mixT_dve"), sem("wout_ps")
        var1, rstd1, h1_hat, h1_ok, h1T_ps, h1T_act, h1T_dve, logit_ps = (sem("var1"), sem("rstd1"), sem("h1_hat"), sem("h1_ok"), sem("h1T_ps"),
                                                                          sem("h1T_act"), sem("h1T_dve"), sem("logit_ps"))
        top_ok, gexp, mask_ok, pos_ps, pos_ok, GT_ps, GT_ok, acc0 = sem("top_ok"), sem("gexp"), sem("mask_ok"), sem("pos_ps"), sem("pos_ok"), sem("GT_ps"), sem("GT_ok"), sem("acc0")
        iota_ok, bparts_ok, extra_ok, list_ok = sem("iota_ok"), sem("bparts_ok"), sem("extra_ok"), sem("list_ok")
        sel_ok, gath_ps, xT_ok, selT_ps, selGT_ok = sem("sel_ok"), sem("gath_ps"), sem("xT_ok"), sem("selT_ps"), sem("selGT_ok")
        g_ps, u_ps, a_ok, sig_ok, u_ok, as_ok, hid_ok = sem("g_ps"), sem("u_ps"), sem("a_ok"), sem("sig_ok"), sem("u_ok"), sem("as_ok"), sem("hid_ok")
        hidT_ps, hidT_ok, d_ps, yd_ok, scat = sem("hidT_ps"), sem("hidT_ok"), sem("d_ps"), sem("yd_ok"), sem("scat")
        z2_ok, rstd2, fin = sem("z2_ok"), sem("rstd2"), sem("fin")

        def linker(eng, s):
            n = [0]

            def link(ins):
                n[0] += 1
                ins.then_inc(s, 1)
                eng.wait_ge(s, n[0])
            return link

        def row(v):
            return v[0, :].rearrange("(a n) -> a n", a=1)

        def spread(v, n):
            return v.broadcast_to([n, v.shape[1]]) if v.shape[0] == 1 else v

        units = {0: w_gate, 1: w_up, 2: w_down}

        def unit_src(e, u):
            m = units[u // (UPE // 3)]
            q = u % (UPE // 3)
            return m[0, e].rearrange("(k p) n -> p k n", p=P)[:, 2 * q:2 * q + 2, :] if isinstance(e, int) else \
                m[0, bass.ds(e, 1)].rearrange("a (k p) n -> p (a k) n", p=P)[:, 2 * q:2 * q + 2, :]

        def slot(s):
            return ring[:, s, :].rearrange("p (k n) -> p k n", k=2)

        block = ctx.enter_context(nc.Block())

        @block.sync
        def _(sp):
            for t in range(NT):
                sp.dma_start(xh[:, t, :], x[0, t * P:(t + 1) * P, :]).then_inc(x_in[t], 16)
            for n, c0 in enumerate(W_ORDER):
                sp.dma_start(ring[:, n, :].rearrange("p (k n) -> p k n", k=KT),
                             w_in[0, :, c0:c0 + 256].rearrange("(k p) n -> p k n", p=P)).then_inc(landed[n], 16)
                if n == 3:
                    sp.dma_start(w_small[:, :, 0:GRANK], w_in[0, :, C_A1:C_A1 + GRANK].rearrange("(k p) n -> p k n", p=P)).then_inc(small_in, 16)
                    sp.dma_start(w_small[:, :, GRANK:24], w_in[0, :, C_DT:C_DT + SHEADS].rearrange("(k p) n -> p k n", p=P)).then_inc(small_in, 16)
            for n in range(4):
                sp.dma_start(ring[:, U_OUT + n, :].rearrange("p (k n) -> p k n", k=KT),
                             w_out[0, :, 256 * n:256 * n + 256].rearrange("(k p) n -> p k n", p=P)).then_inc(landed[U_OUT + n], 16)

            w_used = [(conv_ps, 2), (conv_ps, 4), (conv_ps, 6), (conv_ps, 8), (k_ps, 1), (half_used, 1), (v_ps, 3), (q_ps, 1),
                      (half_used, 2), (z_ps, 2), (half_used, 3), (og_ps, 2), (wout_ps, 3), (wout_ps, 3), (wout_ps, 4), (wout_ps, 4)]

            def experts(it, peeled):
                for i in range(UPE * UNROLL):
                    before = i - RING
                    if peeled and before < 0:
                        sp.wait_ge(*w_used[i])
                    else:
                        k, u = before // UPE, before % UPE
                        m, q = u // 4, u % 4
                        if q == 3:
                            sp.wait_ge((g_ps, u_ps, d_ps)[m], it * UNROLL + (k + 1))
                        else:
                            sp.wait_ge(unit_used, (it * UNROLL + k) * 9 + (3 * m + q + 1))
                    sp.dma_start(slot(i % RING), unit_src(it * UNROLL + i // UPE, i % UPE)).then_inc(landed[i % RING], 16)
            experts(0, True)
            with sp.Fori(1, NE // UNROLL) as it:
                experts(it, False)
            sp.wait_ge(list_ok, 1)
            nx = sp.value_load(xcount[0:1, 0:1], min_val=0, max_val=MAXX)
            with sp.If(nx > 0):
                sp.wait_ge(list_ok, 2)
                with sp.Fori(0, nx) as i:
                    sp.wait_ge(d_ps, i + NE)
                    e = sp.value_load(xlist[0:1, bass.ds(i, 1)], min_val=0, max_val=NE - 1)
                    for u in range(UPE):
                        sp.dma_start(slot(u), unit_src(e, u)).then_inc(landed[u], 16)

        @block.gpsimd
        def _(pool):
            link = linker(pool, pool_step)
            link(nc.gpsimd.memset(ident[:, :], 0.0))
            nc.gpsimd.affine_select(out=ident[:, :], in_=ident[:, :], compare_op=ALU.not_equal, fill=1.0,
                                    base=0, pattern=[[-1, P]], channel_multiplier=1).then_inc(consts, 1)
            nc.gpsimd.memset(ones[:, :], 1.0).then_inc(consts, 1)
            link(nc.gpsimd.memset(tri[:, :], 1.0 / TAU))
            link(nc.gpsimd.affine_select(out=tri[:, :], in_=tri[:, :], compare_op=ALU.is_gt, fill=0.0,
                                         base=0, pattern=[[-1, P]], channel_multiplier=1))
            nc.gpsimd.memset(tri[CHUNK:P, 0:CHUNK], 0.0).then_inc(consts, 1)
            pool.wait_ge(lnin_in, 32)
            pool.wait_ge(hT_ps, KT)
            for t in range(NT):
                link(nc.gpsimd.tensor_tensor(xh[:, t, :], xh[:, t, :], lnbc[:, 0, :], ALU.mult))
                ins = nc.gpsimd.tensor_tensor(xh[:, t, :], xh[:, t, :], lnbc[:, 1, :], ALU.add)
                ins.then_inc(h_ok, 1)
            for c in range(XC):
                pool.wait_ge(csig_ok, c + 1)
                if c < 6:
                    dst, at = cacc[:, c % 2, :], slice(0, TOK)
                else:
                    dst, at = CT[:, c - 6, :], slice(META, TOK)
                nc.gpsimd.tensor_tensor(dst, cacc[:, c % 2, at], csig[:, c % 2, at], ALU.mult).then_inc(silu, 1)
            pool.wait_ge(cT_ok, 4)
            for t in range(NT):
                ins = nc.gpsimd.tensor_tensor(y1[:, t, :].rearrange("p (h q) -> p h q", h=SHEADS),
                                              xs[:, t, :].rearrange("p (h q) -> p h q", h=SHEADS),
                                              dskip.unsqueeze(2).broadcast_to([P, SHEADS, SHD]), ALU.mult)
            ins.then_inc(y1_ok, 1)
            pool.wait_ge(normg_in, 32)
            for t in range(NT):
                pool.wait_ge(og_ok, t + 1)
                nc.gpsimd.tensor_tensor(og[:, t, :], og[:, t, :], normg[:, 0:GVAL], ALU.mult).then_inc(og_g, 1)
            pool.wait_ge(y_ps, NCH)
            pool.wait_ge(o_ps, 2)
            nc.gpsimd.iota(iota[:, :, :].rearrange("p j (h s) -> p j h s", h=2), [[SL, NJ], [0, 2], [1, SL]], base=0,
                           channel_multiplier=0, allow_small_or_imprecise_dtypes=True).then_inc(iota_ok, 1)
            link(nc.gpsimd.memset(eid, 0.0))
            for q in range(3):
                v = eid[NE * q:NE * (q + 1), 0:NE]
                link(nc.gpsimd.affine_select(out=v, in_=v, compare_op=ALU.not_equal, fill=1.0, base=0, pattern=[[-1, NE]],
                                             channel_multiplier=1))
            link(nc.gpsimd.memset(tri_s[:, :], 1.0))
            nc.gpsimd.affine_select(out=tri_s[:, :], in_=tri_s[:, :], compare_op=ALU.is_gt, fill=0.0, base=0, pattern=[[1, P]],
                                    channel_multiplier=-1).then_inc(iota_ok, 1)
            pool.wait_ge(bias_in, 96)
            pool.wait_ge(us_ps, NCH + 1)
            link(nc.gpsimd.tensor_copy(bparts[:, :, :], braw[:, :, :]))
            for q, times in ((1, 1), (2, 2)):
                r = slice(NE * q, NE * (q + 1))
                for k in range(times):
                    link(nc.gpsimd.tensor_tensor(braw[r, :, :], braw[r, :, :], bparts[r, :, :], ALU.subtract))
                    ins = nc.gpsimd.tensor_copy(bparts[r, :, :], braw[r, :, :])
                    if q == 2 and k:
                        ins.then_inc(bparts_ok, 1)
                    else:
                        link(ins)
            pool.wait_ge(ln1_in, 32)
            pool.wait_ge(bparts_ok, 1)
            for t in range(NT):
                pool.wait_ge(h1T_ps, 2 * t + 2)
                link(nc.gpsimd.tensor_tensor(xh[:, t, :], xh[:, t, :], lnbc[:, 0, :], ALU.mult))
                nc.gpsimd.tensor_tensor(xh[:, t, :], xh[:, t, :], lnbc[:, 1, :], ALU.add).then_inc(h1_ok, 1)

        @block.scalar
        def _(act):
            link = linker(act, act_step)
            act.dma_start(metah[:, :], meta).then_inc(meta_in, 16)
            act.dma_start(prow[0:8, :], ln_in_g.rearrange("(c p) -> c p", p=P)).then_inc(params_in, 16)
            act.dma_start(prow[8:16, :], ln_in_b.rearrange("(c p) -> c p", p=P)).then_inc(params_in, 16)
            act.dma_start(prow[16:48, :], ssd_conv_w[0].rearrange("j (c p) -> (j c) p", p=P)).then_inc(params_in, 16)
            act.dma_start(prow[48:56, :], ssd_conv_b[0].rearrange("(c p) -> c p", p=P)).then_inc(params_in, 16)
            act.dma_start(prow[56:64, :], ln1_g[0].rearrange("(c p) -> c p", p=P)).then_inc(params_in, 16)
            act.dma_start(prow[64:72, :], ln1_b[0].rearrange("(c p) -> c p", p=P)).then_inc(params_in, 16)
            act.wait_ge(zeroed, 1)
            act.dma_start(w_a2e[0:GRANK, :], gla_w_a2[0]).then_inc(small_in, 16)
            act.dma_start(w_a2e[24:25, :], gla_b_a).then_inc(small_in, 16)
            act.dma_start(dtb, ssd_dt_bias.broadcast_to([P, SHEADS])).then_inc(small_in, 16)
            act.dma_start(alog, ssd_a_log.broadcast_to([P, SHEADS])).then_inc(small_in, 16)
            act.dma_start(dskip, ssd_d.broadcast_to([P, SHEADS])).then_inc(small_in, 16)
            act.dma_start(lnbc[:, 0, :], ln_in_g.rearrange("(a n) -> a n", a=1).broadcast_to([P, D])).then_inc(lnin_in, 16)
            act.dma_start(lnbc[:, 1, :], ln_in_b.rearrange("(a n) -> a n", a=1).broadcast_to([P, D])).then_inc(lnin_in, 16)
            act.dma_start(normg[:, 0:GVAL], gla_norm_g.broadcast_to([P, GVAL])).then_inc(normg_in, 16)
            act.dma_start(normg[:, GVAL:D], ssd_norm_g.broadcast_to([P, SIN])).then_inc(normg_in, 16)

            def inv_sqrt(src, dst, wait_for, n, done):
                act.wait_ge(wait_for, n)
                link(nc.scalar.activation(dst, src, ACT.Ln))
                nc.scalar.activation(dst, dst, ACT.Exp, scale=-0.5).then_inc(done, 1)

            def mixT_evac(b, kt):
                nc.scalar.activation(mixT[:, kt:kt + 2, :].rearrange("p a n -> p (a n)"), b[:, :], ACT.Copy).then_inc(mixT_act, 1)

            inv_sqrt(vtmp, rstd, var_in, 1, rstd_in)
            act.wait_ge(pcol_ok, 1)
            for kt in range(0, KT, 2):
                act.wait_ge(hT_ps, kt + 1)
                nc.scalar.activation(hT[:, kt, :], bank[kt % 4][:, 0:TOK], ACT.Identity, bias=pcol[:, 8 + kt:9 + kt],
                                     scale=pcol[:, kt:kt + 1]).then_inc(hT_act, 1)

            def c_evac(c):
                act.wait_ge(cT_ps, c + 1)
                b = bank[7] if c % 2 == 0 else bank[3]
                dst, at = (xs, c * P) if c < 4 else (Bt, (c - 4) * P)
                nc.scalar.activation(dst[:, 0:NT, at:at + P], b[:, 0:2 * P].rearrange("p (t n) -> p t n", t=NT), ACT.Copy)
                nc.scalar.activation(dst[0:META, 2, at:at + P], b[0:META, 2 * P:3 * P], ACT.Copy).then_inc(cT_ok, 1)

            for c in range(XC):
                act.wait_ge(conv, c + 1)
                if c >= 2:
                    act.wait_ge(silu, c - 1)
                nc.scalar.activation(csig[:, c % 2, :], cacc[:, c % 2, :], ACT.Sigmoid).then_inc(csig_ok, 1)
                if c >= 2:
                    c_evac(c - 2)
            act.wait_ge(sT_ps, 1)
            nc.scalar.activation(sT[0:24, :], bank[0][0:24, 0:TOK], ACT.Copy).then_inc(sT_ok, 1)
            act.wait_ge(dtx_ok, 1)
            act.wait_ge(small_in, 112)
            flat = lambda v: v.rearrange("p a b -> p (a b)")
            link(nc.scalar.activation(alog, alog, ACT.Exp))
            link(nc.scalar.activation(flat(dt_a), flat(dt_x), ACT.Abs))
            link(nc.scalar.activation(flat(dt_a), flat(dt_a), ACT.Exp, scale=-1.0))
            nc.scalar.activation(flat(dt_b), flat(dt_a), ACT.Ln, bias=1.0).then_inc(dt_e, 1)
            act.wait_ge(la_ps, 1)
            tmpf = tmp[:, :, :].rearrange("p t n -> p (t n)")
            link(nc.scalar.activation(tmpf, bank[2][:, :], ACT.Abs))
            link(nc.scalar.activation(expD[0:META, :], bank[0][0:META, 0:GKEY], ACT.Abs))
            link(nc.scalar.activation(tmpf, tmpf, ACT.Exp, scale=-1.0))
            link(nc.scalar.activation(expD[0:META, :], expD[0:META, :], ACT.Exp, scale=-1.0))
            link(nc.scalar.activation(tmpf, tmpf, ACT.Ln, bias=1.0))
            nc.scalar.activation(expD[0:META, :], expD[0:META, :], ACT.Ln, bias=1.0).then_inc(la_sp, 1)
            act.wait_ge(h_ok, NT)
            act.dma_start(lnbc[:, 0, :], ln1_g.broadcast_to([P, D])).then_inc(ln1_in, 16)
            act.dma_start(lnbc[:, 1, :], ln1_b.broadcast_to([P, D])).then_inc(ln1_in, 16)
            act.wait_ge(dsum_ps, 1)
            nc.scalar.activation(flat(dt_w[:, 0:NT, :]), bank[6][:, 0:16], ACT.Exp, scale=TAU)
            nc.scalar.activation(dt_w[0:META, 2, :], bank[6][0:META, 16:24], ACT.Exp, scale=TAU)
            nc.scalar.activation(flat(decs), bank[6][:, 32:64], ACT.Exp).then_inc(dsum_ok, 1)
            act.wait_ge(D_ps, 1)
            nc.scalar.activation(tmpf, bank[2][:, :], ACT.Exp)
            nc.scalar.activation(expD[0:META, :], bank[0][0:META, 0:GKEY], ACT.Exp)
            nc.scalar.activation(decg, bank[0][:, GKEY:GKEY + 8], ACT.Exp, scale=1.0 / TAU).then_inc(D_ok, 1)
            for n, (dst, b) in enumerate(((v_t[:, 0, :], bank[5]), (v_t[:, 1, :], bank[7]), (v_m, bank[3]))):
                act.wait_ge(v_ps, n + 1)
                nc.scalar.activation(dst, b[0:dst.shape[0], :], ACT.Copy).then_inc(v_ok, 1)
            act.wait_ge(q_ps, 1)
            nc.scalar.activation(qT[:, :, :].rearrange("p a n -> p (a n)"), bank[5][:, :], ACT.Copy, scale=GDK ** -0.5).then_inc(q_ok, 1)
            for t in range(NT):
                act.wait_ge(z_ps, t + 1)
                act.wait_ge(kdec, 1)
                act.wait_ge(ug_ps, 3)
                nc.scalar.activation(z_t[:, t, :], bank[(0, 5)[t]][:, :], ACT.Sigmoid).then_inc(z_sig, 1)
            for t in range(NT):
                act.wait_ge(og_ps, t + 1)
                nc.scalar.activation(og[:, t, :], bank[(6, 7)[t]][:, :], ACT.Sigmoid).then_inc(og_sig, 1)
            scr = csig[:, :, :].rearrange("p a b -> p (a b)")
            for t in range(NT):
                act.wait_ge(y_mid, t + 1)
                for g in range(SGRP):
                    if g == 0 and t:
                        link(ins)
                    ins = nc.scalar.activation(scr[:, g * 256:(g + 1) * 256], y1[:, t, g * 256:(g + 1) * 256], ACT.Square,
                                               accum_out=ssy[:, t * 2 + g:t * 2 + g + 1])
            ins.then_inc(ssq_y, 1)
            inv_sqrt(rmy, rry, rms_in, 1, rms_y)
            act.wait_ge(mixT_ps, 1)
            mixT_evac(bank[0], 4)
            act.wait_ge(mixT_ps, 2)
            mixT_evac(bank[5], 6)
            act.wait_ge(ssq_y, 1)
            for hb in range(2):
                act.wait_ge(o_ps, hb + 1)
                for t in range(NT):
                    for i in range(2):
                        n = t * 4 + 2 * i + hb
                        if hb and not (t or i):
                            link(ins)
                        ins = nc.scalar.activation(scr[:, (2 * t + i) * GDV:(2 * t + i + 1) * GDV], bank[3 - hb][:, t * 256 + i * P:t * 256 + (i + 1) * P], ACT.Square,
                                                   accum_out=sso[:, n:n + 1])
            ins.then_inc(ssq_o, 1)
            inv_sqrt(rmo, rro, rms_in, 2, rms_o)
            act.wait_ge(ssq_o, 1)
            act.wait_ge(y_ps, NCH)
            act.dma_start(rw[:, :, :], router_w[0].rearrange("(k p) e -> p k e", p=P)).then_inc(late_in, 16)
            act.dma_start(rb, router_b.broadcast_to([P, NE])).then_inc(late_in, 16)
            act.dma_start(b_dn[:, :], b_down[0]).then_inc(late_in, 16)
            for q in range(3):
                act.dma_start(braw[NE * q:NE * (q + 1), 0, :], b_gate[0]).then_inc(bias_in, 16)
                act.dma_start(braw[NE * q:NE * (q + 1), 1, :], b_up[0]).then_inc(bias_in, 16)
            act.wait_ge(mixT_ps, 3)
            mixT_evac(bank[6], 0)
            for t in range(NT):
                inv_sqrt(vtmp[:, t:t + 1], rstd[:, t:t + 1], var1, t + 1, rstd1)
            for t in range(NT):
                act.wait_ge(h1T_ps, 2 * t + 1)
                for kt in range(4):
                    ins = nc.scalar.activation(h1T[:, kt, t * P:(t + 1) * P], bank[(0, 6)[t]][:, kt * P:(kt + 1) * P], ACT.Identity,
                                               bias=pcol[:, 64 + kt:65 + kt], scale=pcol[:, 56 + kt:57 + kt])
                ins.then_inc(h1T_act, 1)
            act.wait_ge(top_ok, 1)
            for t in range(NT):
                ins = nc.scalar.activation(gate4[:, t, 0:4], top8[:, t, 0:4], ACT.Exp, bias=gmax[:, t:t + 1])
            ins.then_inc(gexp, 1)

            act.wait_ge(h1_ok, NT)
            act.dma_start(lnbc[:, 0, :], ln2_g.broadcast_to([P, D])).then_inc(ln2_in, 16)
            act.dma_start(lnbc[:, 1, :], ln2_b.broadcast_to([P, D])).then_inc(ln2_in, 16)

            def xT_evac(n, par):
                act.wait_ge(gath_ps, n + 1)
                if not isinstance(n, int) or n >= 2:
                    act.wait_ge(u_ps, n - 1)
                nc.scalar.activation(xT[:, par, :, :].rearrange("p k s -> p (k s)"), bank[7][:, :], ACT.Copy).then_inc(xT_ok, 1)

            def tile(n, par, first, ahead):
                act.wait_ge(selT_ps, n + 1)
                nc.scalar.activation(selGT, bank[6][:, 0:SEQ], ACT.Copy).then_inc(selGT_ok, 1)
                act.wait_ge(a_ok, n + 1)
                nc.scalar.activation(s_c, a_c, ACT.Sigmoid, scale=SALPHA).then_inc(sig_ok, 1)
                if ahead:
                    xT_evac(n + 1, 1 - par)
                act.wait_ge(hidT_ps, n + 1)
                if not first:
                    act.wait_ge(d_ps, n)
                nc.scalar.activation(hidT[:, :, :].rearrange("p c n -> p (c n)"), bank[7][:, :], ACT.Copy).then_inc(hidT_ok, 1)

            xT_evac(0, 0)
            for k in range(UNROLL):
                tile(k, k % 2, k == 0, True)
            with act.Fori(1, NE // UNROLL) as it:
                for k in range(UNROLL):
                    tile(it * UNROLL + k, k % 2, False, True)
            act.wait_ge(list_ok, 1)
            nx = act.value_load(xcount[0:1, 0:1], min_val=0, max_val=MAXX)
            with act.If(nx > 0):
                with act.Fori(0, nx) as i:
                    xT_evac(i + (NE + 1), 0)
                    tile(i + NE, 0, False, False)
            for t in range(NT):
                inv_sqrt(vtmp[:, t:t + 1], rstd[:, t:t + 1], z2_ok, t + 1, rstd2)
            for t in range(NT):
                act.wait_ge(fin, t + 1)
                act.dma_start(out[0, t * P:(t + 1) * P, :], z2[:, t, :]).then_inc(out_done, 16)
            act.wait_ge(out_done, 16 * NT)

        @block.tensor
        def _(pe):
            link = linker(pe, pe_step)
            mm = nc.tensor.matmul
            tr = nc.tensor.transpose

            def wslot(n, kt, a=0, b=256):
                return ring[:, n, :].rearrange("p (k n) -> p k n", k=KT)[:, kt, a:b]

            pe.wait_ge(consts, 3)
            pe.wait_ge(params_in, 96)
            tr(bank[7][:, 0:72], prow[:, :], ident[0:72, 0:72]).then_inc(pcol_ps, 1)
            pe.wait_ge(xhat, 3)
            for kt in range(KT):
                if kt >= 4:
                    pe.wait_ge(hT_act if kt % 2 == 0 else hT_dve, kt // 2 - 1)
                b = bank[kt % 4]
                tr(b[:, 0:META], metah[:, kt * P:(kt + 1) * P], ident[0:META, 0:META])
                for t in range(NT):
                    ins = tr(b[:, META + t * P:META + (t + 1) * P], xh[:, t, kt * P:(kt + 1) * P], ident[:, :])
                ins.then_inc(hT_ps, 1)
            pe.wait_ge(hT_act, KT // 2)
            pe.wait_ge(hT_dve, KT // 2)
            pe.wait_ge(pads, 1)

            def c_transposes(c):
                b = bank[7] if c % 2 == 0 else bank[3]
                pe.wait_ge(silu, c + 1)
                if c == 0:
                    pe.wait_ge(pcol_ok, 1)
                if c >= 2:
                    pe.wait_ge(cT_ok, c - 1)
                src = cacc[:, c % 2, :]
                for t in range(NT):
                    tr(b[:, t * P:(t + 1) * P], src[:, META + t * P:META + (t + 1) * P], ident[:, :])
                tr(b[0:META, 2 * P:3 * P], src[:, 0:META], ident[:, :]).then_inc(cT_ps, 1)

            for c in range(XC):
                n = U_XBC + c // 2
                pe.wait_ge(landed[n], 16)
                if c >= 3:
                    pe.wait_ge(conv, c - 2)
                for kt in range(KT):
                    ins = mm(bank[4 + c % 3][:, 3:3 + TOK], wslot(n, kt, (c % 2) * P, (c % 2) * P + P), hT[:, kt, :],
                             start=kt == 0, stop=kt == KT - 1)
                ins.then_inc(conv_ps, 1)
                if c >= 2:
                    c_transposes(c - 2)
            pe.wait_ge(small_in, 112)
            for kt in range(KT):
                ins = mm(bank[0][0:24, 0:TOK], w_small[:, kt, :], hT[:, kt, :], start=kt == 0, stop=kt == KT - 1)
            ins.then_inc(sT_ps, 1)

            def token_major(out_x, out_m, n, cols=256):
                for t in range(NT):
                    for kt in range(KT):
                        ins = mm(out_x[t], hT[:, kt, META + t * P:META + (t + 1) * P], wslot(n, kt), start=kt == 0, stop=kt == KT - 1)
                if out_m is not None:
                    for kt in range(KT):
                        ins = mm(out_m, hT[:, kt, 0:META], wslot(n, kt), start=kt == 0, stop=kt == KT - 1)
                return ins

            pe.wait_ge(landed[U_K], 16)
            pe.wait_ge(conv, 7)
            token_major([bank[4][:, t * 256:(t + 1) * 256] for t in range(NT)], bank[1][0:META, 256:512], U_K).then_inc(k_ps, 1)
            pe.wait_ge(sT_ok, 1)
            for t in range(NT):
                tr(bank[1][:, t * 24:(t + 1) * 24], sT[0:24, META + t * P:META + (t + 1) * P], ident[0:24, 0:24])
            tr(bank[1][0:META, 48:72], sT[0:24, 0:META], ident[0:24, 0:24]).then_inc(dtT_ps, 1)
            for t in range(NT):
                mm(bank[2][:, t * 256:(t + 1) * 256], sT[:, META + t * P:META + (t + 1) * P], w_a2e[:, :], start=True, stop=True)
            mm(bank[0][0:META, 0:GKEY], sT[:, 0:META], w_a2e[:, :], start=True, stop=True).then_inc(la_ps, 1)
            pe.wait_ge(landed[U_V], 16)
            pe.wait_ge(conv, 8)
            pe.wait_ge(cT_ok, 6)
            token_major([bank[5][:, 0:256], bank[7][:, 0:256]], bank[3][0:META, 0:256], U_V).then_inc(half_used, 1)
            pe.wait_ge(dt_ok, 1)
            for t in range(NT):
                mm(bank[6][:, t * 8:(t + 1) * 8], tri[:, :], dt_c[:, t, :], start=True, stop=True)
            mm(bank[6][0:META, 16:24], tri[0:META, 0:META], dt_c[0:META, 2, :], start=True, stop=True)
            for c in (0, 2, 1, 3):
                r = CHUNK * (c % 2)
                if c == 1:
                    link(ins)
                ins = mm(bank[6][:, 32 + c * 8:40 + c * 8], ones[r:r + CHUNK, :], dt_c[r:r + CHUNK, c // 2, :], start=True, stop=True)
            ins.then_inc(dsum_ps, 1)
            pe.wait_ge(la_ok, 1)
            for t in range(NT):
                mm(bank[2][:, t * 256:(t + 1) * 256], tri[:, :], la[:, t, :], start=True, stop=True)
            mm(bank[0][0:META, 0:GKEY], tri[0:META, 0:META], la_m[:, :], start=True, stop=True)
            for c in (0, 2, 1, 3):
                r = CHUNK * (c % 2)
                if c == 1:
                    link(ins)
                for i in range(2):
                    ins = mm(bank[0][:, GKEY + i * 4 + c:GKEY + i * 4 + c + 1], la[r:r + CHUNK, c // 2, i * P:(i + 1) * P],
                             ones[r:r + CHUNK, 0:1], start=True, stop=True)
            ins.then_inc(D_ps, 1)
            pe.wait_ge(landed[U_V + 1], 16)
            n = U_V + 1
            for dst, at, m in ((bank[5], META, P), (bank[7], META + P, P), (bank[3], 0, META)):
                for kt in range(KT):
                    ins = mm(dst[0:m, 256:512], hT[:, kt, at:at + m], wslot(n, kt), start=kt == 0, stop=kt == KT - 1)
                ins.then_inc(v_ps, 1)
            pe.wait_ge(wx_ok, 1)
            ssd_banks = (1, 6, 4, 1, 6)

            def ssd_update(c):
                b = bank[ssd_banks[c]]
                for g in range(SGRP):
                    if c == 0:
                        k, w = Bt[0:META, 2, g * SST:(g + 1) * SST], xs[0:META, 2, g * 256:(g + 1) * 256]
                    else:
                        r = CHUNK * ((c - 1) % 2)
                        k, w = Bt[r:r + CHUNK, (c - 1) // 2, g * SST:(g + 1) * SST], xs[r:r + CHUNK, (c - 1) // 2, g * 256:(g + 1) * 256]
                    ins = mm(b[:, g * 256:(g + 1) * 256], k, w, start=True, stop=True)
                ins.then_inc(us_ps, 1)

            pe.wait_ge(kdec, 1)
            for c in range(3):
                ssd_update(c)
            pe.wait_ge(landed[U_Q], 16)
            pe.wait_ge(v_ok, 1)
            for i in range(2):
                for kt in range(KT):
                    ins = mm(bank[5][:, i * SEQ:(i + 1) * SEQ], wslot(U_Q, kt, i * P, (i + 1) * P), hT[:, kt, META:TOK],
                             start=kt == 0, stop=kt == KT - 1)
            ins.then_inc(q_ps, 1)
            pe.wait_ge(v_ok, 3)

            def gla_update(c):
                b, at = (bank[7], 0) if c == 0 else (bank[3] if c % 2 else bank[2], ((c - 1) // 2) * 256)
                for h in range(GH):
                    dst = b[64 * (h % 2):64 * (h % 2) + 64, at + (h // 2) * GDV:at + (h // 2 + 1) * GDV]
                    if c == 0:
                        kk, vv = k_m[:, h * GDK:(h + 1) * GDK], v_m[:, h * GDV:(h + 1) * GDV]
                    else:
                        r = CHUNK * ((c - 1) % 2)
                        kk, vv = k_t[r:r + CHUNK, (c - 1) // 2, h * GDK:(h + 1) * GDK], v_t[r:r + CHUNK, (c - 1) // 2, h * GDV:(h + 1) * GDV]
                    ins = mm(dst, kk, vv, start=True, stop=True)
                return ins

            gla_update(0).then_inc(ug_ps, 1)
            for c in (1, 3):
                ins = gla_update(c)
            ins.then_inc(ug_ps, 1)
            for c in (2, 4):
                ins = gla_update(c)
            ins.then_inc(ug_ps, 1)
            for c in (3, 4):
                pe.wait_ge(Ss_ok, c - 2 + 0)
                ssd_update(c)
            pe.wait_ge(q_ok, 1)
            for hf in range(2):
                n = U_Z + hf
                pe.wait_ge(landed[n], 16)
                for t in range(NT):
                    for kt in range(KT):
                        ins = mm(bank[(0, 5)[t]][:, hf * 256:(hf + 1) * 256], hT[:, kt, META + t * P:META + (t + 1) * P], wslot(n, kt),
                                 start=kt == 0, stop=kt == KT - 1)
                    if hf:
                        ins.then_inc(z_ps, 1)
                if not hf:
                    ins.then_inc(half_used, 1)
            def ssd_out(c):
                pe.wait_ge(Ss_ok, c + 1)
                r = CHUNK * ((c - 1) % 2)
                b = bank[(4, 1)[(c - 1) // 2]]
                for g in range(SGRP):
                    ins = mm(b[r:r + CHUNK, g * 256:(g + 1) * 256], CT[:, g, (c - 1) * CHUNK:c * CHUNK], Ss[:, c % 3, g * 256:(g + 1) * 256],
                             start=True, stop=True)
                ins.then_inc(y_ps, 1)
            pe.wait_ge(silu, XC)
            pe.wait_ge(Ss_ok, 3)
            for c in range(1, NCH + 1):
                ssd_out(c)
            for hf in range(2):
                n = U_OG + hf
                pe.wait_ge(landed[n], 16)
                pe.wait_ge(Ss_ok, NCH + 1)
                pe.wait_ge(Sg_ok, 1)
                for t in range(NT):
                    for kt in range(KT):
                        ins = mm(bank[(6, 7)[t]][:, hf * 256:(hf + 1) * 256], hT[:, kt, META + t * P:META + (t + 1) * P], wslot(n, kt),
                                 start=kt == 0, stop=kt == KT - 1)
                    if hf:
                        ins.then_inc(og_ps, 1)
                if not hf:
                    ins.then_inc(half_used, 1)

            def mix_transposes(b, src, kts):
                for j, kt in enumerate(kts):
                    for t in range(NT):
                        at = (kt % 4) * P
                        ins = tr(b[:, j * SEQ + t * P:j * SEQ + (t + 1) * P], src[:, t, at:at + P], ident[:, :])
                ins.then_inc(mixT_ps, 1)

            pe.wait_ge(mix_y, 2)
            mix_transposes(bank[0], z_t, (4, 5))
            mix_transposes(bank[5], z_t, (6, 7))
            pe.wait_ge(Sg_ok, NCH + 1)
            for hb in range(2):
                for c in range(1, NCH + 1):
                    r = CHUNK * ((c - 1) % 2)
                    t = (c - 1) // 2
                    for i in range(2):
                        q = qT[64 * hb:64 * hb + 64, i, (c - 1) * CHUNK:c * CHUNK]
                        ins = mm(bank[3 - hb][r:r + CHUNK, t * 256 + i * GDV:t * 256 + (i + 1) * GDV], q,
                                 Sg[64 * hb:64 * hb + 64, c, i, :], start=True, stop=True)
                ins.then_inc(o_ps, 1)

            def out_part(t, kts, first):
                for nb in range(2):
                    b = bank[((1, 4), (2, 3))[t][nb]]
                    for kt in kts:
                        ins = mm(b[:, :], mixT[:, kt, t * P:(t + 1) * P],
                                 ring[:, U_OUT + 2 * nb:U_OUT + 2 * nb + 2, kt * 256:(kt + 1) * 256],
                                 start=first and kt == kts[0], stop=(not first) and kt == kts[-1], skip_group_check=True)
                    if not first:
                        ins.then_inc(wout_ps, 1)

            for n in range(4):
                pe.wait_ge(landed[U_OUT + n], 16)
            pe.wait_ge(mixT_act, 2)
            out_part(0, (4, 5, 6, 7), True)
            pe.wait_ge(mix_o, 2)
            mix_transposes(bank[6], og, (0, 1))
            mix_transposes(bank[7], og, (2, 3))
            out_part(1, (4, 5, 6, 7), True)
            pe.wait_ge(mixT_act, 3)
            pe.wait_ge(mixT_dve, 1)
            out_part(0, (0, 1, 2, 3), False)
            out_part(1, (0, 1, 2, 3), False)
            for t in range(NT):
                pe.wait_ge(h1_hat, t + 1)
                for half in range(2):
                    b = bank[((0, 5), (6, 7))[t][half]]
                    for j in range(4):
                        kt = half * 4 + j
                        ins = tr(b[:, j * P:(j + 1) * P], xh[:, t, kt * P:(kt + 1) * P], ident[:, :])
                    ins.then_inc(h1T_ps, 1)
            pe.wait_ge(h1T_act, NT)
            pe.wait_ge(h1T_dve, NT)
            pe.wait_ge(late_in, 48)
            for t in range(NT):
                for kt in range(KT):
                    ins = mm(bank[4][:, t * NE:(t + 1) * NE], h1T[:, kt, t * P:(t + 1) * P], rw[:, kt, :], start=kt == 0, stop=kt == KT - 1)
            ins.then_inc(logit_ps, 1)
            pe.wait_ge(mask_ok, 1)
            pe.wait_ge(iota_ok, 2)
            mm(bank[5][:, 0:NE], tri_s[:, :], mask[:, 0, :], start=True, stop=True)
            mm(bank[5][:, NE:2 * NE], tri_s[:, :], mask[:, 1, :], start=True, stop=False)
            mm(bank[5][:, NE:2 * NE], ones[:, :], mask[:, 0, :], start=False, stop=True)
            mm(bank[5][0:1, 2 * NE:3 * NE], ones[:, 0:1], mask[:, 0, :], start=True, stop=False)
            mm(bank[5][0:1, 2 * NE:3 * NE], ones[:, 0:1], mask[:, 1, :], start=False, stop=True).then_inc(pos_ps, 1)
            pe.wait_ge(mask_ok, 2)
            for t in range(NT):
                ins = tr(bank[6][0:NE, t * P:(t + 1) * P], gate[:, t, 0:NE], ident[:, :])
            ins.then_inc(GT_ps, 1)
            pe.wait_ge(GT_ok, 1)
            for t in range(NT):
                for h in range(2):
                    mm(bank[2 * t + h][:, :], GT[:, t * P:(t + 1) * P], b_dn[:, h * 512:(h + 1) * 512], start=True, stop=False,
                       skip_group_check=True)

            def gather(n, par):
                pe.wait_ge(sel_ok, n + 1)
                for kt in range(KT):
                    for t in range(NT):
                        ins = mm(bank[7][:, kt * SL:(kt + 1) * SL], xh[:, t, kt * P:(kt + 1) * P], sel[:, par, t, :], start=t == 0, stop=t == 1)
                ins.then_inc(gath_ps, 1)

            def scatter(n):
                pe.wait_ge(yd_ok, n + 1)
                for t in range(NT):
                    for h in range(2):
                        ins = mm(bank[2 * t + h][:, :], selGT[h * SL:(h + 1) * SL, t * P:(t + 1) * P], y_s[h * SL:(h + 1) * SL, :],
                                 start=False, stop=False, skip_group_check=True)
                ins.then_inc(scat, 1)

            def tile(n, par, first, unit_at, arrived, ahead, gathered):
                pe.wait_ge(xT_ok, gathered + 1)
                for m, (b, free, done) in enumerate(((bank[4], a_ok, g_ps), (bank[5], u_ok, u_ps))):
                    if not first:
                        pe.wait_ge(free, n)
                    for h in range(2):
                        mm(b[h * SL:(h + 1) * SL, :], oh[:, par, :], bparts[:, m, h * 512:(h + 1) * 512], start=True, stop=False)
                    for q in range(4):
                        arrived(4 * m + q)
                        for k in range(2):
                            kt = 2 * q + k
                            for h in range(2):
                                ins = mm(b[h * SL:(h + 1) * SL, :], xT[:, par, kt, :], slot(unit_at(4 * m + q))[:, k, h * 512:(h + 1) * 512],
                                         start=False, stop=kt == KT - 1)
                        ins.then_inc(done if q == 3 else unit_used, 1)
                if ahead and not first:
                    scatter(n - 1)
                for t in range(NT):
                    ins = tr(bank[6][:, t * P:(t + 1) * P], selG[:, par, t, :], ident[:, :])
                ins.then_inc(selT_ps, 1)
                if ahead:
                    gather(n + 1, 1 - par)
                    pe.wait_ge(xT_ok, n + 2)
                pe.wait_ge(hid_ok, n + 1)
                for c in range(4):
                    ins = tr(bank[7][:, c * P:(c + 1) * P], u_c[:, c * P:(c + 1) * P], ident[:, :])
                ins.then_inc(hidT_ps, 1)
                pe.wait_ge(selGT_ok, n + 1)
                pe.wait_ge(hidT_ok, n + 1)
                for q in range(4):
                    arrived(8 + q)
                    for k in range(2):
                        kt = 2 * q + k
                        for h in range(2):
                            ins = mm(bank[6][h * SL:(h + 1) * SL, :], hidT[:, kt % 4, (kt // 4) * SL:(kt // 4 + 1) * SL],
                                     slot(unit_at(8 + q))[:, k, h * 512:(h + 1) * 512], start=kt == 0, stop=kt == KT - 1)
                    ins.then_inc(d_ps if q == 3 else unit_used, 1)

            def experts(it, peeled):
                for k in range(UNROLL):
                    def at(u):
                        return UPE * k + u

                    def arrived(u):
                        pe.wait_ge(landed[at(u) % RING], it * (UPE * UNROLL // RING * 16) + (2 + at(u) // RING) * 16)
                    n = it * UNROLL + k
                    tile(n, k % 2, peeled and k == 0, lambda u: at(u) % RING, arrived, True, n)

            pe.wait_ge(h1_ok, NT)
            gather(0, 0)
            pe.wait_ge(bparts_ok, 1)
            experts(0, True)
            with pe.Fori(1, NE // UNROLL) as it:
                experts(it, False)
            scatter(NE - 1)
            pe.wait_ge(list_ok, 1)
            nx = pe.value_load(xcount[0:1, 0:1], min_val=0, max_val=MAXX)
            with pe.If(nx > 0):
                with pe.Fori(0, nx) as i:
                    gather(i + (NE + 1), 0)
                    uses = 1 + NE * UPE // RING
                    tile(i + NE, 0, False, lambda u: u, lambda u: pe.wait_ge(landed[u], i * 16 + (uses + 1) * 16), False, i + (NE + 1))
                    scatter(i + NE)

        @block.vector
        def _(dve):
            link = linker(dve, dve_step)
            ts = nc.vector.tensor_scalar
            tt = nc.vector.tensor_tensor
            stt = nc.vector.scalar_tensor_tensor
            copy = nc.vector.tensor_copy

            for b in (4, 5, 6):
                nc.vector.memset(bank[b][:, 0:NCONV - 1], 0.0).then_inc(pads, 1)
            link(nc.vector.memset(sT[:, :], 1.0))
            link(nc.vector.memset(mv[:, :, :], 1.0))
            link(nc.vector.memset(dt_x[:, :, :], 0.0))
            nc.vector.memset(w_a2e[:, :], 0.0).then_inc(zeroed, 1)

            def refine(y, v, t, done=None):
                link(tt(t, y, y, ALU.mult))
                link(tt(t, t, v, ALU.mult))
                link(ts(t, t, -0.5, 1.5, ALU.mult, ALU.add))
                link(tt(y, y, t, ALU.mult))

            def moments(src, n, t):
                for i in range(2):
                    last = nc.vector.bn_stats(stats[0:n, i, :], src[:, i * 512:(i + 1) * 512])
                link(last)
                link(nc.vector.bn_aggr(mv[0:n, t, :], stats[0:n, :, :]))

            for t in range(NT):
                dve.wait_ge(x_in[t], 16)
                moments(xh[:, t, :], P, t)
            dve.wait_ge(meta_in, 16)
            moments(metah[:, :], META, 2)
            ts(vtmp, mv[:, :, 1], LN_EPS, None, ALU.add).then_inc(var_in, 1)
            dve.wait_ge(pcol_ps, 1)
            copy(pcol, bank[7][:, 0:72]).then_inc(pcol_ok, 1)
            dve.wait_ge(rstd_in, 1)
            dve.wait_ge(var_in, 1)
            refine(rstd, vtmp, vnew)
            for t in range(NT):
                ts(xh[:, t, :], xh[:, t, :], mv[:, t, 0:1], rstd[:, t:t + 1], ALU.subtract, ALU.mult).then_inc(xhat, 1)
            ts(metah[:, :], metah[:, :], mv[0:META, 2, 0:1], rstd[0:META, 2:3], ALU.subtract, ALU.mult).then_inc(xhat, 1)
            dve.wait_ge(pcol_ok, 1)
            for kt in range(1, KT, 2):
                dve.wait_ge(hT_ps, kt + 1)
                ts(hT[:, kt, :], bank[kt % 4][:, 0:TOK], pcol[:, kt:kt + 1], pcol[:, 8 + kt:9 + kt], ALU.mult, ALU.add).then_inc(hT_dve, 1)
            dve.wait_ge(pads, 3)
            for c in range(XC):
                dve.wait_ge(conv_ps, c + 1)
                if c >= 2:
                    dve.wait_ge(cT_ps, c - 1)
                acc, b = cacc[:, c % 2, :], bank[4 + c % 3]
                link(ts(acc, b[:, 0:TOK], pcol[:, 16 + c:17 + c], pcol[:, 48 + c:49 + c], ALU.mult, ALU.add))
                for j in range(1, NCONV):
                    ins = stt(acc, b[:, j:j + TOK], pcol[:, 16 + 8 * j + c:17 + 8 * j + c], acc, ALU.mult, ALU.add)
                    if j < NCONV - 1:
                        link(ins)
                ins.then_inc(conv, 1)
            dve.wait_ge(dtT_ps, 1)
            dve.wait_ge(small_in, 112)
            tt(dt_x[:, 0:NT, :], bank[1][:, 0:48].rearrange("p (t n) -> p t n", t=NT)[:, :, GRANK:24],
               dtb.unsqueeze(1).broadcast_to([P, NT, SHEADS]), ALU.add)
            tt(dt_x[0:META, 2, :], bank[1][0:META, 48 + GRANK:72], dtb[0:META, :], ALU.add).then_inc(dtx_ok, 1)
            dve.wait_ge(dt_e, 1)
            link(ts(dt_c, dt_a, 1.0, None, ALU.add))
            link(ts(dt_w, dt_c, -1.0, None, ALU.add))
            link(tt(dt_w, dt_a, dt_w, ALU.subtract))
            link(nc.vector.reciprocal(dt_c, dt_c))
            link(tt(dt_w, dt_w, dt_c, ALU.mult))
            link(tt(dt_b, dt_b, dt_w, ALU.add))
            link(stt(dt_x, dt_x, 0.0, dt_b, ALU.max, ALU.add))
            stt(dt_c, dt_x, -1.0, alog.unsqueeze(1).broadcast_to([P, 3, SHEADS]), ALU.mult, ALU.mult).then_inc(dt_ok, 1)
            dve.wait_ge(la_sp, 1)
            stt(la[:, :, :].rearrange("p t n -> p (t n)"), bank[2][:, :], 0.0, tmp[:, :, :].rearrange("p t n -> p (t n)"), ALU.min, ALU.subtract)
            stt(la_m, bank[0][0:META, 0:GKEY], 0.0, expD[0:META, :], ALU.min, ALU.subtract).then_inc(la_ok, 1)
            dve.wait_ge(dsum_ok, 1)
            tt(dt_w[:, 0:NT, :], dt_w[:, 0:NT, :], dt_x[:, 0:NT, :], ALU.mult)
            link(tt(dt_w[0:META, 2, :], dt_w[0:META, 2, :], dt_x[0:META, 2, :], ALU.mult))
            dve.wait_ge(y1_ok, 1)
            for t, m in ((0, P), (1, P), (2, META)):
                v = xs[0:m, t, :].rearrange("p (h q) -> p h q", h=SHEADS)
                ins = tt(v, v, dt_w[0:m, t, :].unsqueeze(2).broadcast_to([m, SHEADS, SHD]), ALU.mult)
            ins.then_inc(wx_ok, 1)
            dve.wait_ge(D_ok, 1)
            dve.wait_ge(k_ps, 1)
            tt(k_t[:, :, :].rearrange("p t n -> p (t n)"), bank[4][:, :], tmp[:, :, :].rearrange("p t n -> p (t n)"), ALU.mult)
            tt(k_m, bank[1][0:META, 256:512], expD[0:META, :], ALU.mult).then_inc(kdec, 1)
            ssd_banks = (1, 6, 4, 1, 6)

            def ssd_scan(c):
                dve.wait_ge(us_ps, c + 1)
                if c == 0:
                    copy(Ss[:, 0, :], bank[1][:, :]).then_inc(Ss_ok, 1)
                    return
                dve.wait_ge(Ss_ok, c)
                if c == NCH:
                    dve.wait_ge(y_ps, 1)
                new = Ss[:, c % 3, :]
                link(tt(new.rearrange("p (h q) -> p h q", h=SHEADS), Ss[:, (c - 1) % 3, :].rearrange("p (h q) -> p h q", h=SHEADS),
                        decs[:, c - 1, :].unsqueeze(2).broadcast_to([P, SHEADS, SHD]), ALU.mult))
                tt(new, new, bank[ssd_banks[c]][:, :], ALU.add).then_inc(Ss_ok, 1)

            for c in range(3):
                ssd_scan(c)
            dve.wait_ge(ug_ps, 1)
            copy(Sg[:, 0, :, :].rearrange("p a n -> p (a n)"), bank[7][:, 0:2 * GDV]).then_inc(Sg_ok, 1)
            for c in range(1, NCH + 1):
                dve.wait_ge(ug_ps, 2 if c % 2 else 3)
                dve.wait_ge(Sg_ok, c)
                b, at = bank[3] if c % 2 else bank[2], ((c - 1) // 2) * 256
                for i in range(2):
                    ins = stt(Sg[:, c, i, :], Sg[:, c - 1, i, :], decg[:, i * 4 + c - 1:i * 4 + c], b[:, at + i * GDV:at + (i + 1) * GDV],
                              ALU.mult, ALU.add)
                ins.then_inc(Sg_ok, 1)
            for c in (3, 4):
                ssd_scan(c)
            for t in range(NT):
                dve.wait_ge(z_sig, t + 1)
                tt(z_t[:, t, :], z_t[:, t, :], bank[(0, 5)[t]][:, :], ALU.mult).then_inc(z_ok, 1)
            for t in range(NT):
                dve.wait_ge(y_ps, 2 * t + 2)
                link(tt(y1[:, t, :], y1[:, t, :], bank[(4, 1)[t]][:, :], ALU.add))
                dve.wait_ge(z_ok, t + 1)
                tt(y1[:, t, :], y1[:, t, :], z_t[:, t, :], ALU.mult).then_inc(y_mid, 1)
            dve.wait_ge(ssq_y, 1)
            ts(rmy, ssy, 1.0 / 256, RMS_EPS, ALU.mult, ALU.add).then_inc(rms_in, 1)
            dve.wait_ge(rms_y, 1)
            dve.wait_ge(rms_in, 1)
            refine(rry, rmy, rmt[:, 0:4])
            dve.wait_ge(normg_in, 32)
            for t in range(NT):
                for g in range(SGRP):
                    at = slice(g * 256, (g + 1) * 256)
                    ins = stt(z_t[:, t, at], y1[:, t, at], rry[:, 2 * t + g:2 * t + g + 1], normg[:, GVAL + g * 256:GVAL + (g + 1) * 256],
                              ALU.mult, ALU.mult)
                ins.then_inc(mix_y, 1)
            for t in range(NT):
                dve.wait_ge(og_sig, t + 1)
                tt(og[:, t, :], og[:, t, :], bank[(6, 7)[t]][:, :], ALU.mult).then_inc(og_ok, 1)
            dve.wait_ge(ssq_o, 1)
            ts(rmo, sso, 1.0 / GDV, RMS_EPS, ALU.mult, ALU.add).then_inc(rms_in, 1)
            dve.wait_ge(rms_o, 1)
            dve.wait_ge(rms_in, 2)
            refine(rro, rmo, rmt)
            for t in range(NT):
                dve.wait_ge(og_g, t + 1)
                for h in range(GH):
                    at = slice(h * GDV, (h + 1) * GDV)
                    ins = stt(og[:, t, at], bank[3 - h % 2][:, t * 256 + (h // 2) * GDV:t * 256 + (h // 2 + 1) * GDV],
                              rro[:, t * 4 + h:t * 4 + h + 1], og[:, t, at], ALU.mult, ALU.mult)
                ins.then_inc(mix_o, 1)
            dve.wait_ge(mixT_ps, 4)
            copy(mixT[:, 2:4, :].rearrange("p a n -> p (a n)"), bank[7][:, :]).then_inc(mixT_dve, 1)
            dve.wait_ge(h_ok, NT)
            for t in range(NT):
                for nb in range(2):
                    dve.wait_ge(wout_ps, 2 * t + nb + 1)
                    ins = stt(xh[:, t, nb * 512:(nb + 1) * 512], xh[:, t, nb * 512:(nb + 1) * 512], DN_ALPHA,
                              bank[((1, 4), (2, 3))[t][nb]][:, :], ALU.mult, ALU.add)
                    link(ins)
                moments(xh[:, t, :], P, t)
                ts(vtmp[:, t:t + 1], mv[:, t, 1:2], LN_EPS, None, ALU.add).then_inc(var1, 1)
                dve.wait_ge(rstd1, t + 1)
                dve.wait_ge(var1, t + 1)
                refine(rstd[:, t:t + 1], vtmp[:, t:t + 1], vnew[:, t:t + 1])
                ts(xh[:, t, :], xh[:, t, :], mv[:, t, 0:1], rstd[:, t:t + 1], ALU.subtract, ALU.mult).then_inc(h1_hat, 1)
            for t in range(NT):
                dve.wait_ge(h1T_ps, 2 * t + 2)
                for j in range(4):
                    kt = 4 + j
                    ins = ts(h1T[:, kt, t * P:(t + 1) * P], bank[(5, 7)[t]][:, j * P:(j + 1) * P], pcol[:, 56 + kt:57 + kt],
                             pcol[:, 64 + kt:65 + kt], ALU.mult, ALU.add)
                ins.then_inc(h1T_dve, 1)
            nc.vector.memset(gate[:, :, :], 0.0)
            nc.vector.memset(posm[:, :, :], -1.0)
            dve.wait_ge(late_in, 48)
            dve.wait_ge(logit_ps, 1)
            link(tt(logit, bank[4][:, 0:NT * NE].rearrange("p (t e) -> p t e", t=NT), rb.unsqueeze(1).broadcast_to([P, NT, NE]), ALU.add))
            for t in range(NT):
                ins = nc.vector.max(top8[:, t, :], logit[:, t, :])
            link(ins)
            ts(gmax, top8[:, :, 0], -1.0, None, ALU.mult).then_inc(top_ok, 1)
            for t in range(NT):
                ins = nc.vector.max_index(idx8[:, t, :], top8[:, t, :], logit[:, t, :])
            link(ins)
            link(copy(idxf, idx8[:, :, 0:4]))
            dve.wait_ge(iota_ok, 2)
            oh4 = onehot[:, :, :, :].rearrange("p t k e -> p (t k) e")
            gh4 = ghot[:, :, :, :].rearrange("p t k e -> p (t k) e")
            link(tt(oh4, iota[:, 0, 0:NE].unsqueeze(1).broadcast_to([P, NT * 4, NE]),
                    idxf[:, :, :].rearrange("p t k -> p (t k)").unsqueeze(2).broadcast_to([P, NT * 4, NE]), ALU.is_equal))
            nc.vector.tensor_reduce(mask, onehot[:, :, :, :].rearrange("p t k e -> p t e k"), AX_X, ALU.add).then_inc(mask_ok, 1)
            dve.wait_ge(gexp, 1)
            link(nc.vector.tensor_reduce(gsum, gate4[:, :, 0:4], AX_X, ALU.add))
            link(nc.vector.reciprocal(gsum, gsum))
            link(tt(gate4[:, :, 4:8], gate4[:, :, 0:4], gsum.unsqueeze(2).broadcast_to([P, NT, 4]), ALU.mult))
            for t in range(NT):
                ins = tt(ghot[:, t, :, :], onehot[:, t, :, :], gate4[:, t, 4:8].unsqueeze(2).broadcast_to([P, 4, NE]), ALU.mult)
            link(ins)
            nc.vector.tensor_reduce(gate[:, :, 0:NE], ghot[:, :, :, :].rearrange("p t k e -> p t e k"), AX_X, ALU.add).then_inc(mask_ok, 1)
            dve.wait_ge(pos_ps, 1)
            link(stt(posm[:, :, 0:NE], bank[5][:, 0:NT * NE].rearrange("p (t e) -> p t e", t=NT), 1.0, mask, ALU.add, ALU.mult))
            link(ts(posm[:, :, 0:NE], posm[:, :, 0:NE], -1.0, None, ALU.add))
            dve.wait_ge(mask_ok, 2)

            def select(n, e, par, j=0):
                if not isinstance(n, int) or n >= 2:
                    dve.wait_ge(gath_ps, n - 1)
                    dve.wait_ge(u_ps, n - 1)
                    dve.wait_ge(selT_ps, n - 1)
                at = (slice(e, e + 1) if isinstance(e, int) else bass.ds(e, 1))
                jj = j if isinstance(j, int) else bass.ds(j, 1)
                slots = iota[:, jj, :] if isinstance(j, int) else iota[:, jj, :].rearrange("p a s -> p (a s)")
                for t in range(NT):
                    ts(sel[:, par, t, :], slots[:, 0:SL], posm[:, t, at], None, ALU.is_equal)
                    ts(selG[:, par, t, :], slots, posm[:, t, at], gate[:, t, at], ALU.is_equal, ALU.mult)
                ts(oh[:, par, :], ones[0:96, 0:SL], eid[0:96, at], None, ALU.mult).then_inc(sel_ok, 1)

            select(0, 0, 0)
            for j in range(1, NJ):
                ins = ts(flag[:, j - 1, :], bank[5][0:1, 2 * NE:3 * NE], float(SL * j), None, ALU.is_gt)
            link(ins)
            flagf = flag[:, :, :].rearrange("p j e -> p (j e)")
            link(nc.vector.tensor_tensor_scan(rank, flagf, ones[0:1, 0:3 * NE], 0.0, ALU.add, ALU.mult))
            copy(xcount, rank[:, 3 * NE - 1:3 * NE]).then_inc(list_ok, 1)
            dve.wait_ge(GT_ps, 1)
            copy(GT, bank[6][0:NE, 0:SEQ]).then_inc(GT_ok, 1)

            def tile(n, par, first, after):
                if after is not None:
                    select(n + 1, after, 1 - par)
                dve.wait_ge(g_ps, n + 1)
                ts(a_c, bank[4][:, :], LIMIT, None, ALU.min).then_inc(a_ok, 1)
                dve.wait_ge(u_ps, n + 1)
                if not first:
                    dve.wait_ge(hidT_ps, n)
                ts(u_c, bank[5][:, :], LIMIT, -LIMIT, ALU.min, ALU.max).then_inc(u_ok, 1)
                dve.wait_ge(sig_ok, n + 1)
                tt(a_c, a_c, s_c, ALU.mult).then_inc(as_ok, 1)
                dve.wait_ge(u_ok, n + 1)
                dve.wait_ge(as_ok, n + 1)
                stt(u_c, u_c, 1.0, a_c, ALU.add, ALU.mult).then_inc(hid_ok, 1)
                dve.wait_ge(d_ps, n + 1)
                if not first:
                    dve.wait_ge(scat, n)
                copy(y_s, bank[6][:, :]).then_inc(yd_ok, 1)

            for k in range(UNROLL):
                tile(k, k % 2, k == 0, k + 1)
            with dve.Fori(1, NE // UNROLL) as it:
                for k in range(UNROLL):
                    tile(it * UNROLL + k, k % 2, False, it * UNROLL + (k + 1))
            nx = dve.value_load(xcount[0:1, 0:1], min_val=0, max_val=MAXX)
            with dve.If(nx > 0):
                dve.wait_ge(scat, NE)
                link_x = [0]

                def lx(ins):
                    link_x[0] += 1
                    ins.then_inc(xstep, 1)
                    dve.wait_ge(xstep, link_x[0])
                for j in range(1, NJ):
                    ts(flag_j[:, j - 1, :], flag[:, j - 1, :], float(j), None, ALU.mult)
                lx(tt(flag_e[:, :, :], flag[:, :, :], iota[0:1, 0, 0:NE].unsqueeze(1).broadcast_to([1, 3, NE]), ALU.mult))
                for i in range(MAXX):
                    for src, dst in ((flag_e, xlf[:, 0, :]), (flag_j, xlf[:, 1, :])):
                        lx(stt(xscr, rank, float(i + 1), src[:, :, :].rearrange("p j e -> p (j e)"), ALU.is_equal, ALU.mult,
                               accum_out=dst[:, i:i + 1]))
                copy(xlist2[:, :, :], xlf[:, :, :]).then_inc(list_ok, 1)
                dve.wait_ge(list_ok, 2)
                with dve.Fori(0, nx) as i:
                    e = dve.value_load(xlist[0:1, bass.ds(i, 1)], min_val=0, max_val=NE - 1)
                    j = dve.value_load(xlist2[0:1, 1, bass.ds(i, 1)], min_val=1, max_val=NJ - 1)
                    select(i + (NE + 1), e, 0, j)
                    tile(i + NE, 0, False, None)
            dve.wait_ge(scat, nx + NE)
            dve.wait_ge(ln2_in, 32)
            for t in range(NT):
                for h in range(2):
                    at = slice(h * 512, (h + 1) * 512)
                    link(stt(z2[:, t, at], xh[:, t, at], DN_ALPHA, bank[2 * t + h][:, :], ALU.mult, ALU.add))
                moments(z2[:, t, :], P, t)
                ts(vtmp[:, t:t + 1], mv[:, t, 1:2], LN_EPS, None, ALU.add).then_inc(z2_ok, 1)
            for t in range(NT):
                dve.wait_ge(rstd2, t + 1)
                dve.wait_ge(z2_ok, t + 1)
                refine(rstd[:, t:t + 1], vtmp[:, t:t + 1], vnew[:, t:t + 1])
                link(ts(z2[:, t, :], z2[:, t, :], mv[:, t, 0:1], rstd[:, t:t + 1], ALU.subtract, ALU.mult))
                link(tt(z2[:, t, :], z2[:, t, :], lnbc[:, 0, :], ALU.mult))
                tt(z2[:, t, :], z2[:, t, :], lnbc[:, 1, :], ALU.add).then_inc(fin, 1)


_INS = ["x", "meta_tokens", "ln_in_g", "ln_in_b", "w_in", "gla_w_a2", "gla_b_a", "gla_norm_g", "ssd_conv_w", "ssd_conv_b",
        "ssd_dt_bias", "ssd_a_log", "ssd_d", "ssd_norm_g", "w_out", "ln1_g", "ln1_b", "router_w", "router_b",
        "moe_w_gate", "moe_w_up", "moe_b_gate", "moe_b_up", "moe_w_down", "moe_b_down", "ln2_g", "ln2_b"]


def kernel(**inputs):
    import numpy as np
    import concourse.bacc as bacc
    from concourse.bass_utils import run_bass_kernel_spmd

    nc = bacc.Bacc("TRN2", target_bir_lowering=False, num_devices=1)
    arrays, args = {}, []
    for name in _INS:
        a = np.ascontiguousarray(inputs[name])
        arrays[f"in_{name}"] = a
        args.append(nc.dram_tensor(f"in_{name}", a.shape, mybir.dt.from_np(a.dtype), kind="ExternalInput").ap())
    args.append(nc.dram_tensor("out_h", (1, SEQ, D), F32, kind="ExternalOutput").ap())
    build(nc, *args)
    return run_bass_kernel_spmd(nc, [arrays], core_ids=[0]).results[0]["out_h"]
```

```python
import concourse.bass as bass
from concourse import mybir
from contextlib import ExitStack

F32 = mybir.dt.float32
BF16 = mybir.dt.bfloat16
I32 = mybir.dt.int32
U32 = mybir.dt.uint32
ALU = mybir.AluOpType
ACT = mybir.ActivationFunctionType
AX_X = mybir.AxisListType.X

P = 128
D = 1024
KT = D // P
SEQ = 256
NT = SEQ // P
META = 16
TOK = META + SEQ
CHUNK = 64
NCH = SEQ // CHUNK
GKEY, GVAL, GH, GDK, GDV, GRANK = 256, 512, 4, 64, 128, 16
TAU = 16.0
SIN, SHD, SHEADS, SGRP, SST, NCONV = 512, 64, 8, 2, 128, 4
XBC = SIN + 2 * SGRP * SST
XC = XBC // P
NE, FF = 32, 1024
LIMIT, SALPHA = 7.0, 1.702
DN_ALPHA = 2.0 ** 0.25
LN_EPS, RMS_EPS = 1e-5, 1e-6

C_Q, C_K, C_V, C_OG, C_A1, C_Z = 0, 256, 512, 1024, 1536, 1552
C_XBC, C_DT = C_Z + SIN, C_Z + SIN + XBC

RING = 16
UW = 2048
UPE = 3 * D * FF // (P * UW)
UNROLL = 4
SL = 64
NJ = SEQ // SL
MAXX = NT * P * 4 // SL

W_ORDER = [C_XBC + 256 * i for i in range(4)] + [C_K, C_V, C_V + 256, C_Q, C_Z, C_Z + 256, C_OG, C_OG + 256]
U_XBC, U_K, U_V, U_Q, U_Z, U_OG, U_OUT = 0, 4, 5, 7, 8, 10, 12


def build(nc, x, meta, ln_in_g, ln_in_b, w_in, gla_w_a2, gla_b_a, gla_norm_g, ssd_conv_w, ssd_conv_b,
          ssd_dt_bias, ssd_a_log, ssd_d, ssd_norm_g, w_out, ln1_g, ln1_b, router_w, router_b,
          w_gate, w_up, b_gate, b_up, w_down, b_down, ln2_g, ln2_b, out):
    with ExitStack() as ctx:
        def sb(name, shape, dt=F32):
            return ctx.enter_context(nc.sbuf_tensor(name, shape, dt))

        def sem(name):
            return ctx.enter_context(nc.semaphore(name))

        ring = sb("ring", [P, RING, UW])
        arena = sb("arena", [P, 19392])
        bank = [ctx.enter_context(nc.psum_tensor(f"bank{i}", [P, 512], F32)) for i in range(8)]

        def cut(at, *shape, parts=P, dt=F32):
            n = 1
            for s in shape:
                n *= s
            words = n if dt in (F32, I32, U32) else n // 2
            v = arena[0:parts, at:at + words]
            if dt is not F32:
                v = v.bitcast(dt)
            if len(shape) == 2:
                v = v.rearrange("p (a b) -> p a b", a=shape[0])
            if len(shape) == 3:
                v = v.rearrange("p (a b c) -> p a b c", a=shape[0], b=shape[1])
            return v

        xh = cut(0, NT, D)
        metah = cut(2048, D, parts=META)
        k_m = cut(2048, GKEY, parts=META)
        v_m = cut(2304, GVAL, parts=META)
        la_m = cut(2816, GKEY, parts=META)
        hT = cut(3072, KT, TOK)
        mixT = cut(3072, KT, SEQ)
        h1T = cut(3072, KT, SEQ)
        lnbc = cut(5248, 2, D)
        normg = cut(7296, D)
        v_t = cut(8320, NT, GVAL)
        og = cut(8320, NT, GVAL)
        k_t = cut(9344, NT, GKEY)
        tmp = cut(9856, NT, GKEY)
        z_t = cut(9344, NT, SIN)
        o_n = cut(10368, NT, GVAL)
        la = cut(10368, NT, GKEY)
        expD = cut(10880, GKEY)
        qT = cut(11136, 2, SEQ)
        cacc = cut(11648, 2, TOK)
        csig = cut(12192, 2, TOK)
        CT = cut(12736, SGRP, SEQ)
        xs = cut(13248, 3, SIN)
        y1 = cut(14784, NT, SIN)
        Bt = cut(15808, 3, SGRP * SST)
        Sg = cut(16576, NCH + 1, 2, GDV)
        prow = cut(16576, P, parts=72)
        w_a2e = cut(16704, GKEY, parts=25)
        w_small = cut(16960, KT, 24)
        Ss = cut(17856, 3, SIN)
        sT = cut(17856, TOK, parts=25)
        b_dn = cut(11648, D, parts=NE)
        rw = cut(12672, KT, NE)
        rb = cut(12928, NE)
        eid = cut(13100, NE + 1)
        bparts = cut(13248, 2, FF, parts=96, dt=BF16)
        braw = cut(16576, 2, FF, parts=96)
        xT = cut(8320, 2, KT, SL)
        a_c = cut(9344, 512)
        s_c = cut(9856, 512)
        u_c = cut(11136, 512)
        hidT = cut(10368, 4, P)
        y_s = cut(14784, 512)
        GT = cut(15296, SEQ, parts=NE)
        selG = cut(7296, 2, NT, P)
        sel = cut(7808, 2, NT, SL)
        selGT = cut(15808, SEQ)
        oh = cut(16064, 2, SL, parts=96, dt=BF16)
        iota = cut(18624, NJ, P)
        tri_s = cut(12960, P)
        z2 = cut(11648, NT, D)
        logit = cut(2048, NT, NE)
        top8 = cut(2112, NT, 8)
        idx8 = cut(2128, NT, 8, dt=U32)
        idxf = cut(2144, NT, 4)
        onehot = cut(2160, NT, 4, NE)
        ghot = cut(2416, NT, 4, NE)
        mask = cut(2672, NT, NE)
        gate = cut(2736, NT, NE + 1)
        posm = cut(2802, NT, NE + 1)
        gate4 = cut(2868, NT, 8)
        flag = cut(8064, 3, NE, parts=1)
        rank = cut(8160, 3 * NE, parts=1)
        xcount = cut(8256, 1, parts=1, dt=I32)
        xlist2 = cut(8260, 2, MAXX, parts=1, dt=I32)
        xlist = xlist2[:, 0, :]
        flag_e = cut(9344, 3, NE, parts=1)
        flag_j = cut(9440, 3, NE, parts=1)
        xlf = cut(9536, 2, MAXX, parts=1)
        xscr = cut(9568, 3 * NE, parts=1)

        small = sb("small", [P, 336])
        o = [0]

        def sm(*shape):
            n = 1
            for s in shape:
                n *= s
            v = small[:, o[0]:o[0] + n]
            o[0] += n
            if len(shape) == 2:
                v = v.rearrange("p (a b) -> p a b", a=shape[0])
            return v

        stats = sm(2, 6)
        mv = sm(3, 2)
        rstd = sm(3)
        vtmp = sm(3)
        pcol = sm(72)
        dtb = sm(SHEADS)
        alog = sm(SHEADS)
        dskip = sm(SHEADS)
        dt_x = sm(3, SHEADS)
        dt_a = sm(3, SHEADS)
        dt_b = sm(3, SHEADS)
        dt_c = sm(3, SHEADS)
        dt_w = sm(3, SHEADS)
        decs = sm(NCH, SHEADS)
        decg = sm(8)
        ssy, sso = sm(4), sm(8)
        rm, rr, rmt = sm(12), sm(12), sm(12)
        rry, rro = rr[:, 0:4], rr[:, 4:12]
        vnew = sm(3)
        gmax = sm(NT)
        gsum = sm(NT)
        ident = sb("ident", [P, P])
        tri = sb("tri", [P, P])
        ones = sb("ones", [P, P])
        x_in = [sem(f"x_in{t}") for t in range(NT)]
        meta_in, params_in, small_in, lnin_in, normg_in = sem("meta_in"), sem("params_in"), sem("small_in"), sem("lnin_in"), sem("normg_in")
        ln1_in, ln2_in, bias_in, late_in, out_done = sem("ln1_in"), sem("ln2_in"), sem("bias_in"), sem("late_in"), sem("out_done")
        landed = [sem(f"landed{s}") for s in range(RING)]
        unit_used = sem("unit_used")
        half_used = sem("half_used")
        consts, zeroed, pads = sem("consts"), sem("zeroed"), sem("pads")
        pe_step, dve_step, act_step, pool_step, xstep = sem("pe_step"), sem("dve_step"), sem("act_step"), sem("pool_step"), sem("xstep")
        var_in, rstd_in, xhat = sem("var_in"), sem("rstd_in"), sem("xhat")
        pcol_ps, pcol_ok, hT_ps, hT_act, hT_dve, h_ok = sem("pcol_ps"), sem("pcol_ok"), sem("hT_ps"), sem("hT_act"), sem("hT_dve"), sem("h_ok")
        conv_ps, conv, csig_ok, silu, cT_ps, cT_ok = sem("conv_ps"), sem("conv"), sem("csig_ok"), sem("silu"), sem("cT_ps"), sem("cT_ok")
        sT_ps, sT_ok, dtT_ps, dtx_ok, dt_e, dt_ok = sem("sT_ps"), sem("sT_ok"), sem("dtT_ps"), sem("dtx_ok"), sem("dt_e"), sem("dt_ok")
        dsum_ps, dsum_ok, wx_ok, y1_ok = sem("dsum_ps"), sem("dsum_ok"), sem("wx_ok"), sem("y1_ok")
        la_ps, la_sp, la_ok, D_ps, D_ok, kdec = sem("la_ps"), sem("la_sp"), sem("la_ok"), sem("D_ps"), sem("D_ok"), sem("kdec")
        k_ps, v_ps, v_ok, q_ps, q_ok = sem("k_ps"), sem("v_ps"), sem("v_ok"), sem("q_ps"), sem("q_ok")
        us_ps, Ss_ok, ug_ps, Sg_ok, y_ps, o_ps = sem("us_ps"), sem("Ss_ok"), sem("ug_ps"), sem("Sg_ok"), sem("y_ps"), sem("o_ps")
        z_ps, z_sig, z_ok, og_ps, og_sig = sem("z_ps"), sem("z_sig"), sem("z_ok"), sem("og_ps"), sem("og_sig")
        y_mid, ssq, rms_in, rms, mix_y, o_ok, mix_o = sem("y_mid"), sem("ssq"), sem("rms_in"), sem("rms"), sem("mix_y"), sem("o_ok"), sem("mix_o")
        mixT_ps, mixT_act, mixT_dve, wout_ps = sem("mixT_ps"), sem("mixT_act"), sem("mixT_dve"), sem("wout_ps")
        var1, rstd1, h1_hat, h1_ok, h1T_ps, h1T_act, h1T_dve, logit_ps = (sem("var1"), sem("rstd1"), sem("h1_hat"), sem("h1_ok"), sem("h1T_ps"),
                                                                          sem("h1T_act"), sem("h1T_dve"), sem("logit_ps"))
        top_ok, gexp, mask_ok, pos_ps, GT_ps, GT_ok = sem("top_ok"), sem("gexp"), sem("mask_ok"), sem("pos_ps"), sem("GT_ps"), sem("GT_ok")
        iota_ok, bparts_ok, list_ok = sem("iota_ok"), sem("bparts_ok"), sem("list_ok")
        sel_ok, gath_ps, xT_ok, selT_ps, selGT_ok = sem("sel_ok"), sem("gath_ps"), sem("xT_ok"), sem("selT_ps"), sem("selGT_ok")
        g_ps, u_ps, a_ok, sig_ok, u_ok, as_ok, hid_ok = sem("g_ps"), sem("u_ps"), sem("a_ok"), sem("sig_ok"), sem("u_ok"), sem("as_ok"), sem("hid_ok")
        hidT_ps, hidT_ok, d_ps, yd_ok = sem("hidT_ps"), sem("hidT_ok"), sem("d_ps"), sem("yd_ok")
        scat = [sem(f"scat{t}") for t in range(NT)]
        z2_ok, rstd2, rstd_ok, scaled, fin0, fin1 = sem("z2_ok"), sem("rstd2"), sem("rstd_ok"), sem("scaled"), sem("fin0"), sem("fin1")

        def linker(eng, s):
            n = [0]

            def link(ins):
                n[0] += 1
                ins.then_inc(s, 1)
                eng.wait_ge(s, n[0])
            return link

        def unit_src(e, u):
            m = (w_gate, w_up, w_down)[u // (UPE // 3)]
            q = u % (UPE // 3)
            return m[0, e].rearrange("(k p) n -> p k n", p=P)[:, 2 * q:2 * q + 2, :] if isinstance(e, int) else \
                m[0, bass.ds(e, 1)].rearrange("a (k p) n -> p (a k) n", p=P)[:, 2 * q:2 * q + 2, :]

        def slot(s):
            return ring[:, s, :].rearrange("p (k n) -> p k n", k=2)

        block = ctx.enter_context(nc.Block())

        @block.sync
        def _(sp):
            for t in range(NT):
                sp.dma_start(xh[:, t, :], x[0, t * P:(t + 1) * P, :]).then_inc(x_in[t], 16)
            sp.dma_start(prow[0:8, :], ln_in_g.rearrange("(c p) -> c p", p=P)).then_inc(params_in, 16)
            sp.dma_start(prow[8:16, :], ln_in_b.rearrange("(c p) -> c p", p=P)).then_inc(params_in, 16)
            sp.dma_start(prow[16:48, :], ssd_conv_w[0].rearrange("j (c p) -> (j c) p", p=P)).then_inc(params_in, 16)
            sp.dma_start(prow[48:56, :], ssd_conv_b[0].rearrange("(c p) -> c p", p=P)).then_inc(params_in, 16)
            sp.dma_start(prow[56:64, :], ln1_g[0].rearrange("(c p) -> c p", p=P)).then_inc(params_in, 16)
            sp.dma_start(prow[64:72, :], ln1_b[0].rearrange("(c p) -> c p", p=P)).then_inc(params_in, 16)
            for n, c0 in enumerate(W_ORDER):
                sp.dma_start(ring[:, n, :].rearrange("p (k n) -> p k n", k=KT),
                             w_in[0, :, c0:c0 + 256].rearrange("(k p) n -> p k n", p=P)).then_inc(landed[n], 16)
                if n == 3:
                    sp.dma_start(w_small[:, :, 0:GRANK], w_in[0, :, C_A1:C_A1 + GRANK].rearrange("(k p) n -> p k n", p=P)).then_inc(small_in, 16)
                    sp.dma_start(w_small[:, :, GRANK:24], w_in[0, :, C_DT:C_DT + SHEADS].rearrange("(k p) n -> p k n", p=P)).then_inc(small_in, 16)
                    sp.wait_ge(zeroed, 1)
                    sp.dma_start(w_a2e[0:GRANK, :], gla_w_a2[0]).then_inc(small_in, 16)
                    sp.dma_start(w_a2e[24:25, :], gla_b_a).then_inc(small_in, 16)
                    sp.dma_start(dtb, ssd_dt_bias.broadcast_to([P, SHEADS])).then_inc(small_in, 16)
                    sp.dma_start(alog, ssd_a_log.broadcast_to([P, SHEADS])).then_inc(small_in, 16)
                    sp.dma_start(dskip, ssd_d.broadcast_to([P, SHEADS])).then_inc(small_in, 16)
            sp.dma_start(lnbc[:, 0, :], ln_in_g.rearrange("(a n) -> a n", a=1).broadcast_to([P, D])).then_inc(lnin_in, 16)
            sp.dma_start(lnbc[:, 1, :], ln_in_b.rearrange("(a n) -> a n", a=1).broadcast_to([P, D])).then_inc(lnin_in, 16)
            sp.dma_start(normg[:, 0:GVAL], gla_norm_g.broadcast_to([P, GVAL])).then_inc(normg_in, 16)
            sp.dma_start(normg[:, GVAL:D], ssd_norm_g.broadcast_to([P, SIN])).then_inc(normg_in, 16)
            for n in range(4):
                sp.dma_start(ring[:, U_OUT + n, :].rearrange("p (k n) -> p k n", k=KT),
                             w_out[0, :, 256 * n:256 * n + 256].rearrange("(k p) n -> p k n", p=P)).then_inc(landed[U_OUT + n], 16)

            w_used = [(conv_ps, 2), (conv_ps, 4), (conv_ps, 6), (conv_ps, 8), (k_ps, 1), (half_used, 1), (v_ps, 3), (q_ps, 1),
                      (half_used, 2), (z_ps, 2), (half_used, 3), (og_ps, 2), (wout_ps, 3), (wout_ps, 3), (wout_ps, 4), (wout_ps, 4)]

            def experts(it, peeled):
                for i in range(UPE * UNROLL):
                    before = i - RING
                    if peeled and before < 0:
                        sp.wait_ge(*w_used[i])
                    else:
                        k, u = before // UPE, before % UPE
                        m, q = u // 4, u % 4
                        if q == 3:
                            sp.wait_ge((g_ps, u_ps, d_ps)[m], it * UNROLL + (k + 1))
                        else:
                            sp.wait_ge(unit_used, (it * UNROLL + k) * 9 + (3 * m + q + 1))
                    sp.dma_start(slot(i % RING), unit_src(it * UNROLL + i // UPE, i % UPE)).then_inc(landed[i % RING], 16)
            experts(0, True)
            with sp.Fori(1, NE // UNROLL) as it:
                experts(it, False)
            sp.wait_ge(list_ok, 1)
            nx = sp.value_load(xcount[0:1, 0:1], min_val=0, max_val=MAXX)
            with sp.If(nx > 0):
                sp.wait_ge(list_ok, 2)
                with sp.Fori(0, nx) as i:
                    sp.wait_ge(d_ps, i + NE)
                    e = sp.value_load(xlist[0:1, bass.ds(i, 1)], min_val=0, max_val=NE - 1)
                    for u in range(UPE):
                        sp.dma_start(slot(u), unit_src(e, u)).then_inc(landed[u], 16)
            sp.wait_ge(fin0, 1)
            sp.dma_start(out[0, 0:P, :], z2[:, 0, :]).then_inc(out_done, 16)

        @block.gpsimd
        def _(pool):
            link = linker(pool, pool_step)
            link(nc.gpsimd.memset(ident[:, :], 0.0))
            nc.gpsimd.affine_select(out=ident[:, :], in_=ident[:, :], compare_op=ALU.not_equal, fill=1.0,
                                    base=0, pattern=[[-1, P]], channel_multiplier=1).then_inc(consts, 1)
            nc.gpsimd.memset(ones[:, :], 1.0).then_inc(consts, 1)
            link(nc.gpsimd.memset(tri[:, :], 1.0 / TAU))
            link(nc.gpsimd.affine_select(out=tri[:, :], in_=tri[:, :], compare_op=ALU.is_gt, fill=0.0,
                                         base=0, pattern=[[-1, P]], channel_multiplier=1))
            nc.gpsimd.memset(tri[CHUNK:P, 0:CHUNK], 0.0).then_inc(consts, 1)
            for c in range(XC):
                pool.wait_ge(csig_ok, c + 1)
                if c < 6:
                    dst, at = cacc[:, c % 2, :], slice(0, TOK)
                else:
                    dst, at = CT[:, c - 6, :], slice(META, TOK)
                nc.gpsimd.tensor_tensor(dst, cacc[:, c % 2, at], csig[:, c % 2, at], ALU.mult).then_inc(silu, 1)
            pool.wait_ge(small_in, 112)
            pool.wait_ge(cT_ok, 4)
            for t in range(NT):
                ins = nc.gpsimd.tensor_tensor(y1[:, t, :].rearrange("p (h q) -> p h q", h=SHEADS),
                                              xs[:, t, :].rearrange("p (h q) -> p h q", h=SHEADS),
                                              dskip.unsqueeze(2).broadcast_to([P, SHEADS, SHD]), ALU.mult)
            ins.then_inc(y1_ok, 1)
            pool.wait_ge(lnin_in, 32)
            pool.wait_ge(hT_ps, KT)
            for t in range(NT):
                link(nc.gpsimd.tensor_tensor(xh[:, t, :], xh[:, t, :], lnbc[:, 0, :], ALU.mult))
                ins = nc.gpsimd.tensor_tensor(xh[:, t, :], xh[:, t, :], lnbc[:, 1, :], ALU.add)
                ins.then_inc(h_ok, 1)
            pool.wait_ge(y_ps, NCH)
            pool.wait_ge(o_ps, 2)
            nc.gpsimd.iota(iota[:, :, :].rearrange("p j (h s) -> p j h s", h=2), [[SL, NJ], [0, 2], [1, SL]], base=0,
                           channel_multiplier=0, allow_small_or_imprecise_dtypes=True).then_inc(iota_ok, 1)
            link(nc.gpsimd.memset(eid, 0.0))
            for q in range(3):
                v = eid[NE * q:NE * (q + 1), 0:NE]
                link(nc.gpsimd.affine_select(out=v, in_=v, compare_op=ALU.not_equal, fill=1.0, base=0, pattern=[[-1, NE]],
                                             channel_multiplier=1))
            link(nc.gpsimd.memset(tri_s[:, :], 1.0))
            nc.gpsimd.affine_select(out=tri_s[:, :], in_=tri_s[:, :], compare_op=ALU.is_gt, fill=0.0, base=0, pattern=[[1, P]],
                                    channel_multiplier=-1).then_inc(iota_ok, 1)
            pool.wait_ge(ln1_in, 32)
            for t in range(NT):
                pool.wait_ge(h1T_ps, 2 * t + 2)
                link(nc.gpsimd.tensor_tensor(xh[:, t, :], xh[:, t, :], lnbc[:, 0, :], ALU.mult))
                nc.gpsimd.tensor_tensor(xh[:, t, :], xh[:, t, :], lnbc[:, 1, :], ALU.add).then_inc(h1_ok, 1)
            pool.wait_ge(scaled, 1)
            nc.gpsimd.tensor_tensor(z2[:, 0, :], z2[:, 0, :], lnbc[:, 1, :], ALU.add).then_inc(fin0, 1)

        @block.scalar
        def _(act):
            link = linker(act, act_step)
            act.dma_start(metah[:, :], meta).then_inc(meta_in, 16)

            def inv_sqrt(src, dst, wait_for, n, done):
                act.wait_ge(wait_for, n)
                link(nc.scalar.activation(dst, src, ACT.Ln))
                nc.scalar.activation(dst, dst, ACT.Exp, scale=-0.5).then_inc(done, 1)

            def mixT_evac(b, kt):
                nc.scalar.activation(mixT[:, kt:kt + 2, :].rearrange("p a n -> p (a n)"), b[:, :], ACT.Copy).then_inc(mixT_act, 1)

            inv_sqrt(vtmp, rstd, var_in, 1, rstd_in)
            act.wait_ge(pcol_ok, 1)
            for kt in range(0, KT, 2):
                act.wait_ge(hT_ps, kt + 1)
                nc.scalar.activation(hT[:, kt, :], bank[kt % 4][:, 0:TOK], ACT.Identity, bias=pcol[:, 8 + kt:9 + kt],
                                     scale=pcol[:, kt:kt + 1]).then_inc(hT_act, 1)

            def c_evac(c):
                act.wait_ge(cT_ps, c + 1)
                b = bank[7] if c % 2 == 0 else bank[3]
                dst, at = (xs, c * P) if c < 4 else (Bt, (c - 4) * P)
                nc.scalar.activation(dst[:, 0:NT, at:at + P], b[:, 0:2 * P].rearrange("p (t n) -> p t n", t=NT), ACT.Copy)
                nc.scalar.activation(dst[0:META, 2, at:at + P], b[0:META, 2 * P:3 * P], ACT.Copy).then_inc(cT_ok, 1)

            for c in range(XC):
                act.wait_ge(conv, c + 1)
                if c >= 2:
                    act.wait_ge(silu, c - 1)
                nc.scalar.activation(csig[:, c % 2, :], cacc[:, c % 2, :], ACT.Sigmoid).then_inc(csig_ok, 1)
                if c >= 2:
                    c_evac(c - 2)
            act.wait_ge(sT_ps, 1)
            nc.scalar.activation(sT[0:24, :], bank[0][0:24, 0:TOK], ACT.Copy).then_inc(sT_ok, 1)
            act.wait_ge(dtx_ok, 1)
            act.wait_ge(small_in, 112)
            flat = lambda v: v.rearrange("p a b -> p (a b)")
            link(nc.scalar.activation(alog, alog, ACT.Exp))
            link(nc.scalar.activation(flat(dt_a), flat(dt_x), ACT.Abs))
            link(nc.scalar.activation(flat(dt_a), flat(dt_a), ACT.Exp, scale=-1.0))
            nc.scalar.activation(flat(dt_b), flat(dt_a), ACT.Ln, bias=1.0).then_inc(dt_e, 1)
            act.wait_ge(la_ps, 1)
            tmpf = tmp[:, :, :].rearrange("p t n -> p (t n)")
            link(nc.scalar.activation(tmpf, bank[2][:, :], ACT.Abs))
            link(nc.scalar.activation(expD[0:META, :], bank[0][0:META, 0:GKEY], ACT.Abs))
            link(nc.scalar.activation(tmpf, tmpf, ACT.Exp, scale=-1.0))
            link(nc.scalar.activation(expD[0:META, :], expD[0:META, :], ACT.Exp, scale=-1.0))
            link(nc.scalar.activation(tmpf, tmpf, ACT.Ln, bias=1.0))
            nc.scalar.activation(expD[0:META, :], expD[0:META, :], ACT.Ln, bias=1.0).then_inc(la_sp, 1)
            act.wait_ge(dsum_ps, 1)
            nc.scalar.activation(flat(dt_w[:, 0:NT, :]), bank[6][:, 0:16], ACT.Exp, scale=TAU)
            nc.scalar.activation(dt_w[0:META, 2, :], bank[6][0:META, 16:24], ACT.Exp, scale=TAU)
            nc.scalar.activation(flat(decs), bank[6][:, 32:64], ACT.Exp).then_inc(dsum_ok, 1)
            act.wait_ge(D_ps, 1)
            nc.scalar.activation(tmpf, bank[2][:, :], ACT.Exp)
            nc.scalar.activation(expD[0:META, :], bank[0][0:META, 0:GKEY], ACT.Exp)
            nc.scalar.activation(decg, bank[0][:, GKEY:GKEY + 8], ACT.Exp, scale=1.0 / TAU).then_inc(D_ok, 1)
            act.wait_ge(h_ok, NT)
            act.dma_start(lnbc[:, 0, :], ln1_g.broadcast_to([P, D])).then_inc(ln1_in, 16)
            act.dma_start(lnbc[:, 1, :], ln1_b.broadcast_to([P, D])).then_inc(ln1_in, 16)
            for n, (dst, b) in enumerate(((v_t[:, 0, :], bank[5]), (v_t[:, 1, :], bank[7]), (v_m, bank[3]))):
                act.wait_ge(v_ps, n + 1)
                nc.scalar.activation(dst, b[0:dst.shape[0], :], ACT.Copy).then_inc(v_ok, 1)
            act.wait_ge(q_ps, 1)
            nc.scalar.activation(qT[:, :, :].rearrange("p a n -> p (a n)"), bank[5][:, :], ACT.Copy, scale=GDK ** -0.5).then_inc(q_ok, 1)
            for t in range(NT):
                act.wait_ge(z_ps, t + 1)
                act.wait_ge(kdec, 1)
                act.wait_ge(ug_ps, 3)
                nc.scalar.activation(z_t[:, t, :], bank[(0, 5)[t]][:, :], ACT.Sigmoid).then_inc(z_sig, 1)
            scr = cacc[:, :, :].rearrange("p a b -> p (a b)")
            scr_o = csig[:, :, :].rearrange("p a b -> p (a b)")
            for r in range(2):
                act.wait_ge(y_mid, r + 1)
                if r:
                    link(last_y)
                for g in range(SGRP):
                    last_y = nc.scalar.activation(scr[:, g * 256:(g + 1) * 256], y1[:, r, g * 256:(g + 1) * 256], ACT.Square,
                                                  accum_out=ssy[:, r * 2 + g:r * 2 + g + 1])
                act.wait_ge(o_ps, r + 1)
                if r:
                    link(last_y)
                for t in range(NT):
                    for i in range(2):
                        n = t * 4 + 2 * i + r
                        at = (2 * t + i) * GDV
                        last_o = nc.scalar.activation(scr_o[:, at:at + GDV], bank[3 - r][:, t * 256 + i * P:t * 256 + (i + 1) * P],
                                                      ACT.Square, accum_out=sso[:, n:n + 1])
                if r == 0:
                    last_y = last_o
            last_o.then_inc(ssq, 1)
            inv_sqrt(rm, rr, rms_in, 1, rms)
            act.wait_ge(ssq, 1)
            act.wait_ge(y_ps, NCH)
            act.dma_start(rw[:, :, :], router_w[0].rearrange("(k p) e -> p k e", p=P)).then_inc(late_in, 16)
            act.dma_start(rb, router_b.broadcast_to([P, NE])).then_inc(late_in, 16)
            act.dma_start(b_dn[:, :], b_down[0]).then_inc(late_in, 16)
            for q in range(3):
                act.dma_start(braw[NE * q:NE * (q + 1), 0, :], b_gate[0]).then_inc(bias_in, 16)
                act.dma_start(braw[NE * q:NE * (q + 1), 1, :], b_up[0]).then_inc(bias_in, 16)

            def og_sigmoid(t):
                act.wait_ge(og_ps, t + 1)
                nc.scalar.activation(og[:, t, :], bank[(6, 7)[t]][:, :], ACT.Sigmoid).then_inc(og_sig, 1)

            og_sigmoid(0)
            og_sigmoid(1)
            act.wait_ge(mixT_ps, 1)
            mixT_evac(bank[0], 4)
            act.wait_ge(mixT_ps, 2)
            mixT_evac(bank[5], 6)
            act.wait_ge(mixT_ps, 3)
            mixT_evac(bank[6], 0)
            for t in range(NT):
                inv_sqrt(vtmp[:, t:t + 1], rstd[:, t:t + 1], var1, t + 1, rstd1)
            for t in range(NT):
                act.wait_ge(h1T_ps, 2 * t + 1)
                for kt in range(4):
                    ins = nc.scalar.activation(h1T[:, kt, t * P:(t + 1) * P], bank[(0, 6)[t]][:, kt * P:(kt + 1) * P], ACT.Identity,
                                               bias=pcol[:, 64 + kt:65 + kt], scale=pcol[:, 56 + kt:57 + kt])
                ins.then_inc(h1T_act, 1)
            act.wait_ge(top_ok, 1)
            for t in range(NT):
                ins = nc.scalar.activation(gate4[:, t, 0:4], top8[:, t, 0:4], ACT.Exp, bias=gmax[:, t:t + 1])
            ins.then_inc(gexp, 1)

            act.wait_ge(GT_ps, 1)
            nc.scalar.activation(GT, bank[6][0:NE, 0:SEQ], ACT.Copy).then_inc(GT_ok, 1)
            act.wait_ge(h1_ok, NT)
            act.dma_start(lnbc[:, 0, :], ln2_g.broadcast_to([P, D])).then_inc(ln2_in, 16)
            act.dma_start(lnbc[:, 1, :], ln2_b.broadcast_to([P, D])).then_inc(ln2_in, 16)

            def xT_evac(n, par):
                act.wait_ge(gath_ps, n + 1)
                if not isinstance(n, int) or n >= 2:
                    act.wait_ge(u_ps, n - 1)
                nc.scalar.activation(xT[:, par, :, :].rearrange("p k s -> p (k s)"), bank[7][:, :], ACT.Copy).then_inc(xT_ok, 1)

            def tile(n, par, first, ahead):
                act.wait_ge(a_ok, n + 1)
                nc.scalar.activation(s_c, a_c, ACT.Sigmoid, scale=SALPHA).then_inc(sig_ok, 1)
                if ahead:
                    xT_evac(n + 1, 1 - par)
                act.wait_ge(selT_ps, n + 1)
                nc.scalar.activation(selGT, bank[6][:, 0:SEQ], ACT.Copy).then_inc(selGT_ok, 1)
                act.wait_ge(hidT_ps, n + 1)
                if not first:
                    act.wait_ge(d_ps, n)
                nc.scalar.activation(hidT[:, :, :].rearrange("p c n -> p (c n)"), bank[7][:, :], ACT.Copy).then_inc(hidT_ok, 1)

            xT_evac(0, 0)
            for k in range(UNROLL):
                tile(k, k % 2, k == 0, True)
            with act.Fori(1, NE // UNROLL) as it:
                for k in range(UNROLL):
                    tile(it * UNROLL + k, k % 2, False, True)
            act.wait_ge(list_ok, 1)
            nx = act.value_load(xcount[0:1, 0:1], min_val=0, max_val=MAXX)
            with act.If(nx > 0):
                with act.Fori(0, nx) as i:
                    xT_evac(i + (NE + 1), 0)
                    tile(i + NE, 0, False, False)
            for t in range(NT):
                inv_sqrt(vtmp[:, t:t + 1], rstd[:, t:t + 1], z2_ok, t + 1, rstd2)
                if t == 0:
                    act.wait_ge(rstd_ok, 1)
                    nc.scalar.activation(z2[:, 0, :], z2[:, 0, :], ACT.Copy, scale=rstd[:, 0:1]).then_inc(scaled, 1)
            for h in range(2):
                at = slice(h * 512, (h + 1) * 512)
                act.wait_ge(fin1, h + 1)
                act.dma_start(out[0, P:2 * P, at], z2[:, 1, at]).then_inc(out_done, 16)
            act.wait_ge(out_done, 48)

        @block.tensor
        def _(pe):
            link = linker(pe, pe_step)
            mm = nc.tensor.matmul
            tr = nc.tensor.transpose

            def wslot(n, kt, a=0, b=256):
                return ring[:, n, :].rearrange("p (k n) -> p k n", k=KT)[:, kt, a:b]

            pe.wait_ge(consts, 3)
            pe.wait_ge(params_in, 96)
            tr(bank[7][:, 0:72], prow[:, :], ident[0:72, 0:72]).then_inc(pcol_ps, 1)
            pe.wait_ge(xhat, 3)
            for kt in range(KT):
                if kt >= 4:
                    pe.wait_ge(hT_act if kt % 2 == 0 else hT_dve, kt // 2 - 1)
                b = bank[kt % 4]
                tr(b[:, 0:META], metah[:, kt * P:(kt + 1) * P], ident[0:META, 0:META])
                for t in range(NT):
                    ins = tr(b[:, META + t * P:META + (t + 1) * P], xh[:, t, kt * P:(kt + 1) * P], ident[:, :])
                ins.then_inc(hT_ps, 1)
            pe.wait_ge(hT_act, KT // 2)
            pe.wait_ge(hT_dve, KT // 2)
            pe.wait_ge(pads, 1)

            def c_transposes(c):
                b = bank[7] if c % 2 == 0 else bank[3]
                pe.wait_ge(silu, c + 1)
                if c == 0:
                    pe.wait_ge(pcol_ok, 1)
                if c >= 2:
                    pe.wait_ge(cT_ok, c - 1)
                src = cacc[:, c % 2, :]
                for t in range(NT):
                    tr(b[:, t * P:(t + 1) * P], src[:, META + t * P:META + (t + 1) * P], ident[:, :])
                tr(b[0:META, 2 * P:3 * P], src[:, 0:META], ident[:, :]).then_inc(cT_ps, 1)

            for c in range(XC):
                n = U_XBC + c // 2
                pe.wait_ge(landed[n], 16)
                if c >= 3:
                    pe.wait_ge(conv, c - 2)
                for kt in range(KT):
                    ins = mm(bank[4 + c % 3][:, 3:3 + TOK], wslot(n, kt, (c % 2) * P, (c % 2) * P + P), hT[:, kt, :],
                             start=kt == 0, stop=kt == KT - 1)
                ins.then_inc(conv_ps, 1)
                if c >= 2:
                    c_transposes(c - 2)
            pe.wait_ge(small_in, 112)
            for kt in range(KT):
                ins = mm(bank[0][0:24, 0:TOK], w_small[:, kt, :], hT[:, kt, :], start=kt == 0, stop=kt == KT - 1)
            ins.then_inc(sT_ps, 1)

            def token_major(out_x, out_m, n, cols=256):
                for t in range(NT):
                    for kt in range(KT):
                        ins = mm(out_x[t], hT[:, kt, META + t * P:META + (t + 1) * P], wslot(n, kt), start=kt == 0, stop=kt == KT - 1)
                if out_m is not None:
                    for kt in range(KT):
                        ins = mm(out_m, hT[:, kt, 0:META], wslot(n, kt), start=kt == 0, stop=kt == KT - 1)
                return ins

            pe.wait_ge(landed[U_K], 16)
            pe.wait_ge(conv, 7)
            token_major([bank[4][:, t * 256:(t + 1) * 256] for t in range(NT)], bank[1][0:META, 256:512], U_K).then_inc(k_ps, 1)
            pe.wait_ge(sT_ok, 1)
            for t in range(NT):
                tr(bank[1][:, t * 24:(t + 1) * 24], sT[0:24, META + t * P:META + (t + 1) * P], ident[0:24, 0:24])
            tr(bank[1][0:META, 48:72], sT[0:24, 0:META], ident[0:24, 0:24]).then_inc(dtT_ps, 1)
            for t in range(NT):
                mm(bank[2][:, t * 256:(t + 1) * 256], sT[:, META + t * P:META + (t + 1) * P], w_a2e[:, :], start=True, stop=True)
            mm(bank[0][0:META, 0:GKEY], sT[:, 0:META], w_a2e[:, :], start=True, stop=True).then_inc(la_ps, 1)
            pe.wait_ge(landed[U_V], 16)
            pe.wait_ge(conv, 8)
            pe.wait_ge(cT_ok, 6)
            token_major([bank[5][:, 0:256], bank[7][:, 0:256]], bank[3][0:META, 0:256], U_V).then_inc(half_used, 1)
            pe.wait_ge(dt_ok, 1)
            for t in range(NT):
                mm(bank[6][:, t * 8:(t + 1) * 8], tri[:, :], dt_c[:, t, :], start=True, stop=True)
            mm(bank[6][0:META, 16:24], tri[0:META, 0:META], dt_c[0:META, 2, :], start=True, stop=True)
            for c in (0, 2, 1, 3):
                r = CHUNK * (c % 2)
                if c == 1:
                    link(ins)
                ins = mm(bank[6][:, 32 + c * 8:40 + c * 8], ones[r:r + CHUNK, :], dt_c[r:r + CHUNK, c // 2, :], start=True, stop=True)
            ins.then_inc(dsum_ps, 1)
            pe.wait_ge(la_ok, 1)
            for t in range(NT):
                mm(bank[2][:, t * 256:(t + 1) * 256], tri[:, :], la[:, t, :], start=True, stop=True)
            mm(bank[0][0:META, 0:GKEY], tri[0:META, 0:META], la_m[:, :], start=True, stop=True)
            for c in (0, 2, 1, 3):
                r = CHUNK * (c % 2)
                if c == 1:
                    link(ins)
                for i in range(2):
                    ins = mm(bank[0][:, GKEY + i * 4 + c:GKEY + i * 4 + c + 1], la[r:r + CHUNK, c // 2, i * P:(i + 1) * P],
                             ones[r:r + CHUNK, 0:1], start=True, stop=True)
            ins.then_inc(D_ps, 1)
            pe.wait_ge(landed[U_V + 1], 16)
            n = U_V + 1
            for dst, at, m in ((bank[5], META, P), (bank[7], META + P, P), (bank[3], 0, META)):
                for kt in range(KT):
                    ins = mm(dst[0:m, 256:512], hT[:, kt, at:at + m], wslot(n, kt), start=kt == 0, stop=kt == KT - 1)
                ins.then_inc(v_ps, 1)
            pe.wait_ge(wx_ok, 1)
            ssd_banks = (1, 6, 4, 1, 6)

            def ssd_update(c):
                b = bank[ssd_banks[c]]
                for g in range(SGRP):
                    if c == 0:
                        k, w = Bt[0:META, 2, g * SST:(g + 1) * SST], xs[0:META, 2, g * 256:(g + 1) * 256]
                    else:
                        r = CHUNK * ((c - 1) % 2)
                        k, w = Bt[r:r + CHUNK, (c - 1) // 2, g * SST:(g + 1) * SST], xs[r:r + CHUNK, (c - 1) // 2, g * 256:(g + 1) * 256]
                    ins = mm(b[:, g * 256:(g + 1) * 256], k, w, start=True, stop=True)
                ins.then_inc(us_ps, 1)

            pe.wait_ge(kdec, 1)
            for c in range(3):
                ssd_update(c)
            pe.wait_ge(landed[U_Q], 16)
            pe.wait_ge(v_ok, 1)
            for i in range(2):
                for kt in range(KT):
                    ins = mm(bank[5][:, i * SEQ:(i + 1) * SEQ], wslot(U_Q, kt, i * P, (i + 1) * P), hT[:, kt, META:TOK],
                             start=kt == 0, stop=kt == KT - 1)
            ins.then_inc(q_ps, 1)
            pe.wait_ge(v_ok, 3)

            def gla_update(c):
                b, at = (bank[7], 0) if c == 0 else (bank[3] if c % 2 else bank[2], ((c - 1) // 2) * 256)
                for h in range(GH):
                    dst = b[64 * (h % 2):64 * (h % 2) + 64, at + (h // 2) * GDV:at + (h // 2 + 1) * GDV]
                    if c == 0:
                        kk, vv = k_m[:, h * GDK:(h + 1) * GDK], v_m[:, h * GDV:(h + 1) * GDV]
                    else:
                        r = CHUNK * ((c - 1) % 2)
                        kk, vv = k_t[r:r + CHUNK, (c - 1) // 2, h * GDK:(h + 1) * GDK], v_t[r:r + CHUNK, (c - 1) // 2, h * GDV:(h + 1) * GDV]
                    ins = mm(dst, kk, vv, start=True, stop=True)
                return ins

            gla_update(0).then_inc(ug_ps, 1)
            for c in (1, 3):
                ins = gla_update(c)
            ins.then_inc(ug_ps, 1)
            for c in (2, 4):
                ins = gla_update(c)
            ins.then_inc(ug_ps, 1)
            for c in (3, 4):
                pe.wait_ge(Ss_ok, c - 2 + 0)
                ssd_update(c)
            pe.wait_ge(q_ok, 1)
            for hf in range(2):
                n = U_Z + hf
                pe.wait_ge(landed[n], 16)
                for t in range(NT):
                    for kt in range(KT):
                        ins = mm(bank[(0, 5)[t]][:, hf * 256:(hf + 1) * 256], hT[:, kt, META + t * P:META + (t + 1) * P], wslot(n, kt),
                                 start=kt == 0, stop=kt == KT - 1)
                    if hf:
                        ins.then_inc(z_ps, 1)
                if not hf:
                    ins.then_inc(half_used, 1)
            def ssd_out(c):
                pe.wait_ge(Ss_ok, c + 1)
                r = CHUNK * ((c - 1) % 2)
                b = bank[(4, 1)[(c - 1) // 2]]
                for g in range(SGRP):
                    ins = mm(b[r:r + CHUNK, g * 256:(g + 1) * 256], CT[:, g, (c - 1) * CHUNK:c * CHUNK], Ss[:, c % 3, g * 256:(g + 1) * 256],
                             start=True, stop=True)
                ins.then_inc(y_ps, 1)
            pe.wait_ge(silu, XC)
            pe.wait_ge(Ss_ok, 3)
            def gla_out(hb):
                for c in range(1, NCH + 1):
                    r = CHUNK * ((c - 1) % 2)
                    t = (c - 1) // 2
                    for i in range(2):
                        q = qT[64 * hb:64 * hb + 64, i, (c - 1) * CHUNK:c * CHUNK]
                        ins = mm(bank[3 - hb][r:r + CHUNK, t * 256 + i * GDV:t * 256 + (i + 1) * GDV], q,
                                 Sg[64 * hb:64 * hb + 64, c, i, :], start=True, stop=True)
                ins.then_inc(o_ps, 1)

            for c in range(1, NCH):
                ssd_out(c)
            pe.wait_ge(Sg_ok, NCH + 1)
            gla_out(0)
            ssd_out(NCH)
            gla_out(1)

            def mix_transposes(b, src, kts):
                for j, kt in enumerate(kts):
                    for t in range(NT):
                        at = (kt % 4) * P
                        ins = tr(b[:, j * SEQ + t * P:j * SEQ + (t + 1) * P], src[:, t, at:at + P], ident[:, :])
                ins.then_inc(mixT_ps, 1)

            for hf in range(2):
                n = U_OG + hf
                pe.wait_ge(landed[n], 16)
                for t in range(NT):
                    for kt in range(KT):
                        ins = mm(bank[(6, 7)[t]][:, hf * 256:(hf + 1) * 256], hT[:, kt, META + t * P:META + (t + 1) * P], wslot(n, kt),
                                 start=kt == 0, stop=kt == KT - 1)
                    if hf:
                        ins.then_inc(og_ps, 1)
                if not hf:
                    ins.then_inc(half_used, 1)
            pe.wait_ge(mix_y, 2)
            mix_transposes(bank[0], z_t, (4, 5))
            mix_transposes(bank[5], z_t, (6, 7))

            def out_part(t, kts, first):
                for nb in range(2):
                    b = bank[((1, 4), (2, 3))[t][nb]]
                    for kt in kts:
                        ins = mm(b[:, :], mixT[:, kt, t * P:(t + 1) * P],
                                 ring[:, U_OUT + 2 * nb:U_OUT + 2 * nb + 2, kt * 256:(kt + 1) * 256],
                                 start=first and kt == kts[0], stop=(not first) and kt == kts[-1], skip_group_check=True)
                    if not first:
                        ins.then_inc(wout_ps, 1)

            for n in range(4):
                pe.wait_ge(landed[U_OUT + n], 16)
            pe.wait_ge(mixT_act, 2)
            out_part(0, (4, 5, 6, 7), True)
            pe.wait_ge(mix_o, 2)
            mix_transposes(bank[6], og, (0, 1))
            mix_transposes(bank[7], og, (2, 3))
            out_part(1, (4, 5, 6, 7), True)
            pe.wait_ge(mixT_act, 3)
            pe.wait_ge(mixT_dve, 1)
            out_part(0, (0, 1, 2, 3), False)
            out_part(1, (0, 1, 2, 3), False)
            for t in range(NT):
                pe.wait_ge(h1_hat, t + 1)
                for half in range(2):
                    b = bank[((0, 5), (6, 7))[t][half]]
                    for j in range(4):
                        kt = half * 4 + j
                        ins = tr(b[:, j * P:(j + 1) * P], xh[:, t, kt * P:(kt + 1) * P], ident[:, :])
                    ins.then_inc(h1T_ps, 1)
            pe.wait_ge(late_in, 48)
            for t in range(NT):
                pe.wait_ge(h1T_act, t + 1)
                pe.wait_ge(h1T_dve, t + 1)
                for kt in range(KT):
                    ins = mm(bank[4][:, t * NE:(t + 1) * NE], h1T[:, kt, t * P:(t + 1) * P], rw[:, kt, :], start=kt == 0, stop=kt == KT - 1)
            ins.then_inc(logit_ps, 1)
            pe.wait_ge(mask_ok, 1)
            pe.wait_ge(iota_ok, 2)
            mm(bank[5][:, 0:NE], tri_s[:, :], mask[:, 0, :], start=True, stop=True)
            mm(bank[5][:, NE:2 * NE], tri_s[:, :], mask[:, 1, :], start=True, stop=False)
            mm(bank[5][:, NE:2 * NE], ones[:, :], mask[:, 0, :], start=False, stop=True)
            mm(bank[5][0:1, 2 * NE:3 * NE], ones[:, 0:1], mask[:, 0, :], start=True, stop=False)
            mm(bank[5][0:1, 2 * NE:3 * NE], ones[:, 0:1], mask[:, 1, :], start=False, stop=True).then_inc(pos_ps, 1)
            pe.wait_ge(mask_ok, 2)
            for t in range(NT):
                ins = tr(bank[6][0:NE, t * P:(t + 1) * P], gate[:, t, 0:NE], ident[:, :])
            ins.then_inc(GT_ps, 1)
            def start_sums():
                pe.wait_ge(GT_ok, 1)
                for t in range(NT):
                    for h in range(2):
                        mm(bank[2 * t + h][:, :], GT[:, t * P:(t + 1) * P], b_dn[:, h * 512:(h + 1) * 512], start=True, stop=False,
                           skip_group_check=True)

            def gather(n, par):
                pe.wait_ge(sel_ok, n + 1)
                for kt in range(KT):
                    for t in range(NT):
                        ins = mm(bank[7][:, kt * SL:(kt + 1) * SL], xh[:, t, kt * P:(kt + 1) * P], sel[:, par, t, :], start=t == 0, stop=t == 1)
                ins.then_inc(gath_ps, 1)

            def scatter(n, t):
                pe.wait_ge(yd_ok, n + 1)
                for h in range(2):
                    ins = mm(bank[2 * t + h][:, :], selGT[h * SL:(h + 1) * SL, t * P:(t + 1) * P], y_s[h * SL:(h + 1) * SL, :],
                             start=False, stop=False, skip_group_check=True)
                ins.then_inc(scat[t], 1)

            def tile(n, par, first, unit_at, arrived, ahead, gathered):
                def hidden(m, b, free, done):
                    if not first:
                        pe.wait_ge(free, n)
                    for h in range(2):
                        mm(b[h * SL:(h + 1) * SL, :], oh[:, par, :], bparts[:, m, h * 512:(h + 1) * 512], start=True, stop=False)
                    for q in range(4):
                        arrived(4 * m + q)
                        for k in range(2):
                            kt = 2 * q + k
                            for h in range(2):
                                ins = mm(b[h * SL:(h + 1) * SL, :], xT[:, par, kt, :], slot(unit_at(4 * m + q))[:, k, h * 512:(h + 1) * 512],
                                         start=False, stop=kt == KT - 1)
                        ins.then_inc(done if q == 3 else unit_used, 1)

                pe.wait_ge(xT_ok, gathered + 1)
                hidden(0, bank[4], a_ok, g_ps)
                if ahead:
                    if not first:
                        pe.wait_ge(hidT_ok, n)
                    gather(n + 1, 1 - par)
                if ahead and not first:
                    scatter(n - 1, 0)
                hidden(1, bank[5], u_ok, u_ps)
                if ahead and not first:
                    scatter(n - 1, 1)
                if first:
                    start_sums()
                for t in range(NT):
                    ins = tr(bank[6][:, t * P:(t + 1) * P], selG[:, par, t, :], ident[:, :])
                ins.then_inc(selT_ps, 1)
                if ahead:
                    pe.wait_ge(xT_ok, n + 2)
                pe.wait_ge(hid_ok, n + 1)
                for c in range(4):
                    ins = tr(bank[7][:, c * P:(c + 1) * P], u_c[:, c * P:(c + 1) * P], ident[:, :])
                ins.then_inc(hidT_ps, 1)
                pe.wait_ge(selGT_ok, n + 1)
                pe.wait_ge(hidT_ok, n + 1)
                for q in range(4):
                    arrived(8 + q)
                    for k in range(2):
                        kt = 2 * q + k
                        for h in range(2):
                            ins = mm(bank[6][h * SL:(h + 1) * SL, :], hidT[:, kt % 4, (kt // 4) * SL:(kt // 4 + 1) * SL],
                                     slot(unit_at(8 + q))[:, k, h * 512:(h + 1) * 512], start=kt == 0, stop=kt == KT - 1)
                    ins.then_inc(d_ps if q == 3 else unit_used, 1)

            def experts(it, peeled):
                for k in range(UNROLL):
                    def at(u):
                        return UPE * k + u

                    def arrived(u):
                        pe.wait_ge(landed[at(u) % RING], it * (UPE * UNROLL // RING * 16) + (2 + at(u) // RING) * 16)
                    n = it * UNROLL + k
                    tile(n, k % 2, peeled and k == 0, lambda u: at(u) % RING, arrived, True, n)

            pe.wait_ge(h1_ok, NT)
            gather(0, 0)
            pe.wait_ge(bparts_ok, 1)
            experts(0, True)
            with pe.Fori(1, NE // UNROLL) as it:
                experts(it, False)
            for t in range(NT):
                scatter(NE - 1, t)
            pe.wait_ge(list_ok, 1)
            nx = pe.value_load(xcount[0:1, 0:1], min_val=0, max_val=MAXX)
            with pe.If(nx > 0):
                with pe.Fori(0, nx) as i:
                    gather(i + (NE + 1), 0)
                    uses = 1 + NE * UPE // RING
                    tile(i + NE, 0, False, lambda u: u, lambda u: pe.wait_ge(landed[u], i * 16 + (uses + 1) * 16), False, i + (NE + 1))
                    for t in range(NT):
                        scatter(i + NE, t)

        @block.vector
        def _(dve):
            link = linker(dve, dve_step)
            ts = nc.vector.tensor_scalar
            tt = nc.vector.tensor_tensor
            stt = nc.vector.scalar_tensor_tensor
            copy = nc.vector.tensor_copy

            for b in (4, 5, 6):
                nc.vector.memset(bank[b][:, 0:NCONV - 1], 0.0).then_inc(pads, 1)
            link(nc.vector.memset(sT[:, :], 1.0))
            link(nc.vector.memset(mv[:, :, :], 1.0))
            link(nc.vector.memset(dt_x[:, :, :], 0.0))
            nc.vector.memset(w_a2e[:, :], 0.0).then_inc(zeroed, 1)

            def refine_step(k, y, v, t):
                return (lambda: tt(t, y, y, ALU.mult), lambda: tt(t, t, v, ALU.mult), lambda: ts(t, t, -0.5, 1.5, ALU.mult, ALU.add),
                        lambda: tt(y, y, t, ALU.mult))[k]()

            def refine(y, v, t):
                for k in range(4):
                    link(refine_step(k, y, v, t))

            def moments(src, n, t):
                for i in range(2):
                    last = nc.vector.bn_stats(stats[0:n, i, :], src[:, i * 512:(i + 1) * 512])
                link(last)
                link(nc.vector.bn_aggr(mv[0:n, t, :], stats[0:n, :, :]))

            for t in range(NT):
                dve.wait_ge(x_in[t], 16)
                moments(xh[:, t, :], P, t)
            dve.wait_ge(meta_in, 16)
            moments(metah[:, :], META, 2)
            ts(vtmp, mv[:, :, 1], LN_EPS, None, ALU.add).then_inc(var_in, 1)
            dve.wait_ge(pcol_ps, 1)
            copy(pcol, bank[7][:, 0:72]).then_inc(pcol_ok, 1)
            dve.wait_ge(rstd_in, 1)
            dve.wait_ge(var_in, 1)
            refine(rstd, vtmp, vnew)
            for t in range(NT):
                ts(xh[:, t, :], xh[:, t, :], mv[:, t, 0:1], rstd[:, t:t + 1], ALU.subtract, ALU.mult).then_inc(xhat, 1)
            ts(metah[:, :], metah[:, :], mv[0:META, 2, 0:1], rstd[0:META, 2:3], ALU.subtract, ALU.mult).then_inc(xhat, 1)
            dve.wait_ge(pcol_ok, 1)
            for kt in range(1, KT, 2):
                dve.wait_ge(hT_ps, kt + 1)
                ts(hT[:, kt, :], bank[kt % 4][:, 0:TOK], pcol[:, kt:kt + 1], pcol[:, 8 + kt:9 + kt], ALU.mult, ALU.add).then_inc(hT_dve, 1)
            dve.wait_ge(pads, 3)
            for c in range(XC):
                dve.wait_ge(conv_ps, c + 1)
                if c >= 2:
                    dve.wait_ge(cT_ps, c - 1)
                acc, b = cacc[:, c % 2, :], bank[4 + c % 3]
                link(ts(acc, b[:, 0:TOK], pcol[:, 16 + c:17 + c], pcol[:, 48 + c:49 + c], ALU.mult, ALU.add))
                for j in range(1, NCONV):
                    ins = stt(acc, b[:, j:j + TOK], pcol[:, 16 + 8 * j + c:17 + 8 * j + c], acc, ALU.mult, ALU.add)
                    if j < NCONV - 1:
                        link(ins)
                ins.then_inc(conv, 1)
            dve.wait_ge(dtT_ps, 1)
            dve.wait_ge(small_in, 112)
            tt(dt_x[:, 0:NT, :], bank[1][:, 0:48].rearrange("p (t n) -> p t n", t=NT)[:, :, GRANK:24],
               dtb.unsqueeze(1).broadcast_to([P, NT, SHEADS]), ALU.add)
            tt(dt_x[0:META, 2, :], bank[1][0:META, 48 + GRANK:72], dtb[0:META, :], ALU.add).then_inc(dtx_ok, 1)
            dve.wait_ge(dt_e, 1)
            link(ts(dt_c, dt_a, 1.0, None, ALU.add))
            link(ts(dt_w, dt_c, -1.0, None, ALU.add))
            link(tt(dt_w, dt_a, dt_w, ALU.subtract))
            link(nc.vector.reciprocal(dt_c, dt_c))
            link(tt(dt_w, dt_w, dt_c, ALU.mult))
            link(tt(dt_b, dt_b, dt_w, ALU.add))
            link(stt(dt_x, dt_x, 0.0, dt_b, ALU.max, ALU.add))
            stt(dt_c, dt_x, -1.0, alog.unsqueeze(1).broadcast_to([P, 3, SHEADS]), ALU.mult, ALU.mult).then_inc(dt_ok, 1)
            dve.wait_ge(la_sp, 1)
            stt(la[:, :, :].rearrange("p t n -> p (t n)"), bank[2][:, :], 0.0, tmp[:, :, :].rearrange("p t n -> p (t n)"), ALU.min, ALU.subtract)
            stt(la_m, bank[0][0:META, 0:GKEY], 0.0, expD[0:META, :], ALU.min, ALU.subtract).then_inc(la_ok, 1)
            dve.wait_ge(dsum_ok, 1)
            tt(dt_w[:, 0:NT, :], dt_w[:, 0:NT, :], dt_x[:, 0:NT, :], ALU.mult)
            link(tt(dt_w[0:META, 2, :], dt_w[0:META, 2, :], dt_x[0:META, 2, :], ALU.mult))
            dve.wait_ge(y1_ok, 1)
            for t, m in ((0, P), (1, P), (2, META)):
                v = xs[0:m, t, :].rearrange("p (h q) -> p h q", h=SHEADS)
                ins = tt(v, v, dt_w[0:m, t, :].unsqueeze(2).broadcast_to([m, SHEADS, SHD]), ALU.mult)
            ins.then_inc(wx_ok, 1)
            dve.wait_ge(D_ok, 1)
            dve.wait_ge(k_ps, 1)
            tt(k_t[:, :, :].rearrange("p t n -> p (t n)"), bank[4][:, :], tmp[:, :, :].rearrange("p t n -> p (t n)"), ALU.mult)
            tt(k_m, bank[1][0:META, 256:512], expD[0:META, :], ALU.mult).then_inc(kdec, 1)
            ssd_banks = (1, 6, 4, 1, 6)

            def ssd_scan(c):
                dve.wait_ge(us_ps, c + 1)
                if c == 0:
                    copy(Ss[:, 0, :], bank[1][:, :]).then_inc(Ss_ok, 1)
                    return
                dve.wait_ge(Ss_ok, c)
                if c == NCH:
                    dve.wait_ge(y_ps, 1)
                new = Ss[:, c % 3, :]
                link(tt(new.rearrange("p (h q) -> p h q", h=SHEADS), Ss[:, (c - 1) % 3, :].rearrange("p (h q) -> p h q", h=SHEADS),
                        decs[:, c - 1, :].unsqueeze(2).broadcast_to([P, SHEADS, SHD]), ALU.mult))
                tt(new, new, bank[ssd_banks[c]][:, :], ALU.add).then_inc(Ss_ok, 1)

            for c in range(3):
                ssd_scan(c)
            dve.wait_ge(ug_ps, 1)
            copy(Sg[:, 0, :, :].rearrange("p a n -> p (a n)"), bank[7][:, 0:2 * GDV]).then_inc(Sg_ok, 1)
            for c in range(1, NCH + 1):
                dve.wait_ge(ug_ps, 2 if c % 2 else 3)
                dve.wait_ge(Sg_ok, c)
                b, at = bank[3] if c % 2 else bank[2], ((c - 1) // 2) * 256
                for i in range(2):
                    ins = stt(Sg[:, c, i, :], Sg[:, c - 1, i, :], decg[:, i * 4 + c - 1:i * 4 + c], b[:, at + i * GDV:at + (i + 1) * GDV],
                              ALU.mult, ALU.add)
                ins.then_inc(Sg_ok, 1)
            for c in (3, 4):
                ssd_scan(c)
            for t in range(NT):
                dve.wait_ge(z_sig, t + 1)
                tt(z_t[:, t, :], z_t[:, t, :], bank[(0, 5)[t]][:, :], ALU.mult).then_inc(z_ok, 1)
            for t in range(NT):
                dve.wait_ge(y_ps, 2 * t + 2)
                link(tt(y1[:, t, :], y1[:, t, :], bank[(4, 1)[t]][:, :], ALU.add))
                dve.wait_ge(z_ok, t + 1)
                tt(y1[:, t, :], y1[:, t, :], z_t[:, t, :], ALU.mult).then_inc(y_mid, 1)
            dve.wait_ge(ssq, 1)
            link(ts(rm[:, 0:4], ssy, 1.0 / 256, RMS_EPS, ALU.mult, ALU.add))
            ts(rm[:, 4:12], sso, 1.0 / GDV, RMS_EPS, ALU.mult, ALU.add).then_inc(rms_in, 1)
            dve.wait_ge(rms, 1)
            dve.wait_ge(rms_in, 1)
            refine(rr, rm, rmt)
            dve.wait_ge(normg_in, 32)
            for t in range(NT):
                for g in range(SGRP):
                    at = slice(g * 256, (g + 1) * 256)
                    ins = stt(z_t[:, t, at], y1[:, t, at], rry[:, 2 * t + g:2 * t + g + 1], normg[:, GVAL + g * 256:GVAL + (g + 1) * 256],
                              ALU.mult, ALU.mult)
                ins.then_inc(mix_y, 1)
            for t in range(NT):
                for h in range(GH):
                    ins = stt(o_n[:, t, h * GDV:(h + 1) * GDV], bank[3 - h % 2][:, t * 256 + (h // 2) * GDV:t * 256 + (h // 2 + 1) * GDV],
                              rro[:, t * 4 + h:t * 4 + h + 1], normg[:, h * GDV:(h + 1) * GDV], ALU.mult, ALU.mult)
            ins.then_inc(o_ok, 1)
            dve.wait_ge(o_ok, 1)
            for t in range(NT):
                dve.wait_ge(og_sig, t + 1)
                link(tt(og[:, t, :], og[:, t, :], bank[(6, 7)[t]][:, :], ALU.mult))
                tt(og[:, t, :], og[:, t, :], o_n[:, t, :], ALU.mult).then_inc(mix_o, 1)
            dve.wait_ge(mixT_ps, 4)
            copy(mixT[:, 2:4, :].rearrange("p a n -> p (a n)"), bank[7][:, :]).then_inc(mixT_dve, 1)
            dve.wait_ge(bias_in, 96)
            link(copy(bparts[:, :, :], braw[:, :, :]))
            for n in (2 * NE, NE):
                link(tt(braw[0:n, :, :], braw[0:n, :, :], bparts[0:n, :, :], ALU.subtract))
                ins = copy(bparts[0:n, :, :], braw[0:n, :, :])
                if n > NE:
                    link(ins)
            ins.then_inc(bparts_ok, 1)
            dve.wait_ge(h_ok, NT)
            for t in range(NT):
                for nb in range(2):
                    dve.wait_ge(wout_ps, 2 * t + nb + 1)
                    ins = stt(xh[:, t, nb * 512:(nb + 1) * 512], xh[:, t, nb * 512:(nb + 1) * 512], DN_ALPHA,
                              bank[((1, 4), (2, 3))[t][nb]][:, :], ALU.mult, ALU.add)
                    link(ins)
                moments(xh[:, t, :], P, t)
                ts(vtmp[:, t:t + 1], mv[:, t, 1:2], LN_EPS, None, ALU.add).then_inc(var1, 1)
                dve.wait_ge(rstd1, t + 1)
                dve.wait_ge(var1, t + 1)
                refine(rstd[:, t:t + 1], vtmp[:, t:t + 1], vnew[:, t:t + 1])
                ts(xh[:, t, :], xh[:, t, :], mv[:, t, 0:1], rstd[:, t:t + 1], ALU.subtract, ALU.mult).then_inc(h1_hat, 1)
            for t in range(NT):
                dve.wait_ge(h1T_ps, 2 * t + 2)
                for j in range(4):
                    kt = 4 + j
                    ins = ts(h1T[:, kt, t * P:(t + 1) * P], bank[(5, 7)[t]][:, j * P:(j + 1) * P], pcol[:, 56 + kt:57 + kt],
                             pcol[:, 64 + kt:65 + kt], ALU.mult, ALU.add)
                ins.then_inc(h1T_dve, 1)
            nc.vector.memset(gate[:, :, :], 0.0)
            nc.vector.memset(posm[:, :, :], -1.0)
            dve.wait_ge(late_in, 48)
            dve.wait_ge(logit_ps, 1)
            link(tt(logit, bank[4][:, 0:NT * NE].rearrange("p (t e) -> p t e", t=NT), rb.unsqueeze(1).broadcast_to([P, NT, NE]), ALU.add))
            for t in range(NT):
                ins = nc.vector.max(top8[:, t, :], logit[:, t, :])
            link(ins)
            ts(gmax, top8[:, :, 0], -1.0, None, ALU.mult).then_inc(top_ok, 1)
            for t in range(NT):
                ins = nc.vector.max_index(idx8[:, t, :], top8[:, t, :], logit[:, t, :])
            link(ins)
            link(copy(idxf, idx8[:, :, 0:4]))
            dve.wait_ge(iota_ok, 2)
            oh4 = onehot[:, :, :, :].rearrange("p t k e -> p (t k) e")
            gh4 = ghot[:, :, :, :].rearrange("p t k e -> p (t k) e")
            link(tt(oh4, iota[:, 0, 0:NE].unsqueeze(1).broadcast_to([P, NT * 4, NE]),
                    idxf[:, :, :].rearrange("p t k -> p (t k)").unsqueeze(2).broadcast_to([P, NT * 4, NE]), ALU.is_equal))
            nc.vector.tensor_reduce(mask, onehot[:, :, :, :].rearrange("p t k e -> p t e k"), AX_X, ALU.add).then_inc(mask_ok, 1)
            dve.wait_ge(gexp, 1)
            link(nc.vector.tensor_reduce(gsum, gate4[:, :, 0:4], AX_X, ALU.add))
            link(nc.vector.reciprocal(gsum, gsum))
            link(tt(gate4[:, :, 4:8], gate4[:, :, 0:4], gsum.unsqueeze(2).broadcast_to([P, NT, 4]), ALU.mult))
            for t in range(NT):
                ins = tt(ghot[:, t, :, :], onehot[:, t, :, :], gate4[:, t, 4:8].unsqueeze(2).broadcast_to([P, 4, NE]), ALU.mult)
            link(ins)
            nc.vector.tensor_reduce(gate[:, :, 0:NE], ghot[:, :, :, :].rearrange("p t k e -> p t e k"), AX_X, ALU.add).then_inc(mask_ok, 1)
            dve.wait_ge(pos_ps, 1)
            link(stt(posm[:, :, 0:NE], bank[5][:, 0:NT * NE].rearrange("p (t e) -> p t e", t=NT), 1.0, mask, ALU.add, ALU.mult))
            link(ts(posm[:, :, 0:NE], posm[:, :, 0:NE], -1.0, None, ALU.add))
            dve.wait_ge(mask_ok, 2)

            def select(n, e, par, j=0):
                if not isinstance(n, int) or n >= 2:
                    dve.wait_ge(gath_ps, n - 1)
                    dve.wait_ge(u_ps, n - 1)
                    dve.wait_ge(selT_ps, n - 1)
                at = (slice(e, e + 1) if isinstance(e, int) else bass.ds(e, 1))
                jj = j if isinstance(j, int) else bass.ds(j, 1)
                slots = iota[:, jj, :] if isinstance(j, int) else iota[:, jj, :].rearrange("p a s -> p (a s)")
                for t in range(NT):
                    ts(sel[:, par, t, :], slots[:, 0:SL], posm[:, t, at], None, ALU.is_equal)
                    ts(selG[:, par, t, :], slots, posm[:, t, at], gate[:, t, at], ALU.is_equal, ALU.mult)
                ts(oh[:, par, :], ones[0:96, 0:SL], eid[0:96, at], None, ALU.mult).then_inc(sel_ok, 1)

            select(0, 0, 0)
            for j in range(1, NJ):
                ins = ts(flag[:, j - 1, :], bank[5][0:1, 2 * NE:3 * NE], float(SL * j), None, ALU.is_gt)
            link(ins)
            flagf = flag[:, :, :].rearrange("p j e -> p (j e)")
            link(nc.vector.tensor_tensor_scan(rank, flagf, ones[0:1, 0:3 * NE], 0.0, ALU.add, ALU.mult))
            copy(xcount, rank[:, 3 * NE - 1:3 * NE]).then_inc(list_ok, 1)

            def tile(n, par, first, after):
                if after is not None:
                    select(n + 1, after, 1 - par)
                dve.wait_ge(g_ps, n + 1)
                ts(a_c, bank[4][:, :], LIMIT, None, ALU.min).then_inc(a_ok, 1)
                dve.wait_ge(u_ps, n + 1)
                if not first:
                    dve.wait_ge(hidT_ps, n)
                ts(u_c, bank[5][:, :], LIMIT, -LIMIT, ALU.min, ALU.max).then_inc(u_ok, 1)
                dve.wait_ge(sig_ok, n + 1)
                tt(a_c, a_c, s_c, ALU.mult).then_inc(as_ok, 1)
                dve.wait_ge(u_ok, n + 1)
                dve.wait_ge(as_ok, n + 1)
                stt(u_c, u_c, 1.0, a_c, ALU.add, ALU.mult).then_inc(hid_ok, 1)
                dve.wait_ge(d_ps, n + 1)
                if not first:
                    dve.wait_ge(scat[1], n)
                copy(y_s, bank[6][:, :]).then_inc(yd_ok, 1)

            for k in range(UNROLL):
                tile(k, k % 2, k == 0, k + 1)
            with dve.Fori(1, NE // UNROLL) as it:
                for k in range(UNROLL):
                    tile(it * UNROLL + k, k % 2, False, it * UNROLL + (k + 1))
            nx = dve.value_load(xcount[0:1, 0:1], min_val=0, max_val=MAXX)
            with dve.If(nx > 0):
                dve.wait_ge(scat[1], NE)
                link_x = [0]

                def lx(ins):
                    link_x[0] += 1
                    ins.then_inc(xstep, 1)
                    dve.wait_ge(xstep, link_x[0])
                for j in range(1, NJ):
                    ts(flag_j[:, j - 1, :], flag[:, j - 1, :], float(j), None, ALU.mult)
                lx(tt(flag_e[:, :, :], flag[:, :, :], iota[0:1, 0, 0:NE].unsqueeze(1).broadcast_to([1, 3, NE]), ALU.mult))
                for i in range(MAXX):
                    for src, dst in ((flag_e, xlf[:, 0, :]), (flag_j, xlf[:, 1, :])):
                        lx(stt(xscr, rank, float(i + 1), src[:, :, :].rearrange("p j e -> p (j e)"), ALU.is_equal, ALU.mult,
                               accum_out=dst[:, i:i + 1]))
                copy(xlist2[:, :, :], xlf[:, :, :]).then_inc(list_ok, 1)
                dve.wait_ge(list_ok, 2)
                with dve.Fori(0, nx) as i:
                    e = dve.value_load(xlist[0:1, bass.ds(i, 1)], min_val=0, max_val=NE - 1)
                    j = dve.value_load(xlist2[0:1, 1, bass.ds(i, 1)], min_val=1, max_val=NJ - 1)
                    select(i + (NE + 1), e, 0, j)
                    tile(i + NE, 0, False, None)
            dve.wait_ge(ln2_in, 32)
            for t in range(NT):
                dve.wait_ge(scat[t], nx + NE)
                for h in range(2):
                    at = slice(h * 512, (h + 1) * 512)
                    ins = stt(z2[:, t, at], xh[:, t, at], DN_ALPHA, bank[2 * t + h][:, :], ALU.mult, ALU.add)
                link(ins)
                moments(z2[:, t, :], P, t)
                ts(vtmp[:, t:t + 1], mv[:, t, 1:2], LN_EPS, None, ALU.add).then_inc(z2_ok, 1)
                ins = stt(z2[:, t, :], z2[:, t, :], mv[:, t, 0:1], lnbc[:, 0, :], ALU.subtract, ALU.mult)
                link(ins)
                dve.wait_ge(rstd2, t + 1)
                dve.wait_ge(z2_ok, t + 1)
                for k in range(3):
                    link(refine_step(k, rstd[:, t:t + 1], vtmp[:, t:t + 1], vnew[:, t:t + 1]))
                refine_step(3, rstd[:, t:t + 1], vtmp[:, t:t + 1], vnew[:, t:t + 1]).then_inc(rstd_ok, 1)
            dve.wait_ge(rstd_ok, NT)
            for h in range(2):
                at = slice(h * 512, (h + 1) * 512)
                stt(z2[:, 1, at], z2[:, 1, at], rstd[:, 1:2], lnbc[:, 1, at], ALU.mult, ALU.add).then_inc(fin1, 1)


_INS = ["x", "meta_tokens", "ln_in_g", "ln_in_b", "w_in", "gla_w_a2", "gla_b_a", "gla_norm_g", "ssd_conv_w", "ssd_conv_b",
        "ssd_dt_bias", "ssd_a_log", "ssd_d", "ssd_norm_g", "w_out", "ln1_g", "ln1_b", "router_w", "router_b",
        "moe_w_gate", "moe_w_up", "moe_b_gate", "moe_b_up", "moe_w_down", "moe_b_down", "ln2_g", "ln2_b"]


def kernel(**inputs):
    import numpy as np
    import concourse.bacc as bacc
    from concourse.bass_utils import run_bass_kernel_spmd

    nc = bacc.Bacc("TRN2", target_bir_lowering=False, num_devices=1)
    arrays, args = {}, []
    for name in _INS:
        a = np.ascontiguousarray(inputs[name])
        arrays[f"in_{name}"] = a
        args.append(nc.dram_tensor(f"in_{name}", a.shape, mybir.dt.from_np(a.dtype), kind="ExternalInput").ap())
    args.append(nc.dram_tensor("out_h", (1, SEQ, D), F32, kind="ExternalOutput").ap())
    build(nc, *args)
    return run_bass_kernel_spmd(nc, [arrays], core_ids=[0]).results[0]["out_h"]
```

```python
import concourse.bass as bass
from concourse import mybir
from contextlib import ExitStack

F32 = mybir.dt.float32
BF16 = mybir.dt.bfloat16
I32 = mybir.dt.int32
U32 = mybir.dt.uint32
ALU = mybir.AluOpType
ACT = mybir.ActivationFunctionType
AX_X = mybir.AxisListType.X

P = 128
D = 1024
KT = D // P
SEQ = 256
NT = SEQ // P
META = 16
TOK = META + SEQ
CHUNK = 64
NCH = SEQ // CHUNK
GKEY, GVAL, GH, GDK, GDV, GRANK = 256, 512, 4, 64, 128, 16
TAU = 16.0
SIN, SHD, SHEADS, SGRP, SST, NCONV = 512, 64, 8, 2, 128, 4
XBC = SIN + 2 * SGRP * SST
XC = XBC // P
NE, FF = 32, 1024
LIMIT, SALPHA = 7.0, 1.702
DN_ALPHA = 2.0 ** 0.25
LN_EPS, RMS_EPS = 1e-5, 1e-6

C_Q, C_K, C_V, C_OG, C_A1, C_Z = 0, 256, 512, 1024, 1536, 1552
C_XBC, C_DT = C_Z + SIN, C_Z + SIN + XBC

MH = (slice(0, META), slice(64, 64 + META))
MH1 = 64 + META
SR = 64 + GRANK + SHEADS
HK, HV = GKEY // 2, GVAL // 2

RING = 16
UW = 2048
UPE = 3 * D * FF // (P * UW)
UNROLL = 4
ROUNDS = NE // UNROLL
SPARE = 4
SL = 64
NJ = SEQ // SL
MAXX = NT * P * 4 // SL

W_ORDER = [C_XBC + 256 * i for i in range(4)] + [C_K, C_V, C_V + 256, C_Q, C_Z, C_Z + 256, C_OG, C_OG + 256]
U_XBC, U_K, U_V, U_Q, U_Z, U_OG, U_OUT = 0, 4, 5, 7, 8, 10, 12


def build(nc, x, meta, ln_in_g, ln_in_b, w_in, gla_w_a2, gla_b_a, gla_norm_g, ssd_conv_w, ssd_conv_b,
          ssd_dt_bias, ssd_a_log, ssd_d, ssd_norm_g, w_out, ln1_g, ln1_b, router_w, router_b,
          w_gate, w_up, b_gate, b_up, w_down, b_down, ln2_g, ln2_b, out):
    with ExitStack() as ctx:
        def sb(name, shape, dt=F32):
            return ctx.enter_context(nc.sbuf_tensor(name, shape, dt))

        def sem(name):
            return ctx.enter_context(nc.semaphore(name))

        ring = sb("ring", [P, RING, UW])
        arena = sb("arena", [P, 19392])
        bank = [ctx.enter_context(nc.psum_tensor(f"bank{i}", [P, 512], F32)) for i in range(8)]

        def cut(at, *shape, parts=P, dt=F32):
            n = 1
            for s in shape:
                n *= s
            words = n if dt in (F32, I32, U32) else n // 2
            v = arena[0:parts, at:at + words]
            if dt is not F32:
                v = v.bitcast(dt)
            if len(shape) == 2:
                v = v.rearrange("p (a b) -> p a b", a=shape[0])
            if len(shape) == 3:
                v = v.rearrange("p (a b c) -> p a b c", a=shape[0], b=shape[1])
            return v

        xh = cut(0, NT, D)
        metah = cut(2048, D, parts=META)
        k_m = cut(2048, GKEY // 2, parts=MH1)
        v_m = cut(2176, GVAL // 2, parts=MH1)
        la_m = cut(2432, GKEY // 2, parts=MH1)
        hT = cut(3072, KT, TOK)
        mixT = cut(3072, KT, SEQ)
        h1T = cut(3072, KT, SEQ)
        lnbc = cut(5248, 2, D)
        normg = cut(7296, D)
        v_t = cut(8320, NT, GVAL)
        og = cut(8320, NT, GVAL)
        k_t = cut(9344, NT, GKEY)
        tmp = cut(9856, NT, GKEY)
        z_t = cut(9344, NT, SIN)
        o_n = cut(10368, NT, GVAL)
        la = cut(10368, NT, GKEY)
        expD = cut(10880, GKEY // 2, parts=MH1)
        qT = cut(11136, 2, SEQ)
        cacc = cut(11648, 2, TOK)
        csig = cut(12192, 2, TOK)
        CT = cut(12736, SGRP, SEQ)
        xs = cut(13248, 3, SIN)
        y1 = cut(14784, NT, SIN)
        Bt = cut(15808, 3, SGRP * SST)
        Sg = cut(16576, NCH + 1, 2, GDV)
        prow = cut(16576, P, parts=72)
        w_a2e = cut(16704, GKEY, parts=SR)
        w_small = cut(16960, KT, 24)
        Ss = cut(17856, 3, SIN)
        sT = cut(17856, TOK, parts=SR)
        b_dn = cut(11648, D, parts=NE)
        rw = cut(12672, KT, NE)
        rb = cut(12928, NE)
        eid = cut(13184, NE)
        bparts = cut(13248, 2, FF, parts=96, dt=BF16)
        braw = cut(16576, 2, FF, parts=96)
        spare = [cut(at, 2, D) for at in (8320, 16576, 3072, 5248)]
        xT = [cut(at, KT, SL) for at in (2048, 12672)]
        a_c = cut(14272, 512)
        s_c = cut(15808, 512)
        u_c = cut(11136, 512)
        hidT = cut(10368, 4, P)
        y_s = cut(14784, 512)
        GT = cut(15296, SEQ, parts=NE)
        selG = cut(7296, 2, NT, P)
        sel = cut(7808, 2, NT, SL)
        selGT = cut(10880, SEQ)
        oh = cut(15552, 2, SL, parts=96, dt=BF16)
        iota = cut(18624, NJ, P)
        tri_s = cut(12960, P)
        z2 = cut(11648, NT, D)
        logit = cut(2048, NT, NE)
        top8 = cut(2112, NT, 8)
        idx8 = cut(2128, NT, 8, dt=U32)
        idxf = cut(2144, NT, 4)
        onehot = cut(2160, NT, 4, NE)
        ghot = cut(2416, NT, 4, NE)
        mask = cut(2672, NT, NE)
        gate = cut(2736, NT, NE)
        posm = cut(2802, NT, NE)
        gate4 = cut(2868, NT, 8)
        flag = cut(8064, 3, NE, parts=1)
        rank = cut(8160, 3 * NE, parts=1)
        xcount = cut(8256, 1, parts=1, dt=I32)
        xlist2 = cut(8260, 2, MAXX, parts=1, dt=I32)
        xlist = xlist2[:, 0, :]
        flag_e = cut(9344, 3, NE, parts=1)
        flag_j = cut(9440, 3, NE, parts=1)
        xlf = cut(9536, 2, MAXX, parts=1)
        xscr = cut(9568, 3 * NE, parts=1)

        small = sb("small", [P, 336])
        o = [0]

        def sm(*shape):
            n = 1
            for s in shape:
                n *= s
            v = small[:, o[0]:o[0] + n]
            o[0] += n
            if len(shape) == 2:
                v = v.rearrange("p (a b) -> p a b", a=shape[0])
            return v

        stats = sm(2, 6)
        mv = sm(3, 2)
        rstd = sm(3)
        vtmp = sm(3)
        pcol = sm(72)
        dtb = sm(SHEADS)
        alog = sm(SHEADS)
        dskip = sm(SHEADS)
        dt_x = sm(3, SHEADS)
        dt_a = sm(3, SHEADS)
        dt_b = sm(3, SHEADS)
        dt_c = sm(3, SHEADS)
        dt_w = sm(3, SHEADS)
        decs = sm(NCH, SHEADS)
        decg = sm(8)
        ssy, sso = sm(4), sm(8)
        rm, rr, rmt = sm(12), sm(12), sm(12)
        rry, rro = rr[:, 0:4], rr[:, 4:12]
        vnew = sm(3)
        gmax = sm(NT)
        gsum = sm(NT)
        ident = sb("ident", [P, P])
        tri = sb("tri", [P, P])
        residual = tri
        ones = sb("ones", [P, P])
        x_in = [sem(f"x_in{t}") for t in range(NT)]
        meta_in, params_in, small_in, lnin_in, normg_in = sem("meta_in"), sem("params_in"), sem("small_in"), sem("lnin_in"), sem("normg_in")
        ln1_in, ln2_in, bias_in, late_in, out_done = sem("ln1_in"), sem("ln2_in"), sem("bias_in"), sem("late_in"), sem("out_done")
        landed = [sem(f"landed{s}") for s in range(RING)]
        spare_in = sem("spare_in")
        unit_used = sem("unit_used")
        half_used = sem("half_used")
        consts, zeroed, pads = sem("consts"), sem("zeroed"), sem("pads")
        pe_step, dve_step, act_step, pool_step, xstep = sem("pe_step"), sem("dve_step"), sem("act_step"), sem("pool_step"), sem("xstep")
        var_in, rstd_in, xhat = sem("var_in"), sem("rstd_in"), sem("xhat")
        pcol_ps, pcol_ok, hT_ps, hT_act, hT_dve, h_ok = sem("pcol_ps"), sem("pcol_ok"), sem("hT_ps"), sem("hT_act"), sem("hT_dve"), sem("h_ok")
        conv_ps, conv, csig_ok, silu, cT_ps, cT_ok = sem("conv_ps"), sem("conv"), sem("csig_ok"), sem("silu"), sem("cT_ps"), sem("cT_ok")
        sT_ps, sT_ok, dtT_ps, dtx_ok, dt_e, dt_ok = sem("sT_ps"), sem("sT_ok"), sem("dtT_ps"), sem("dtx_ok"), sem("dt_e"), sem("dt_ok")
        dsum_ps, dsum_ok, wx_ok, y1_ok = sem("dsum_ps"), sem("dsum_ok"), sem("wx_ok"), sem("y1_ok")
        la_ps, la_sp, la_ok, D_ps, D_ok, kdec = sem("la_ps"), sem("la_sp"), sem("la_ok"), sem("D_ps"), sem("D_ok"), sem("kdec")
        k_ps, v_ps, v_ok, q_ps, q_ok = sem("k_ps"), sem("v_ps"), sem("v_ok"), sem("q_ps"), sem("q_ok")
        us_ps, Ss_ok, ug_ps, Sg_ok, y_ps, o_ps = sem("us_ps"), sem("Ss_ok"), sem("ug_ps"), sem("Sg_ok"), sem("y_ps"), sem("o_ps")
        z_ps, z_sig, z_ok, og_ps, og_sig = sem("z_ps"), sem("z_sig"), sem("z_ok"), sem("og_ps"), sem("og_sig")
        y_mid, ssq, rms_in, rms, mix_y, o_ok, mix_o = sem("y_mid"), sem("ssq"), sem("rms_in"), sem("rms"), sem("mix_y"), sem("o_ok"), sem("mix_o")
        mixT_ps, mixT_act, mixT_dve, wout_ps = sem("mixT_ps"), sem("mixT_act"), sem("mixT_dve"), sem("wout_ps")
        var1, rstd1, h1_hat, h1_ok, h1T_ps, h1T_act, h1T_dve, logit_ps = (sem("var1"), sem("rstd1"), sem("h1_hat"), sem("h1_ok"), sem("h1T_ps"),
                                                                          sem("h1T_act"), sem("h1T_dve"), sem("logit_ps"))
        top_ok, gexp, mask_ok, pos_ps, GT_ps, GT_ok = sem("top_ok"), sem("gexp"), sem("mask_ok"), sem("pos_ps"), sem("GT_ps"), sem("GT_ok")
        iota_ok, residual_ok, bparts_ok, list_ok = sem("iota_ok"), sem("residual_ok"), sem("bparts_ok"), sem("list_ok")
        sel_ok, selG_ok, gath_ps, xT_ok, selT_ps, selGT_ok = sem("sel_ok"), sem("selG_ok"), sem("gath_ps"), sem("xT_ok"), sem("selT_ps"), sem("selGT_ok")
        g_ps, u_ps, a_ok, sig_ok, u_ok, as_ok, hid_ok = sem("g_ps"), sem("u_ps"), sem("a_ok"), sem("sig_ok"), sem("u_ok"), sem("as_ok"), sem("hid_ok")
        hidT_ps, hidT_ok, d_ps, yd_ok = sem("hidT_ps"), sem("hidT_ok"), sem("d_ps"), sem("yd_ok")
        scat = [sem(f"scat{t}") for t in range(NT)]
        var2, rstd2, fin = sem("var2"), sem("rstd2"), sem("fin")

        def linker(eng, s):
            n = [0]

            def link(ins):
                n[0] += 1
                ins.then_inc(s, 1)
                eng.wait_ge(s, n[0])
            return link

        def unit_src(e, u):
            m = (w_gate, w_up, w_down)[u // (UPE // 3)]
            q = u % (UPE // 3)
            return m[0, e].rearrange("(k p) n -> p k n", p=P)[:, 2 * q:2 * q + 2, :] if isinstance(e, int) else \
                m[0, bass.ds(e, 1)].rearrange("a (k p) n -> p (a k) n", p=P)[:, 2 * q:2 * q + 2, :]

        def slot(s):
            return ring[:, s, :].rearrange("p (k n) -> p k n", k=2)

        def ring_at(it, i):
            if isinstance(it, int) and it == ROUNDS - 1:
                return None if i < SPARE else i - SPARE
            return i

        block = ctx.enter_context(nc.Block())

        @block.sync
        def _(sp):
            for t in range(NT):
                sp.dma_start(xh[:, t, :], x[0, t * P:(t + 1) * P, :]).then_inc(x_in[t], 16)
            sp.dma_start(prow[0:8, :], ln_in_g.rearrange("(c p) -> c p", p=P)).then_inc(params_in, 16)
            sp.dma_start(prow[8:16, :], ln_in_b.rearrange("(c p) -> c p", p=P)).then_inc(params_in, 16)
            sp.dma_start(prow[16:48, :], ssd_conv_w[0].rearrange("j (c p) -> (j c) p", p=P)).then_inc(params_in, 16)
            sp.dma_start(prow[48:56, :], ssd_conv_b[0].rearrange("(c p) -> c p", p=P)).then_inc(params_in, 16)
            sp.dma_start(prow[56:64, :], ln1_g[0].rearrange("(c p) -> c p", p=P)).then_inc(params_in, 16)
            sp.dma_start(prow[64:72, :], ln1_b[0].rearrange("(c p) -> c p", p=P)).then_inc(params_in, 16)
            for n, c0 in enumerate(W_ORDER):
                sp.dma_start(ring[:, n, :].rearrange("p (k n) -> p k n", k=KT),
                             w_in[0, :, c0:c0 + 256].rearrange("(k p) n -> p k n", p=P)).then_inc(landed[n], 16)
                if n == 3:
                    sp.dma_start(w_small[:, :, 0:GRANK], w_in[0, :, C_A1:C_A1 + GRANK].rearrange("(k p) n -> p k n", p=P)).then_inc(small_in, 16)
                    sp.dma_start(w_small[:, :, GRANK:24], w_in[0, :, C_DT:C_DT + SHEADS].rearrange("(k p) n -> p k n", p=P)).then_inc(small_in, 16)
                    sp.wait_ge(zeroed, 1)
                    sp.dma_start(w_a2e[0:GRANK, :], gla_w_a2[0]).then_inc(small_in, 16)
                    sp.dma_start(w_a2e[64:64 + GRANK, :], gla_w_a2[0]).then_inc(small_in, 16)
                    sp.dma_start(w_a2e[24:25, :], gla_b_a).then_inc(small_in, 16)
                    sp.dma_start(dtb, ssd_dt_bias.broadcast_to([P, SHEADS])).then_inc(small_in, 16)
                    sp.dma_start(alog, ssd_a_log.broadcast_to([P, SHEADS])).then_inc(small_in, 16)
                    sp.dma_start(dskip, ssd_d.broadcast_to([P, SHEADS])).then_inc(small_in, 16)
            sp.dma_start(lnbc[:, 0, :], ln_in_g.rearrange("(a n) -> a n", a=1).broadcast_to([P, D])).then_inc(lnin_in, 16)
            sp.dma_start(lnbc[:, 1, :], ln_in_b.rearrange("(a n) -> a n", a=1).broadcast_to([P, D])).then_inc(lnin_in, 16)
            sp.dma_start(normg[:, 0:GVAL], gla_norm_g.broadcast_to([P, GVAL])).then_inc(normg_in, 16)
            sp.dma_start(normg[:, GVAL:D], ssd_norm_g.broadcast_to([P, SIN])).then_inc(normg_in, 16)
            for n in range(4):
                sp.dma_start(ring[:, U_OUT + n, :].rearrange("p (k n) -> p k n", k=KT),
                             w_out[0, :, 256 * n:256 * n + 256].rearrange("(k p) n -> p k n", p=P)).then_inc(landed[U_OUT + n], 16)

            w_used = [(conv_ps, 2), (conv_ps, 4), (conv_ps, 6), (conv_ps, 8), (k_ps, 1), (v_ps, 3), (v_ps, 3), (q_ps, 1),
                      (half_used, 1), (z_ps, 2), (half_used, 2), (og_ps, 2), (wout_ps, 3), (wout_ps, 3), (wout_ps, 4), (wout_ps, 4)]

            def load_spare(q):
                sp.dma_start(spare[q], unit_src(NE - UNROLL, q)).then_inc(spare_in, 16)

            def experts(it):
                first = isinstance(it, int) and it == 0
                for i in range(UPE * UNROLL):
                    at = ring_at(it, i)
                    if at is None:
                        continue
                    before = at - RING
                    if before >= 0:
                        before += i - at
                    if first and i == U_OUT:
                        sp.wait_ge(mixT_ps, 4)
                        load_spare(0)
                        sp.wait_ge(bparts_ok, 1)
                        load_spare(1)
                    if first and before < 0:
                        sp.wait_ge(*w_used[i])
                    else:
                        k, u = before // UPE, before % UPE
                        m, q = u // 4, u % 4
                        if q == 3:
                            sp.wait_ge((g_ps, u_ps, d_ps)[m], it * UNROLL + (k + 1))
                        else:
                            sp.wait_ge(unit_used, (it * UNROLL + k) * 9 + (3 * m + q + 1))
                    sp.dma_start(slot(at % RING), unit_src(it * UNROLL + i // UPE, i % UPE)).then_inc(landed[at % RING], 16)
                    if first and i == RING - 1:
                        sp.wait_ge(logit_ps, 1)
                        load_spare(2)
                        sp.wait_ge(h1_ok, NT)
                        load_spare(3)
            experts(0)
            with sp.Fori(1, ROUNDS - 1) as it:
                experts(it)
            experts(ROUNDS - 1)
            sp.wait_ge(g_ps, NE - UNROLL + 1)
            sp.dma_start(lnbc[:, 0, :], ln2_g.broadcast_to([P, D])).then_inc(ln2_in, 16)
            sp.dma_start(lnbc[:, 1, :], ln2_b.broadcast_to([P, D])).then_inc(ln2_in, 16)
            sp.wait_ge(list_ok, 1)
            nx = sp.value_load(xcount[0:1, 0:1], min_val=0, max_val=MAXX)
            with sp.If(nx > 0):
                sp.wait_ge(list_ok, 2)
                with sp.Fori(0, nx) as i:
                    sp.wait_ge(d_ps, i + NE)
                    e = sp.value_load(xlist[0:1, bass.ds(i, 1)], min_val=0, max_val=NE - 1)
                    for u in range(UPE):
                        sp.dma_start(slot(u), unit_src(e, u)).then_inc(landed[u], 16)
            for t in range(NT):
                sp.wait_ge(fin, 2 * t + 1)
                sp.dma_start(out[0, t * P:(t + 1) * P, 0:512], z2[:, t, 0:512]).then_inc(out_done, 16)

        @block.gpsimd
        def _(pool):
            link = linker(pool, pool_step)
            link(nc.gpsimd.memset(ident[:, :], 0.0))
            nc.gpsimd.affine_select(out=ident[:, :], in_=ident[:, :], compare_op=ALU.not_equal, fill=1.0,
                                    base=0, pattern=[[-1, P]], channel_multiplier=1).then_inc(consts, 1)
            nc.gpsimd.memset(ones[:, :], 1.0).then_inc(consts, 1)
            link(nc.gpsimd.memset(tri[:, :], 1.0 / TAU))
            link(nc.gpsimd.affine_select(out=tri[:, :], in_=tri[:, :], compare_op=ALU.is_gt, fill=0.0,
                                         base=0, pattern=[[-1, P]], channel_multiplier=1))
            nc.gpsimd.memset(tri[CHUNK:P, 0:CHUNK], 0.0).then_inc(consts, 1)
            for c in range(XC):
                pool.wait_ge(csig_ok, c + 1)
                if c < 6:
                    dst, at = cacc[:, c % 2, :], slice(0, TOK)
                else:
                    dst, at = CT[:, c - 6, :], slice(META, TOK)
                nc.gpsimd.tensor_tensor(dst, cacc[:, c % 2, at], csig[:, c % 2, at], ALU.mult).then_inc(silu, 1)
            pool.wait_ge(small_in, 128)
            pool.wait_ge(cT_ok, 4)
            for t in range(NT):
                ins = nc.gpsimd.tensor_tensor(y1[:, t, :].rearrange("p (h q) -> p h q", h=SHEADS),
                                              xs[:, t, :].rearrange("p (h q) -> p h q", h=SHEADS),
                                              dskip.unsqueeze(2).broadcast_to([P, SHEADS, SHD]), ALU.mult)
            ins.then_inc(y1_ok, 1)
            pool.wait_ge(lnin_in, 32)
            pool.wait_ge(hT_ps, KT)
            for t in range(NT):
                link(nc.gpsimd.tensor_tensor(xh[:, t, :], xh[:, t, :], lnbc[:, 0, :], ALU.mult))
                ins = nc.gpsimd.tensor_tensor(xh[:, t, :], xh[:, t, :], lnbc[:, 1, :], ALU.add)
                ins.then_inc(h_ok, 1)
            pool.wait_ge(y_ps, NCH)
            pool.wait_ge(o_ps, 2)
            nc.gpsimd.iota(iota[:, :, :].rearrange("p j (h s) -> p j h s", h=2), [[SL, NJ], [0, 2], [1, SL]], base=0,
                           channel_multiplier=0, allow_small_or_imprecise_dtypes=True).then_inc(iota_ok, 1)
            link(nc.gpsimd.memset(eid, 0.0))
            for q in range(3):
                v = eid[NE * q:NE * (q + 1), 0:NE]
                link(nc.gpsimd.affine_select(out=v, in_=v, compare_op=ALU.not_equal, fill=1.0, base=0, pattern=[[-1, NE]],
                                             channel_multiplier=1))
            link(nc.gpsimd.memset(tri_s[:, :], 1.0))
            nc.gpsimd.affine_select(out=tri_s[:, :], in_=tri_s[:, :], compare_op=ALU.is_gt, fill=0.0, base=0, pattern=[[1, P]],
                                    channel_multiplier=-1).then_inc(iota_ok, 1)
            pool.wait_ge(D_ps, 1)
            link(nc.gpsimd.memset(residual[:, :], 0.0))
            nc.gpsimd.affine_select(out=residual[:, :], in_=residual[:, :], compare_op=ALU.not_equal, fill=DN_ALPHA,
                                    base=0, pattern=[[-1, P]], channel_multiplier=1).then_inc(residual_ok, 1)
            pool.wait_ge(ln1_in, 32)
            for t in range(NT):
                pool.wait_ge(h1T_ps, 2 * t + 2)
                link(nc.gpsimd.tensor_tensor(xh[:, t, :], xh[:, t, :], lnbc[:, 0, :], ALU.mult))
                nc.gpsimd.tensor_tensor(xh[:, t, :], xh[:, t, :], lnbc[:, 1, :], ALU.add).then_inc(h1_ok, 1)

        @block.scalar
        def _(act):
            link = linker(act, act_step)
            act.dma_start(metah[:, :], meta).then_inc(meta_in, 16)

            def inv_sqrt(src, dst, wait_for, n, done):
                act.wait_ge(wait_for, n)
                link(nc.scalar.activation(dst, src, ACT.Ln))
                nc.scalar.activation(dst, dst, ACT.Exp, scale=-0.5).then_inc(done, 1)

            def mixT_evac(b, kt):
                nc.scalar.activation(mixT[:, kt:kt + 2, :].rearrange("p a n -> p (a n)"), b[:, :], ACT.Copy).then_inc(mixT_act, 1)

            inv_sqrt(vtmp, rstd, var_in, 1, rstd_in)
            act.wait_ge(pcol_ok, 1)
            for kt in range(0, KT, 2):
                act.wait_ge(hT_ps, kt + 1)
                nc.scalar.activation(hT[:, kt, :], bank[kt % 4][:, 0:TOK], ACT.Identity, bias=pcol[:, 8 + kt:9 + kt],
                                     scale=pcol[:, kt:kt + 1]).then_inc(hT_act, 1)

            def c_evac(c):
                act.wait_ge(cT_ps, c + 1)
                b = bank[7] if c % 2 == 0 else bank[3]
                dst, at = (xs, c * P) if c < 4 else (Bt, (c - 4) * P)
                nc.scalar.activation(dst[:, 0:NT, at:at + P], b[:, 0:2 * P].rearrange("p (t n) -> p t n", t=NT), ACT.Copy)
                nc.scalar.activation(dst[0:META, 2, at:at + P], b[0:META, 2 * P:3 * P], ACT.Copy).then_inc(cT_ok, 1)

            for c in range(XC):
                act.wait_ge(conv, c + 1)
                if c >= 2:
                    act.wait_ge(silu, c - 1)
                nc.scalar.activation(csig[:, c % 2, :], cacc[:, c % 2, :], ACT.Sigmoid).then_inc(csig_ok, 1)
                if c >= 2:
                    c_evac(c - 2)
            act.wait_ge(sT_ps, 1)
            nc.scalar.activation(sT[0:24, :], bank[0][0:24, 0:TOK], ACT.Copy)
            nc.scalar.activation(sT[64:SR, :], bank[0][64:SR, 0:TOK], ACT.Copy).then_inc(sT_ok, 1)
            act.wait_ge(dtx_ok, 1)
            act.wait_ge(small_in, 128)
            flat = lambda v: v.rearrange("p a b -> p (a b)")
            link(nc.scalar.activation(alog, alog, ACT.Exp))
            link(nc.scalar.activation(flat(dt_a), flat(dt_x), ACT.Abs))
            link(nc.scalar.activation(flat(dt_a), flat(dt_a), ACT.Exp, scale=-1.0))
            nc.scalar.activation(flat(dt_b), flat(dt_a), ACT.Ln, bias=1.0).then_inc(dt_e, 1)
            act.wait_ge(la_ps, 1)
            tmpf = tmp[:, :, :].rearrange("p t n -> p (t n)")
            link(nc.scalar.activation(tmpf, bank[2][:, :], ACT.Abs))
            for m in MH:
                link(nc.scalar.activation(expD[m, :], bank[0][m, 0:HK], ACT.Abs))
            link(nc.scalar.activation(tmpf, tmpf, ACT.Exp, scale=-1.0))
            for m in MH:
                link(nc.scalar.activation(expD[m, :], expD[m, :], ACT.Exp, scale=-1.0))
            link(nc.scalar.activation(tmpf, tmpf, ACT.Ln, bias=1.0))
            for m in MH:
                ins = nc.scalar.activation(expD[m, :], expD[m, :], ACT.Ln, bias=1.0)
            ins.then_inc(la_sp, 1)
            act.wait_ge(dsum_ps, 1)
            nc.scalar.activation(flat(dt_w[:, 0:NT, :]), bank[6][:, 0:16], ACT.Exp, scale=TAU)
            nc.scalar.activation(dt_w[0:META, 2, :], bank[6][0:META, 16:24], ACT.Exp, scale=TAU)
            nc.scalar.activation(flat(decs), bank[6][:, 32:64], ACT.Exp).then_inc(dsum_ok, 1)
            act.wait_ge(D_ps, 1)
            nc.scalar.activation(tmpf, bank[2][:, :], ACT.Exp)
            for m in MH:
                nc.scalar.activation(expD[m, :], bank[0][m, 0:HK], ACT.Exp)
            nc.scalar.activation(decg, bank[0][:, GKEY:GKEY + 8], ACT.Exp, scale=1.0 / TAU).then_inc(D_ok, 1)
            act.wait_ge(h_ok, NT)
            act.dma_start(lnbc[:, 0, :], ln1_g.broadcast_to([P, D])).then_inc(ln1_in, 16)
            act.dma_start(lnbc[:, 1, :], ln1_b.broadcast_to([P, D])).then_inc(ln1_in, 16)
            for t in range(NT):
                act.wait_ge(v_ps, t + 1)
                nc.scalar.activation(v_t[:, t, :], bank[(5, 7)[t]][:, :], ACT.Copy).then_inc(v_ok, 1)
            act.wait_ge(v_ps, 3)
            for m in MH:
                ins = nc.scalar.activation(v_m[m, :], bank[3][m, 0:HV], ACT.Copy)
            ins.then_inc(v_ok, 1)
            act.wait_ge(q_ps, 1)
            nc.scalar.activation(qT[:, :, :].rearrange("p a n -> p (a n)"), bank[5][:, :], ACT.Copy, scale=GDK ** -0.5).then_inc(q_ok, 1)
            for t in range(NT):
                act.wait_ge(z_ps, t + 1)
                act.wait_ge(kdec, 1)
                act.wait_ge(ug_ps, 3)
                nc.scalar.activation(z_t[:, t, :], bank[(0, 5)[t]][:, :], ACT.Sigmoid).then_inc(z_sig, 1)
            scr = cacc[:, :, :].rearrange("p a b -> p (a b)")
            scr_o = csig[:, :, :].rearrange("p a b -> p (a b)")
            for r in range(2):
                act.wait_ge(y_mid, r + 1)
                if r:
                    link(last_y)
                for g in range(SGRP):
                    last_y = nc.scalar.activation(scr[:, g * 256:(g + 1) * 256], y1[:, r, g * 256:(g + 1) * 256], ACT.Square,
                                                  accum_out=ssy[:, r * 2 + g:r * 2 + g + 1])
                act.wait_ge(o_ps, r + 1)
                if r:
                    link(last_y)
                for t in range(NT):
                    for i in range(2):
                        n = t * 4 + 2 * i + r
                        at = (2 * t + i) * GDV
                        last_o = nc.scalar.activation(scr_o[:, at:at + GDV], bank[3 - r][:, t * 256 + i * P:t * 256 + (i + 1) * P],
                                                      ACT.Square, accum_out=sso[:, n:n + 1])
                if r == 0:
                    last_y = last_o
            last_o.then_inc(ssq, 1)
            inv_sqrt(rm, rr, rms_in, 1, rms)
            act.wait_ge(ssq, 1)
            act.wait_ge(y_ps, NCH)
            act.dma_start(rw[:, :, :], router_w[0].rearrange("(k p) e -> p k e", p=P)).then_inc(late_in, 16)
            act.dma_start(rb, router_b.broadcast_to([P, NE])).then_inc(late_in, 16)
            act.dma_start(b_dn[:, :], b_down[0]).then_inc(late_in, 16)
            for q in range(3):
                act.dma_start(braw[NE * q:NE * (q + 1), 0, :], b_gate[0]).then_inc(bias_in, 16)
                act.dma_start(braw[NE * q:NE * (q + 1), 1, :], b_up[0]).then_inc(bias_in, 16)

            def og_sigmoid(t):
                act.wait_ge(og_ps, t + 1)
                nc.scalar.activation(og[:, t, :], bank[(6, 7)[t]][:, :], ACT.Sigmoid).then_inc(og_sig, 1)

            og_sigmoid(0)
            og_sigmoid(1)
            act.wait_ge(mixT_ps, 1)
            mixT_evac(bank[0], 4)
            act.wait_ge(mixT_ps, 2)
            mixT_evac(bank[5], 6)
            act.wait_ge(mixT_ps, 3)
            mixT_evac(bank[6], 0)
            for t in range(NT):
                inv_sqrt(vtmp[:, t:t + 1], rstd[:, t:t + 1], var1, t + 1, rstd1)
                act.wait_ge(h1T_ps, 2 * t + 1)
                for kt in range(4):
                    nc.scalar.activation(h1T[:, kt, t * P:(t + 1) * P], bank[(0, 6)[t]][:, kt * P:(kt + 1) * P], ACT.Identity,
                                         bias=pcol[:, 64 + kt:65 + kt], scale=pcol[:, 56 + kt:57 + kt]).then_inc(h1T_act, 1)
            act.wait_ge(top_ok, 1)
            for t in range(NT):
                ins = nc.scalar.activation(gate4[:, t, 0:4], top8[:, t, 0:4], ACT.Exp, bias=gmax[:, t:t + 1])
            ins.then_inc(gexp, 1)

            act.wait_ge(GT_ps, 1)
            nc.scalar.activation(GT, bank[6][0:NE, 0:SEQ], ACT.Copy).then_inc(GT_ok, 1)

            def xT_evac(n, par, done):
                act.wait_ge(gath_ps, n + 1)
                if done is not None:
                    act.wait_ge(u_ps, done)
                nc.scalar.activation(xT[par][:, :, :].rearrange("p k s -> p (k s)"), bank[7][:, :], ACT.Copy).then_inc(xT_ok, 1)

            def tile(n, par, first, ahead):
                act.wait_ge(a_ok, n + 1)
                nc.scalar.activation(s_c, a_c, ACT.Sigmoid, scale=SALPHA).then_inc(sig_ok, 1)
                if ahead:
                    xT_evac(n + 1, 1 - par, None if first else n)
                act.wait_ge(selT_ps, n + 1)
                nc.scalar.activation(selGT, bank[6][:, 0:SEQ], ACT.Copy).then_inc(selGT_ok, 1)
                act.wait_ge(hidT_ps, n + 1)
                if not first:
                    act.wait_ge(d_ps, n)
                nc.scalar.activation(hidT[:, :, :].rearrange("p c n -> p (c n)"), bank[7][:, :], ACT.Copy).then_inc(hidT_ok, 1)

            xT_evac(0, 0, None)
            for k in range(UNROLL):
                tile(k, k % 2, k == 0, True)
            with act.Fori(1, ROUNDS - 1) as it:
                for k in range(UNROLL):
                    tile(it * UNROLL + k, k % 2, False, True)
            for k in range(UNROLL):
                tile(NE - UNROLL + k, k % 2, False, k < UNROLL - 1)
            act.wait_ge(list_ok, 1)
            nx = act.value_load(xcount[0:1, 0:1], min_val=0, max_val=MAXX)
            with act.If(nx > 0):
                with act.Fori(0, nx) as i:
                    xT_evac(i + NE, 0, i + NE)
                    tile(i + NE, 0, False, False)
            inv_sqrt(vtmp[:, 0:NT], rstd[:, 0:NT], var2, 1, rstd2)
            for t in range(NT):
                act.wait_ge(fin, 2 * t + 2)
                act.dma_start(out[0, t * P:(t + 1) * P, 512:D], z2[:, t, 512:D]).then_inc(out_done, 16)
            act.wait_ge(out_done, 16 * 2 * NT)

        @block.tensor
        def _(pe):
            link = linker(pe, pe_step)
            mm = nc.tensor.matmul
            tr = nc.tensor.transpose

            def keep_clock(b, n):
                for _ in range(n):
                    tr(b[:, 0:P], ident[:, :], ident[:, :])

            def wslot(n, kt, a=0, b=256):
                return ring[:, n, :].rearrange("p (k n) -> p k n", k=KT)[:, kt, a:b]

            pe.wait_ge(consts, 3)
            pe.wait_ge(params_in, 96)
            tr(bank[7][:, 0:72], prow[:, :], ident[0:72, 0:72]).then_inc(pcol_ps, 1)
            keep_clock(bank[0], 40)
            pe.wait_ge(xhat, 3)
            for kt in range(KT):
                if kt >= 4:
                    pe.wait_ge(hT_act if kt % 2 == 0 else hT_dve, kt // 2 - 1)
                b = bank[kt % 4]
                tr(b[:, 0:META], metah[:, kt * P:(kt + 1) * P], ident[0:META, 0:META])
                for t in range(NT):
                    ins = tr(b[:, META + t * P:META + (t + 1) * P], xh[:, t, kt * P:(kt + 1) * P], ident[:, :])
                ins.then_inc(hT_ps, 1)
            pe.wait_ge(hT_act, KT // 2)
            pe.wait_ge(hT_dve, KT // 2)
            pe.wait_ge(pads, 1)

            def c_transposes(c):
                b = bank[7] if c % 2 == 0 else bank[3]
                pe.wait_ge(silu, c + 1)
                if c == 0:
                    pe.wait_ge(pcol_ok, 1)
                if c >= 2:
                    pe.wait_ge(cT_ok, c - 1)
                src = cacc[:, c % 2, :]
                for t in range(NT):
                    tr(b[:, t * P:(t + 1) * P], src[:, META + t * P:META + (t + 1) * P], ident[:, :])
                tr(b[0:META, 2 * P:3 * P], src[:, 0:META], ident[:, :]).then_inc(cT_ps, 1)

            for c in range(XC):
                n = U_XBC + c // 2
                pe.wait_ge(landed[n], 16)
                if c >= 3:
                    pe.wait_ge(conv, c - 2)
                for kt in range(KT):
                    ins = mm(bank[4 + c % 3][:, 3:3 + TOK], wslot(n, kt, (c % 2) * P, (c % 2) * P + P), hT[:, kt, :],
                             start=kt == 0, stop=kt == KT - 1)
                ins.then_inc(conv_ps, 1)
                if c >= 2:
                    c_transposes(c - 2)
            pe.wait_ge(small_in, 128)
            for kt in range(KT):
                r = 64 * (kt % 2)
                ins = mm(bank[0][r:r + 24, 0:TOK], w_small[:, kt, :], hT[:, kt, :], start=kt < 2, stop=kt >= KT - 2)
            ins.then_inc(sT_ps, 1)

            def token_major(outs, n):
                for t in range(NT):
                    for kt in range(KT):
                        ins = mm(outs[t], hT[:, kt, META + t * P:META + (t + 1) * P], wslot(n, kt), start=kt == 0, stop=kt == KT - 1)
                return ins

            def meta_rows(dst, cols, slots):
                for kt in range(KT):
                    for m, (n, a) in zip(MH, slots):
                        ins = mm(dst[m, :], hT[:, kt, 0:META], wslot(n, kt, a, a + cols), start=kt == 0, stop=kt == KT - 1)
                return ins

            pe.wait_ge(landed[U_K], 16)
            pe.wait_ge(conv, 7)
            token_major([bank[4][:, t * 256:(t + 1) * 256] for t in range(NT)], U_K)
            meta_rows(bank[1][:, 256:256 + HK], HK, ((U_K, 0), (U_K, HK))).then_inc(k_ps, 1)
            pe.wait_ge(sT_ok, 1)
            for dst, a, m in ((bank[1][:, 0:8], META, P), (bank[1][:, 8:16], META + P, P), (bank[1][0:META, 16:24], 0, META)):
                mm(dst, sT[:, a:a + m], ident[0:SR, GRANK:24], start=True, stop=False)
                ins = mm(dst, sT[:, a:a + m], ident[0:SR, 64 + GRANK:SR], start=False, stop=True)
            ins.then_inc(dtT_ps, 1)
            for t in range(NT):
                mm(bank[2][:, t * 256:(t + 1) * 256], sT[:, META + t * P:META + (t + 1) * P], w_a2e[:, :], start=True, stop=True)
            for g, m in enumerate(MH):
                ins = mm(bank[0][m, 0:HK], sT[:, 0:META], w_a2e[:, g * HK:(g + 1) * HK], start=True, stop=True)
            ins.then_inc(la_ps, 1)
            pe.wait_ge(landed[U_V], 16)
            pe.wait_ge(conv, 8)
            pe.wait_ge(cT_ok, 6)
            token_major([bank[5][:, 0:256], bank[7][:, 0:256]], U_V)
            pe.wait_ge(dt_ok, 1)
            for t in range(NT):
                mm(bank[6][:, t * 8:(t + 1) * 8], tri[:, :], dt_c[:, t, :], start=True, stop=True)
            mm(bank[6][0:META, 16:24], tri[0:META, 0:META], dt_c[0:META, 2, :], start=True, stop=True)
            for c in (0, 2, 1, 3):
                r = CHUNK * (c % 2)
                if c == 1:
                    link(ins)
                ins = mm(bank[6][:, 32 + c * 8:40 + c * 8], ones[r:r + CHUNK, :], dt_c[r:r + CHUNK, c // 2, :], start=True, stop=True)
            ins.then_inc(dsum_ps, 1)
            pe.wait_ge(la_ok, 1)
            for t in range(NT):
                mm(bank[2][:, t * 256:(t + 1) * 256], tri[:, :], la[:, t, :], start=True, stop=True)
            mm(bank[0][MH[0], 0:HK], tri[MH[0], MH[0]], la_m[MH[0], :], start=True, stop=True)
            for c in (0, 2, 1, 3):
                r = CHUNK * (c % 2)
                if c == 1:
                    link(ins)
                    mm(bank[0][MH[1], 0:HK], tri[MH[1], MH[1]], la_m[MH[1], :], start=True, stop=True)
                for i in range(2):
                    ins = mm(bank[0][:, GKEY + i * 4 + c:GKEY + i * 4 + c + 1], la[r:r + CHUNK, c // 2, i * P:(i + 1) * P],
                             ones[r:r + CHUNK, 0:1], start=True, stop=True)
            ins.then_inc(D_ps, 1)
            pe.wait_ge(landed[U_V + 1], 16)
            n = U_V + 1
            for dst, at in ((bank[5], META), (bank[7], META + P)):
                for kt in range(KT):
                    ins = mm(dst[:, 256:512], hT[:, kt, at:at + P], wslot(n, kt), start=kt == 0, stop=kt == KT - 1)
                ins.then_inc(v_ps, 1)
            meta_rows(bank[3][:, 0:HV], HV, ((U_V, 0), (U_V + 1, 0))).then_inc(v_ps, 1)
            pe.wait_ge(wx_ok, 1)
            ssd_banks = (1, 6, 4, 1, 6)

            def ssd_update(c):
                b = bank[ssd_banks[c]]
                for g in range(SGRP):
                    if c == 0:
                        k, w = Bt[0:META, 2, g * SST:(g + 1) * SST], xs[0:META, 2, g * 256:(g + 1) * 256]
                    else:
                        r = CHUNK * ((c - 1) % 2)
                        k, w = Bt[r:r + CHUNK, (c - 1) // 2, g * SST:(g + 1) * SST], xs[r:r + CHUNK, (c - 1) // 2, g * 256:(g + 1) * 256]
                    ins = mm(b[:, g * 256:(g + 1) * 256], k, w, start=True, stop=True)
                ins.then_inc(us_ps, 1)

            pe.wait_ge(kdec, 1)
            for c in range(3):
                ssd_update(c)
            pe.wait_ge(landed[U_Q], 16)
            pe.wait_ge(v_ok, 1)
            for i in range(2):
                for kt in range(KT):
                    ins = mm(bank[5][:, i * SEQ:(i + 1) * SEQ], wslot(U_Q, kt, i * P, (i + 1) * P), hT[:, kt, META:TOK],
                             start=kt == 0, stop=kt == KT - 1)
            ins.then_inc(q_ps, 1)
            pe.wait_ge(v_ok, 3)

            def gla_update(c):
                b, at = (bank[7], 0) if c == 0 else (bank[3] if c % 2 else bank[2], ((c - 1) // 2) * 256)
                for h in range(GH):
                    if c == 0 and h == 2:
                        link(ins)
                    dst = b[64 * (h % 2):64 * (h % 2) + 64, at + (h // 2) * GDV:at + (h // 2 + 1) * GDV]
                    if c == 0:
                        m, i = MH[h // 2], h % 2
                        kk, vv = k_m[m, i * GDK:(i + 1) * GDK], v_m[m, i * GDV:(i + 1) * GDV]
                    else:
                        r = CHUNK * ((c - 1) % 2)
                        kk, vv = k_t[r:r + CHUNK, (c - 1) // 2, h * GDK:(h + 1) * GDK], v_t[r:r + CHUNK, (c - 1) // 2, h * GDV:(h + 1) * GDV]
                    ins = mm(dst, kk, vv, start=True, stop=True)
                return ins

            gla_update(0).then_inc(ug_ps, 1)
            for c in (1, 3):
                ins = gla_update(c)
            ins.then_inc(ug_ps, 1)
            for c in (2, 4):
                ins = gla_update(c)
            ins.then_inc(ug_ps, 1)
            for c in (3, 4):
                pe.wait_ge(Ss_ok, c - 2)
                ssd_update(c)
            pe.wait_ge(q_ok, 1)
            for hf in range(2):
                n = U_Z + hf
                pe.wait_ge(landed[n], 16)
                for t in range(NT):
                    for kt in range(KT):
                        ins = mm(bank[(0, 5)[t]][:, hf * 256:(hf + 1) * 256], hT[:, kt, META + t * P:META + (t + 1) * P], wslot(n, kt),
                                 start=kt == 0, stop=kt == KT - 1)
                    if hf:
                        ins.then_inc(z_ps, 1)
                if not hf:
                    ins.then_inc(half_used, 1)
            def ssd_out(c):
                pe.wait_ge(Ss_ok, c + 1)
                r = CHUNK * ((c - 1) % 2)
                b = bank[(4, 1)[(c - 1) // 2]]
                for g in range(SGRP):
                    ins = mm(b[r:r + CHUNK, g * 256:(g + 1) * 256], CT[:, g, (c - 1) * CHUNK:c * CHUNK], Ss[:, c % 3, g * 256:(g + 1) * 256],
                             start=True, stop=True)
                ins.then_inc(y_ps, 1)
            pe.wait_ge(silu, XC)
            pe.wait_ge(Ss_ok, 3)
            def gla_out(hb):
                for c in range(1, NCH + 1):
                    r = CHUNK * ((c - 1) % 2)
                    t = (c - 1) // 2
                    for i in range(2):
                        q = qT[64 * hb:64 * hb + 64, i, (c - 1) * CHUNK:c * CHUNK]
                        ins = mm(bank[3 - hb][r:r + CHUNK, t * 256 + i * GDV:t * 256 + (i + 1) * GDV], q,
                                 Sg[64 * hb:64 * hb + 64, c, i, :], start=True, stop=True)
                ins.then_inc(o_ps, 1)

            for c in range(1, NCH):
                ssd_out(c)
            pe.wait_ge(Sg_ok, NCH + 1)
            gla_out(0)
            ssd_out(NCH)
            gla_out(1)

            def mix_transposes(b, src, kts):
                for j, kt in enumerate(kts):
                    for t in range(NT):
                        at = (kt % 4) * P
                        ins = tr(b[:, j * SEQ + t * P:j * SEQ + (t + 1) * P], src[:, t, at:at + P], ident[:, :])
                ins.then_inc(mixT_ps, 1)

            for hf in range(2):
                n = U_OG + hf
                pe.wait_ge(landed[n], 16)
                for t in range(NT):
                    for kt in range(KT):
                        ins = mm(bank[(6, 7)[t]][:, hf * 256:(hf + 1) * 256], hT[:, kt, META + t * P:META + (t + 1) * P], wslot(n, kt),
                                 start=kt == 0, stop=kt == KT - 1)
                    if hf:
                        ins.then_inc(og_ps, 1)
                if not hf:
                    ins.then_inc(half_used, 1)
            pe.wait_ge(mix_y, 2)
            mix_transposes(bank[0], z_t, (4, 5))
            mix_transposes(bank[5], z_t, (6, 7))

            def out_part(t, kts, first):
                for nb in range(2):
                    b = bank[((1, 4), (2, 3))[t][nb]]
                    for kt in kts:
                        ins = mm(b[:, :], mixT[:, kt, t * P:(t + 1) * P],
                                 ring[:, U_OUT + 2 * nb:U_OUT + 2 * nb + 2, kt * 256:(kt + 1) * 256],
                                 start=first and kt == kts[0], stop=(not first) and kt == kts[-1], skip_group_check=True)
                    if not first:
                        ins.then_inc(wout_ps, 1)

            for n in range(4):
                pe.wait_ge(landed[U_OUT + n], 16)
            pe.wait_ge(mixT_act, 2)
            out_part(0, (4, 5, 6, 7), True)
            pe.wait_ge(mix_o, 2)
            mix_transposes(bank[6], og, (0, 1))
            mix_transposes(bank[7], og, (2, 3))
            out_part(1, (4, 5, 6, 7), True)
            pe.wait_ge(mixT_act, 3)
            pe.wait_ge(mixT_dve, 1)
            out_part(0, (0, 1, 2, 3), False)
            out_part(1, (0, 1, 2, 3), False)
            for t in range(NT):
                pe.wait_ge(h1_hat, t + 1)
                for half in range(2):
                    b = bank[((0, 5), (6, 7))[t][half]]
                    for j in range(4):
                        kt = half * 4 + j
                        ins = tr(b[:, j * P:(j + 1) * P], xh[:, t, kt * P:(kt + 1) * P], ident[:, :])
                    ins.then_inc(h1T_ps, 1)
                if t == 0:
                    keep_clock(bank[1], 18)
                    pe.wait_ge(late_in, 48)
                for j in range(4):
                    for kt, ready in ((j, h1T_act), (4 + j, h1T_dve)):
                        pe.wait_ge(ready, 4 * t + j + 1)
                        ins = mm(bank[4][:, t * NE:(t + 1) * NE], h1T[:, kt, t * P:(t + 1) * P], rw[:, kt, :], start=kt == 0, stop=kt == KT - 1)
                if t == 0:
                    keep_clock(bank[1], 18)
            ins.then_inc(logit_ps, 1)
            keep_clock(bank[1], 18)
            pe.wait_ge(mask_ok, 1)
            pe.wait_ge(iota_ok, 2)
            mm(bank[5][:, 0:NE], tri_s[:, :], mask[:, 0, :], start=True, stop=True)
            mm(bank[5][:, NE:2 * NE], tri_s[:, :], mask[:, 1, :], start=True, stop=False)
            mm(bank[5][:, NE:2 * NE], ones[:, :], mask[:, 0, :], start=False, stop=True)
            mm(bank[5][0:1, 2 * NE:3 * NE], ones[:, 0:1], mask[:, 0, :], start=True, stop=False)
            mm(bank[5][0:1, 2 * NE:3 * NE], ones[:, 0:1], mask[:, 1, :], start=False, stop=True).then_inc(pos_ps, 1)
            pe.wait_ge(mask_ok, 2)
            for t in range(NT):
                ins = tr(bank[6][0:NE, t * P:(t + 1) * P], gate[:, t, 0:NE], ident[:, :])
            ins.then_inc(GT_ps, 1)
            keep_clock(bank[1], 5)
            def start_sums():
                pe.wait_ge(GT_ok, 1)
                for t in range(NT):
                    for h in range(2):
                        mm(bank[2 * t + h][:, :], GT[:, t * P:(t + 1) * P], b_dn[:, h * 512:(h + 1) * 512], start=True, stop=False,
                           skip_group_check=True)

            def add_residual():
                pe.wait_ge(residual_ok, 1)
                for t in range(NT):
                    for h in range(2):
                        mm(bank[2 * t + h][:, :], residual[:, :], xh[:, t, h * 512:(h + 1) * 512], start=False, stop=False,
                           skip_group_check=True)

            def gather(n, par):
                pe.wait_ge(sel_ok, n + 1)
                for kt in range(KT):
                    for t in range(NT):
                        ins = mm(bank[7][:, kt * SL:(kt + 1) * SL], xh[:, t, kt * P:(kt + 1) * P], sel[:, par, t, :], start=t == 0, stop=t == 1)
                ins.then_inc(gath_ps, 1)

            def scatter(n, t):
                pe.wait_ge(yd_ok, n + 1)
                for h in range(2):
                    ins = mm(bank[2 * t + h][:, :], selGT[h * SL:(h + 1) * SL, t * P:(t + 1) * P], y_s[h * SL:(h + 1) * SL, :],
                             start=False, stop=False, skip_group_check=True)
                ins.then_inc(scat[t], 1)

            def tile(n, par, first, unit_at, arrived, gathers, scatters):
                def hidden(m, b, free, done):
                    if not first:
                        pe.wait_ge(free, n)
                    for h in range(2):
                        mm(b[h * SL:(h + 1) * SL, :], oh[:, par, :], bparts[:, m, h * 512:(h + 1) * 512], start=True, stop=False)
                    for q in range(4):
                        arrived(4 * m + q)
                        for k in range(2):
                            kt = 2 * q + k
                            for h in range(2):
                                ins = mm(b[h * SL:(h + 1) * SL, :], xT[par][:, kt, :], unit_at(4 * m + q)[:, k, h * 512:(h + 1) * 512],
                                         start=False, stop=kt == KT - 1)
                        ins.then_inc(done if q == 3 else unit_used, 1)

                pe.wait_ge(selG_ok, n + 1)
                pe.wait_ge(xT_ok, n + 1)
                hidden(0, bank[4], a_ok, g_ps)
                if gathers:
                    gather(n + 1, 1 - par)
                if scatters:
                    scatter(n - 1, 0)
                hidden(1, bank[5], u_ok, u_ps)
                if scatters:
                    scatter(n - 1, 1)
                if first:
                    start_sums()
                for t in range(NT):
                    ins = tr(bank[6][:, t * P:(t + 1) * P], selG[:, par, t, :], ident[:, :])
                ins.then_inc(selT_ps, 1)
                if gathers:
                    pe.wait_ge(xT_ok, n + 2)
                pe.wait_ge(hid_ok, n + 1)
                for c in range(4):
                    ins = tr(bank[7][:, c * P:(c + 1) * P], u_c[:, c * P:(c + 1) * P], ident[:, :])
                ins.then_inc(hidT_ps, 1)
                pe.wait_ge(selGT_ok, n + 1)
                pe.wait_ge(hidT_ok, n + 1)
                for q in range(4):
                    arrived(8 + q)
                    for k in range(2):
                        kt = 2 * q + k
                        for h in range(2):
                            ins = mm(bank[6][h * SL:(h + 1) * SL, :], hidT[:, kt % 4, (kt // 4) * SL:(kt // 4 + 1) * SL],
                                     unit_at(8 + q)[:, k, h * 512:(h + 1) * 512], start=kt == 0, stop=kt == KT - 1)
                    ins.then_inc(d_ps if q == 3 else unit_used, 1)

            def experts(it):
                for k in range(UNROLL):
                    def unit_at(u):
                        at = ring_at(it, UPE * k + u)
                        return spare[u] if at is None else slot(at % RING)

                    def arrived(u):
                        at = ring_at(it, UPE * k + u)
                        if at is None:
                            pe.wait_ge(spare_in, 16 * SPARE)
                        else:
                            pe.wait_ge(landed[at % RING], it * (UPE * UNROLL // RING * 16) + (2 + at // RING) * 16)
                    n = it * UNROLL + k
                    first, last = (isinstance(n, int) and n == m for m in (0, NE - 1))
                    tile(n, k % 2, first, unit_at, arrived, not last, not first)

            pe.wait_ge(h1_ok, NT)
            gather(0, 0)
            pe.wait_ge(bparts_ok, 1)
            experts(0)
            with pe.Fori(1, ROUNDS - 1) as it:
                experts(it)
            add_residual()
            experts(ROUNDS - 1)
            for t in range(NT):
                scatter(NE - 1, t)
            pe.wait_ge(list_ok, 1)
            nx = pe.value_load(xcount[0:1, 0:1], min_val=0, max_val=MAXX)
            with pe.If(nx > 0):
                with pe.Fori(0, nx) as i:
                    gather(i + NE, 0)
                    def arrived(u):
                        uses = 1 + (NE * UPE - SPARE + RING - 1 - u) // RING
                        pe.wait_ge(landed[u], i * 16 + (uses + 1) * 16)
                    tile(i + NE, 0, False, slot, arrived, False, False)
                    for t in range(NT):
                        scatter(i + NE, t)

        @block.vector
        def _(dve):
            link = linker(dve, dve_step)
            ts = nc.vector.tensor_scalar
            tt = nc.vector.tensor_tensor
            stt = nc.vector.scalar_tensor_tensor
            copy = nc.vector.tensor_copy

            for b in (4, 5, 6):
                nc.vector.memset(bank[b][:, 0:NCONV - 1], 0.0).then_inc(pads, 1)
            link(nc.vector.memset(sT[:, :], 1.0))
            link(nc.vector.memset(mv[:, :, :], 1.0))
            link(nc.vector.memset(dt_x[:, :, :], 0.0))
            nc.vector.memset(w_a2e[:, :], 0.0).then_inc(zeroed, 1)

            def refine(y, v, t):
                link(tt(t, y, y, ALU.mult))
                link(tt(t, t, v, ALU.mult))
                link(ts(t, t, -0.5, 1.5, ALU.mult, ALU.add))
                link(tt(y, y, t, ALU.mult))

            def moments(src, n, t):
                for i in range(2):
                    last = nc.vector.bn_stats(stats[0:n, i, :], src[:, i * 512:(i + 1) * 512])
                link(last)
                link(nc.vector.bn_aggr(mv[0:n, t, :], stats[0:n, :, :]))

            for t in range(NT):
                dve.wait_ge(x_in[t], 16)
                moments(xh[:, t, :], P, t)
            dve.wait_ge(meta_in, 16)
            moments(metah[:, :], META, 2)
            ts(vtmp, mv[:, :, 1], LN_EPS, None, ALU.add).then_inc(var_in, 1)
            dve.wait_ge(pcol_ps, 1)
            copy(pcol, bank[7][:, 0:72]).then_inc(pcol_ok, 1)
            dve.wait_ge(rstd_in, 1)
            dve.wait_ge(var_in, 1)
            refine(rstd, vtmp, vnew)
            for t in range(NT):
                ts(xh[:, t, :], xh[:, t, :], mv[:, t, 0:1], rstd[:, t:t + 1], ALU.subtract, ALU.mult).then_inc(xhat, 1)
            ts(metah[:, :], metah[:, :], mv[0:META, 2, 0:1], rstd[0:META, 2:3], ALU.subtract, ALU.mult).then_inc(xhat, 1)
            dve.wait_ge(pcol_ok, 1)
            for kt in range(1, KT, 2):
                dve.wait_ge(hT_ps, kt + 1)
                ts(hT[:, kt, :], bank[kt % 4][:, 0:TOK], pcol[:, kt:kt + 1], pcol[:, 8 + kt:9 + kt], ALU.mult, ALU.add).then_inc(hT_dve, 1)
            dve.wait_ge(pads, 3)
            for c in range(XC):
                dve.wait_ge(conv_ps, c + 1)
                if c >= 2:
                    dve.wait_ge(cT_ps, c - 1)
                acc, b = cacc[:, c % 2, :], bank[4 + c % 3]
                link(ts(acc, b[:, 0:TOK], pcol[:, 16 + c:17 + c], pcol[:, 48 + c:49 + c], ALU.mult, ALU.add))
                for j in range(1, NCONV):
                    ins = stt(acc, b[:, j:j + TOK], pcol[:, 16 + 8 * j + c:17 + 8 * j + c], acc, ALU.mult, ALU.add)
                    if j < NCONV - 1:
                        link(ins)
                ins.then_inc(conv, 1)
            dve.wait_ge(dtT_ps, 1)
            dve.wait_ge(small_in, 128)
            tt(dt_x[:, 0:NT, :], bank[1][:, 0:16].rearrange("p (t n) -> p t n", t=NT),
               dtb.unsqueeze(1).broadcast_to([P, NT, SHEADS]), ALU.add)
            tt(dt_x[0:META, 2, :], bank[1][0:META, 16:24], dtb[0:META, :], ALU.add).then_inc(dtx_ok, 1)
            dve.wait_ge(dt_e, 1)
            link(ts(dt_c, dt_a, 1.0, None, ALU.add))
            link(ts(dt_w, dt_c, -1.0, None, ALU.add))
            link(tt(dt_w, dt_a, dt_w, ALU.subtract))
            link(nc.vector.reciprocal(dt_c, dt_c))
            link(tt(dt_w, dt_w, dt_c, ALU.mult))
            link(tt(dt_b, dt_b, dt_w, ALU.add))
            link(stt(dt_x, dt_x, 0.0, dt_b, ALU.max, ALU.add))
            stt(dt_c, dt_x, -1.0, alog.unsqueeze(1).broadcast_to([P, 3, SHEADS]), ALU.mult, ALU.mult).then_inc(dt_ok, 1)
            dve.wait_ge(la_sp, 1)
            stt(la[:, :, :].rearrange("p t n -> p (t n)"), bank[2][:, :], 0.0, tmp[:, :, :].rearrange("p t n -> p (t n)"), ALU.min, ALU.subtract)
            for m in MH:
                ins = stt(la_m[m, :], bank[0][m, 0:HK], 0.0, expD[m, :], ALU.min, ALU.subtract)
            ins.then_inc(la_ok, 1)
            dve.wait_ge(dsum_ok, 1)
            tt(dt_w[:, 0:NT, :], dt_w[:, 0:NT, :], dt_x[:, 0:NT, :], ALU.mult)
            link(tt(dt_w[0:META, 2, :], dt_w[0:META, 2, :], dt_x[0:META, 2, :], ALU.mult))
            dve.wait_ge(y1_ok, 1)
            for t, m in ((0, P), (1, P), (2, META)):
                v = xs[0:m, t, :].rearrange("p (h q) -> p h q", h=SHEADS)
                ins = tt(v, v, dt_w[0:m, t, :].unsqueeze(2).broadcast_to([m, SHEADS, SHD]), ALU.mult)
            ins.then_inc(wx_ok, 1)
            dve.wait_ge(D_ok, 1)
            dve.wait_ge(k_ps, 1)
            tt(k_t[:, :, :].rearrange("p t n -> p (t n)"), bank[4][:, :], tmp[:, :, :].rearrange("p t n -> p (t n)"), ALU.mult)
            for m in MH:
                ins = tt(k_m[m, :], bank[1][m, 256:256 + HK], expD[m, :], ALU.mult)
            ins.then_inc(kdec, 1)
            ssd_banks = (1, 6, 4, 1, 6)

            def ssd_scan(c):
                dve.wait_ge(us_ps, c + 1)
                if c == 0:
                    copy(Ss[:, 0, :], bank[1][:, :]).then_inc(Ss_ok, 1)
                    return
                dve.wait_ge(Ss_ok, c)
                if c == NCH:
                    dve.wait_ge(y_ps, 1)
                new = Ss[:, c % 3, :]
                link(tt(new.rearrange("p (h q) -> p h q", h=SHEADS), Ss[:, (c - 1) % 3, :].rearrange("p (h q) -> p h q", h=SHEADS),
                        decs[:, c - 1, :].unsqueeze(2).broadcast_to([P, SHEADS, SHD]), ALU.mult))
                tt(new, new, bank[ssd_banks[c]][:, :], ALU.add).then_inc(Ss_ok, 1)

            for c in range(3):
                ssd_scan(c)
            dve.wait_ge(ug_ps, 1)
            copy(Sg[:, 0, :, :].rearrange("p a n -> p (a n)"), bank[7][:, 0:2 * GDV]).then_inc(Sg_ok, 1)
            for c in range(1, NCH + 1):
                dve.wait_ge(ug_ps, 2 if c % 2 else 3)
                dve.wait_ge(Sg_ok, c)
                b, at = bank[3] if c % 2 else bank[2], ((c - 1) // 2) * 256
                for i in range(2):
                    ins = stt(Sg[:, c, i, :], Sg[:, c - 1, i, :], decg[:, i * 4 + c - 1:i * 4 + c], b[:, at + i * GDV:at + (i + 1) * GDV],
                              ALU.mult, ALU.add)
                ins.then_inc(Sg_ok, 1)
            for c in (3, 4):
                ssd_scan(c)
            for t in range(NT):
                dve.wait_ge(z_sig, t + 1)
                tt(z_t[:, t, :], z_t[:, t, :], bank[(0, 5)[t]][:, :], ALU.mult).then_inc(z_ok, 1)
            for t in range(NT):
                dve.wait_ge(y_ps, 2 * t + 2)
                link(tt(y1[:, t, :], y1[:, t, :], bank[(4, 1)[t]][:, :], ALU.add))
                dve.wait_ge(z_ok, t + 1)
                tt(y1[:, t, :], y1[:, t, :], z_t[:, t, :], ALU.mult).then_inc(y_mid, 1)
            dve.wait_ge(ssq, 1)
            link(ts(rm[:, 0:4], ssy, 1.0 / 256, RMS_EPS, ALU.mult, ALU.add))
            ts(rm[:, 4:12], sso, 1.0 / GDV, RMS_EPS, ALU.mult, ALU.add).then_inc(rms_in, 1)
            dve.wait_ge(rms, 1)
            dve.wait_ge(rms_in, 1)
            refine(rr, rm, rmt)
            dve.wait_ge(normg_in, 32)
            for t in range(NT):
                for g in range(SGRP):
                    at = slice(g * 256, (g + 1) * 256)
                    ins = stt(z_t[:, t, at], y1[:, t, at], rry[:, 2 * t + g:2 * t + g + 1], normg[:, GVAL + g * 256:GVAL + (g + 1) * 256],
                              ALU.mult, ALU.mult)
                ins.then_inc(mix_y, 1)
            for t in range(NT):
                for h in range(GH):
                    ins = stt(o_n[:, t, h * GDV:(h + 1) * GDV], bank[3 - h % 2][:, t * 256 + (h // 2) * GDV:t * 256 + (h // 2 + 1) * GDV],
                              rro[:, t * 4 + h:t * 4 + h + 1], normg[:, h * GDV:(h + 1) * GDV], ALU.mult, ALU.mult)
            ins.then_inc(o_ok, 1)
            dve.wait_ge(o_ok, 1)
            for t in range(NT):
                dve.wait_ge(og_sig, t + 1)
                link(tt(og[:, t, :], og[:, t, :], bank[(6, 7)[t]][:, :], ALU.mult))
                tt(og[:, t, :], og[:, t, :], o_n[:, t, :], ALU.mult).then_inc(mix_o, 1)
            dve.wait_ge(mixT_ps, 4)
            copy(mixT[:, 2:4, :].rearrange("p a n -> p (a n)"), bank[7][:, :]).then_inc(mixT_dve, 1)
            dve.wait_ge(bias_in, 96)
            link(copy(bparts[:, :, :], braw[:, :, :]))
            for n in (2 * NE, NE):
                link(tt(braw[0:n, :, :], braw[0:n, :, :], bparts[0:n, :, :], ALU.subtract))
                ins = copy(bparts[0:n, :, :], braw[0:n, :, :])
                if n > NE:
                    link(ins)
            ins.then_inc(bparts_ok, 1)
            def h1T_evac(t):
                dve.wait_ge(h1T_ps, 2 * t + 2)
                for j in range(4):
                    kt = 4 + j
                    ts(h1T[:, kt, t * P:(t + 1) * P], bank[(5, 7)[t]][:, j * P:(j + 1) * P], pcol[:, 56 + kt:57 + kt],
                       pcol[:, 64 + kt:65 + kt], ALU.mult, ALU.add).then_inc(h1T_dve, 1)

            dve.wait_ge(h_ok, NT)
            for t in range(NT):
                for nb in range(2):
                    dve.wait_ge(wout_ps, 2 * t + nb + 1)
                    at = slice(nb * 512, (nb + 1) * 512)
                    link(stt(xh[:, t, at], xh[:, t, at], DN_ALPHA, bank[((1, 4), (2, 3))[t][nb]][:, :], ALU.mult, ALU.add))
                    ins = nc.vector.bn_stats(stats[:, nb, :], xh[:, t, at])
                link(ins)
                link(nc.vector.bn_aggr(mv[:, t, :], stats[:, :, :]))
                ts(vtmp[:, t:t + 1], mv[:, t, 1:2], LN_EPS, None, ALU.add).then_inc(var1, 1)
                if t == 1:
                    h1T_evac(0)
                dve.wait_ge(rstd1, t + 1)
                dve.wait_ge(var1, t + 1)
                refine(rstd[:, t:t + 1], vtmp[:, t:t + 1], vnew[:, t:t + 1])
                ts(xh[:, t, :], xh[:, t, :], mv[:, t, 0:1], rstd[:, t:t + 1], ALU.subtract, ALU.mult).then_inc(h1_hat, 1)
            h1T_evac(1)
            dve.wait_ge(late_in, 48)
            dve.wait_ge(logit_ps, 1)
            link(tt(logit, bank[4][:, 0:NT * NE].rearrange("p (t e) -> p t e", t=NT), rb.unsqueeze(1).broadcast_to([P, NT, NE]), ALU.add))
            for t in range(NT):
                ins = nc.vector.max(top8[:, t, :], logit[:, t, :])
            link(ins)
            ts(gmax, top8[:, :, 0], -1.0, None, ALU.mult).then_inc(top_ok, 1)
            for t in range(NT):
                ins = nc.vector.max_index(idx8[:, t, :], top8[:, t, :], logit[:, t, :])
            link(ins)
            link(copy(idxf, idx8[:, :, 0:4]))
            dve.wait_ge(iota_ok, 2)
            oh4 = onehot[:, :, :, :].rearrange("p t k e -> p (t k) e")
            gh4 = ghot[:, :, :, :].rearrange("p t k e -> p (t k) e")
            link(tt(oh4, iota[:, 0, 0:NE].unsqueeze(1).broadcast_to([P, NT * 4, NE]),
                    idxf[:, :, :].rearrange("p t k -> p (t k)").unsqueeze(2).broadcast_to([P, NT * 4, NE]), ALU.is_equal))
            nc.vector.tensor_reduce(mask, onehot[:, :, :, :].rearrange("p t k e -> p t e k"), AX_X, ALU.add).then_inc(mask_ok, 1)
            dve.wait_ge(gexp, 1)
            link(nc.vector.tensor_reduce(gsum, gate4[:, :, 0:4], AX_X, ALU.add))
            link(nc.vector.reciprocal(gsum, gsum))
            link(tt(gate4[:, :, 4:8], gate4[:, :, 0:4], gsum.unsqueeze(2).broadcast_to([P, NT, 4]), ALU.mult))
            for t in range(NT):
                ins = tt(ghot[:, t, :, :], onehot[:, t, :, :], gate4[:, t, 4:8].unsqueeze(2).broadcast_to([P, 4, NE]), ALU.mult)
            link(ins)
            nc.vector.tensor_reduce(gate[:, :, 0:NE], ghot[:, :, :, :].rearrange("p t k e -> p t e k"), AX_X, ALU.add).then_inc(mask_ok, 1)
            dve.wait_ge(pos_ps, 1)
            link(stt(posm[:, :, 0:NE], bank[5][:, 0:NT * NE].rearrange("p (t e) -> p t e", t=NT), 1.0, mask, ALU.add, ALU.mult))
            link(ts(posm[:, :, 0:NE], posm[:, :, 0:NE], -1.0, None, ALU.add))
            dve.wait_ge(mask_ok, 2)

            def select(done, e, par, j=0):
                if done is not None:
                    dve.wait_ge(gath_ps, done)
                    dve.wait_ge(u_ps, done)
                    dve.wait_ge(selT_ps, done)
                at = (slice(e, e + 1) if isinstance(e, int) else bass.ds(e, 1))
                jj = j if isinstance(j, int) else bass.ds(j, 1)
                slots = iota[:, jj, :] if isinstance(j, int) else iota[:, jj, :].rearrange("p a s -> p (a s)")
                for t in range(NT):
                    ins = ts(sel[:, par, t, :], slots[:, 0:SL], posm[:, t, at], None, ALU.is_equal)
                ins.then_inc(sel_ok, 1)
                for t in range(NT):
                    ts(selG[:, par, t, :], slots, posm[:, t, at], gate[:, t, at], ALU.is_equal, ALU.mult)
                ts(oh[:, par, :], ones[0:96, 0:SL], eid[0:96, at], None, ALU.mult).then_inc(selG_ok, 1)

            select(None, 0, 0)
            for j in range(1, NJ):
                ins = ts(flag[:, j - 1, :], bank[5][0:1, 2 * NE:3 * NE], float(SL * j), None, ALU.is_gt)
            link(ins)
            flagf = flag[:, :, :].rearrange("p j e -> p (j e)")
            link(nc.vector.tensor_tensor_scan(rank, flagf, ones[0:1, 0:3 * NE], 0.0, ALU.add, ALU.mult))
            copy(xcount, rank[:, 3 * NE - 1:3 * NE]).then_inc(list_ok, 1)

            def tile(n, par, first, after):
                if after is not None:
                    select(None if first else n, after, 1 - par)
                dve.wait_ge(g_ps, n + 1)
                ts(a_c, bank[4][:, :], LIMIT, None, ALU.min).then_inc(a_ok, 1)
                dve.wait_ge(u_ps, n + 1)
                if not first:
                    dve.wait_ge(hidT_ps, n)
                ts(u_c, bank[5][:, :], LIMIT, -LIMIT, ALU.min, ALU.max).then_inc(u_ok, 1)
                dve.wait_ge(sig_ok, n + 1)
                tt(a_c, a_c, s_c, ALU.mult).then_inc(as_ok, 1)
                dve.wait_ge(u_ok, n + 1)
                dve.wait_ge(as_ok, n + 1)
                stt(u_c, u_c, 1.0, a_c, ALU.add, ALU.mult).then_inc(hid_ok, 1)
                dve.wait_ge(d_ps, n + 1)
                if not first:
                    dve.wait_ge(scat[1], n)
                copy(y_s, bank[6][:, :]).then_inc(yd_ok, 1)

            for k in range(UNROLL):
                tile(k, k % 2, k == 0, k + 1)
            with dve.Fori(1, ROUNDS - 1) as it:
                for k in range(UNROLL):
                    tile(it * UNROLL + k, k % 2, False, it * UNROLL + (k + 1))
            for n in range(NE - UNROLL, NE):
                tile(n, n % 2, False, n + 1 if n < NE - 1 else None)
            nx = dve.value_load(xcount[0:1, 0:1], min_val=0, max_val=MAXX)
            with dve.If(nx > 0):
                dve.wait_ge(scat[1], NE)
                link_x = [0]

                def lx(ins):
                    link_x[0] += 1
                    ins.then_inc(xstep, 1)
                    dve.wait_ge(xstep, link_x[0])
                for j in range(1, NJ):
                    ts(flag_j[:, j - 1, :], flag[:, j - 1, :], float(j), None, ALU.mult)
                lx(tt(flag_e[:, :, :], flag[:, :, :], iota[0:1, 0, 0:NE].unsqueeze(1).broadcast_to([1, 3, NE]), ALU.mult))
                for i in range(MAXX):
                    for src, dst in ((flag_e, xlf[:, 0, :]), (flag_j, xlf[:, 1, :])):
                        lx(stt(xscr, rank, float(i + 1), src[:, :, :].rearrange("p j e -> p (j e)"), ALU.is_equal, ALU.mult,
                               accum_out=dst[:, i:i + 1]))
                copy(xlist2[:, :, :], xlf[:, :, :]).then_inc(list_ok, 1)
                dve.wait_ge(list_ok, 2)
                with dve.Fori(0, nx) as i:
                    e = dve.value_load(xlist[0:1, bass.ds(i, 1)], min_val=0, max_val=NE - 1)
                    j = dve.value_load(xlist2[0:1, 1, bass.ds(i, 1)], min_val=1, max_val=NJ - 1)
                    select(i + NE, e, 0, j)
                    tile(i + NE, 0, False, None)
            dve.wait_ge(ln2_in, 32)
            for t in range(NT):
                dve.wait_ge(scat[t], nx + NE)
                for h in range(2):
                    ins = nc.vector.bn_stats(stats[:, h, :], bank[2 * t + h][:, :])
                link(ins)
                link(nc.vector.bn_aggr(mv[:, t, :], stats[:, :, :]))
            ts(vtmp[:, 0:NT], mv[:, 0:NT, 1], LN_EPS, None, ALU.add).then_inc(var2, 1)
            for t in range(NT):
                for h in range(2):
                    at = slice(h * 512, (h + 1) * 512)
                    ins = stt(z2[:, t, at], bank[2 * t + h][:, :], mv[:, t, 0:1], lnbc[:, 0, at], ALU.subtract, ALU.mult)
            link(ins)
            dve.wait_ge(rstd2, 1)
            dve.wait_ge(var2, 1)
            refine(rstd[:, 0:NT], vtmp[:, 0:NT], vnew[:, 0:NT])
            for t in range(NT):
                for h in range(2):
                    at = slice(h * 512, (h + 1) * 512)
                    stt(z2[:, t, at], z2[:, t, at], rstd[:, t:t + 1], lnbc[:, 1, at], ALU.mult, ALU.add).then_inc(fin, 1)


_INS = ["x", "meta_tokens", "ln_in_g", "ln_in_b", "w_in", "gla_w_a2", "gla_b_a", "gla_norm_g", "ssd_conv_w", "ssd_conv_b",
        "ssd_dt_bias", "ssd_a_log", "ssd_d", "ssd_norm_g", "w_out", "ln1_g", "ln1_b", "router_w", "router_b",
        "moe_w_gate", "moe_w_up", "moe_b_gate", "moe_b_up", "moe_w_down", "moe_b_down", "ln2_g", "ln2_b"]


def kernel(**inputs):
    import numpy as np
    import concourse.bacc as bacc
    from concourse.bass_utils import run_bass_kernel_spmd

    nc = bacc.Bacc("TRN2", target_bir_lowering=False, num_devices=1)
    arrays, args = {}, []
    for name in _INS:
        a = np.ascontiguousarray(inputs[name])
        arrays[f"in_{name}"] = a
        args.append(nc.dram_tensor(f"in_{name}", a.shape, mybir.dt.from_np(a.dtype), kind="ExternalInput").ap())
    args.append(nc.dram_tensor("out_h", (1, SEQ, D), F32, kind="ExternalOutput").ap())
    build(nc, *args)
    return run_bass_kernel_spmd(nc, [arrays], core_ids=[0]).results[0]["out_h"]
```
